# Optimizing a Trainium2 kernel written in Bass

```python
import jax, jax.numpy as jnp
from jax import lax
import numpy as np

D_MODEL = 2048
BATCH = 1
SEQ = 512
DEPTH = 1

N_META = 16
POOL_WINDOWS = (2, 4, 8, 16)
N_POOL_GROUPS = 4
POOL_GROUP_DIM = D_MODEL // 8
POOL_WIDTH = N_POOL_GROUPS * POOL_GROUP_DIM
N_FOURIER_GROUPS = 4
FOURIER_GROUP_DIM = D_MODEL // 8
FOURIER_WIDTH = N_FOURIER_GROUPS * FOURIER_GROUP_DIM
N_BRANCHES = 2
IN_WIDTH = POOL_WIDTH + FOURIER_WIDTH + N_BRANCHES * D_MODEL
N_EXPERT_GROUPS = 4
EXPERTS_PER_GROUP = 8
N_EXPERTS = N_EXPERT_GROUPS * EXPERTS_PER_GROUP
TOP_K = 2
D_EXPERT = D_MODEL // 4
MOE_BLOCK = 128
DEEPNORM_ALPHA = (2.0 * DEPTH) ** 0.25
DEEPNORM_BETA = (8.0 * DEPTH) ** -0.25
LN_EPS = 1e-5

kernel_name = "hybrid_pool_fourier_hmoe_encoder"

def layer_norm(x, g, b):
    xf = x.astype(jnp.float32)
    mu = jnp.mean(xf, axis=-1, keepdims=True)
    var = jnp.mean(jnp.square(xf - mu), axis=-1, keepdims=True)
    y = (xf - mu) * lax.rsqrt(var + LN_EPS)
    return (y * g.astype(jnp.float32) + b.astype(jnp.float32)).astype(x.dtype)

def centred_window_mean(u, w):
    L = u.shape[1]
    uf = u.astype(jnp.float32)
    c = jnp.concatenate([jnp.zeros_like(uf[:, :1]), jnp.cumsum(uf, axis=1)], axis=1)
    pos = jnp.arange(L, dtype=jnp.int32)
    lo = jnp.clip(pos - w // 2, 0, L - 1)
    hi = jnp.clip(pos + w // 2 - 1, 0, L - 1)
    s = jnp.take(c, hi + 1, axis=1) - jnp.take(c, lo, axis=1)
    cnt = (hi - lo + 1).astype(jnp.float32)
    return (s / cnt[None, :, None]).astype(u.dtype)

def pool_mixer(u_pool, w_group, scale):
    B, L, _ = u_pool.shape
    u = u_pool.reshape(B, L, N_POOL_GROUPS, POOL_GROUP_DIM)
    pooled = jnp.stack([centred_window_mean(u[:, :, g], w) for g, w in enumerate(POOL_WINDOWS)], axis=2)
    z = jnp.einsum('blgc,gcd->blgd', pooled - u, w_group)
    return z.reshape(B, L, POOL_WIDTH) * scale

def fourier_mixer(u_four):
    B, L, _ = u_four.shape
    u = u_four.reshape(B, L, N_FOURIER_GROUPS, FOURIER_GROUP_DIM).astype(jnp.float32)
    f = jnp.fft.fftn(u, axes=(1, 3), norm='ortho').real
    return f.reshape(B, L, FOURIER_WIDTH).astype(u_four.dtype)

def mixer_sublayer(h, w_in, b_gate, w_pool_group, pool_scale, w_branch_pool, w_branch_fourier, w_out):
    B, L, D = h.shape
    proj = h @ w_in
    u_pool = proj[..., :POOL_WIDTH]
    u_four = proj[..., POOL_WIDTH:POOL_WIDTH + FOURIER_WIDTH]
    gate_logits = proj[..., POOL_WIDTH + FOURIER_WIDTH:] + b_gate
    gates = jax.nn.sigmoid(gate_logits.astype(jnp.float32)).astype(h.dtype).reshape(B, L, N_BRANCHES, D)
    y_pool = pool_mixer(u_pool, w_pool_group, pool_scale) @ w_branch_pool
    y_four = fourier_mixer(u_four) @ w_branch_fourier
    merged = gates[:, :, 0] * y_pool + gates[:, :, 1] * y_four
    return merged @ w_out

def hierarchical_moe(x, w_router_group, b_router_group, w_router_expert, b_router_expert, w_gate, w_up, w_down):
    B, L, D = x.shape
    T = B * L
    xt = x.reshape(T, D)
    xf = xt.astype(jnp.float32)
    group_logits = xf @ w_router_group.astype(jnp.float32) + b_router_group.astype(jnp.float32)
    p_group = jax.nn.softmax(group_logits, axis=-1)
    pg_top, g_idx = lax.top_k(p_group, 1)
    exp_logits = (xf @ w_router_expert.astype(jnp.float32) + b_router_expert.astype(jnp.float32))
    exp_logits = exp_logits.reshape(T, N_EXPERT_GROUPS, EXPERTS_PER_GROUP)
    sel_logits = jnp.take_along_axis(exp_logits, g_idx[:, :, None], axis=1)[:, 0]
    p_exp = jax.nn.softmax(sel_logits, axis=-1)
    pe_top, e_local = lax.top_k(p_exp, TOP_K)
    gate = pg_top * pe_top / jnp.sum(pe_top, axis=-1, keepdims=True)
    expert_id = (g_idx * EXPERTS_PER_GROUP + e_local).astype(jnp.int32)

    A = T * TOP_K
    flat_e = expert_id.reshape(A)
    flat_t = jnp.repeat(jnp.arange(T, dtype=jnp.int32), TOP_K)
    flat_w = gate.reshape(A)
    order = jnp.argsort(flat_e)
    se, st, sw = flat_e[order], flat_t[order], flat_w[order]
    counts = jnp.bincount(flat_e, length=N_EXPERTS).astype(jnp.int32)
    padded = (counts + MOE_BLOCK - 1) // MOE_BLOCK * MOE_BLOCK
    start = jnp.cumsum(counts) - counts
    pstart = jnp.cumsum(padded) - padded
    dest = pstart[se] + (jnp.arange(A, dtype=jnp.int32) - start[se])
    n_blocks = (A + N_EXPERTS * (MOE_BLOCK - 1) + MOE_BLOCK - 1) // MOE_BLOCK
    n_slots = n_blocks * MOE_BLOCK
    slot_token = jnp.full((n_slots,), T, jnp.int32).at[dest].set(st)
    x_pad = jnp.concatenate([xt, jnp.zeros((1, D), xt.dtype)], axis=0)
    xs = x_pad[slot_token].reshape(n_blocks, MOE_BLOCK, D)
    block_start = jnp.arange(n_blocks, dtype=jnp.int32) * MOE_BLOCK
    block_expert = jnp.minimum(jnp.searchsorted(jnp.cumsum(padded), block_start, side='right'),
                               N_EXPERTS - 1).astype(jnp.int32)

    def expert_block(args):
        xb, e = args
        hb = jax.nn.silu(xb @ w_gate[e]) * (xb @ w_up[e])
        return hb @ w_down[e]

    ys = lax.map(expert_block, (xs, block_expert)).reshape(n_slots, D)
    contrib = ys[dest] * sw[:, None].astype(ys.dtype)
    out = jnp.zeros((T, D), ys.dtype).at[st].add(contrib)
    return out.reshape(B, L, D)

def setup_inputs(seed: int = 0) -> dict:
    key = jax.random.key(seed)
    ks = jax.random.split(key, 24)
    f32 = jnp.float32
    D = D_MODEL
    nrm = lambda k, shape, scale: jax.random.normal(k, shape, f32) * scale
    return {
        "x": nrm(ks[0], (BATCH, SEQ, D), 1.0),
        "meta_tokens": nrm(ks[1], (N_META, D), 1.0),
        "in_ln_g": 1.0 + nrm(ks[2], (D,), 0.02),
        "in_ln_b": nrm(ks[3], (D,), 0.02),
        "w_in": nrm(ks[4], (DEPTH, D, IN_WIDTH), D ** -0.5),
        "b_gate": nrm(ks[5], (DEPTH, N_BRANCHES * D), 0.02),
        "w_pool_group": nrm(ks[6], (DEPTH, N_POOL_GROUPS, POOL_GROUP_DIM, POOL_GROUP_DIM), POOL_GROUP_DIM ** -0.5),
        "pool_scale": 1.0 + nrm(ks[7], (DEPTH, POOL_WIDTH), 0.02),
        "w_branch_pool": nrm(ks[8], (DEPTH, POOL_WIDTH, D), DEEPNORM_BETA * POOL_WIDTH ** -0.5),
        "w_branch_fourier": nrm(ks[9], (DEPTH, FOURIER_WIDTH, D), DEEPNORM_BETA * FOURIER_WIDTH ** -0.5),
        "w_out": nrm(ks[10], (DEPTH, D, D), DEEPNORM_BETA * D ** -0.5),
        "ln1_g": 1.0 + nrm(ks[11], (DEPTH, D), 0.02),
        "ln1_b": nrm(ks[12], (DEPTH, D), 0.02),
        "w_router_group": nrm(ks[13], (DEPTH, D, N_EXPERT_GROUPS), D ** -0.5),
        "b_router_group": nrm(ks[14], (DEPTH, N_EXPERT_GROUPS), 0.01),
        "w_router_expert": nrm(ks[15], (DEPTH, D, N_EXPERTS), D ** -0.5),
        "b_router_expert": nrm(ks[16], (DEPTH, N_EXPERTS), 0.01),
        "w_gate": nrm(ks[17], (DEPTH, N_EXPERTS, D, D_EXPERT), D ** -0.5),
        "w_up": nrm(ks[18], (DEPTH, N_EXPERTS, D, D_EXPERT), D ** -0.5),
        "w_down": nrm(ks[19], (DEPTH, N_EXPERTS, D_EXPERT, D), DEEPNORM_BETA * D_EXPERT ** -0.5),
        "ln2_g": 1.0 + nrm(ks[20], (DEPTH, D), 0.02),
        "ln2_b": nrm(ks[21], (DEPTH, D), 0.02),
    }

def reference(x, meta_tokens, in_ln_g, in_ln_b, w_in, b_gate, w_pool_group, pool_scale,
              w_branch_pool, w_branch_fourier, w_out, ln1_g, ln1_b,
              w_router_group, b_router_group, w_router_expert, b_router_expert,
              w_gate, w_up, w_down, ln2_g, ln2_b):
    B = x.shape[0]
    meta = jnp.broadcast_to(meta_tokens[None].astype(x.dtype), (B, N_META, D_MODEL))
    h = layer_norm(jnp.concatenate([meta, x], axis=1), in_ln_g, in_ln_b)
    for l in range(DEPTH):
        mix = mixer_sublayer(h, w_in[l], b_gate[l], w_pool_group[l], pool_scale[l],
                             w_branch_pool[l], w_branch_fourier[l], w_out[l])
        h = layer_norm(DEEPNORM_ALPHA * h + mix, ln1_g[l], ln1_b[l])
        ffn = hierarchical_moe(h, w_router_group[l], b_router_group[l], w_router_expert[l],
                               b_router_expert[l], w_gate[l], w_up[l], w_down[l])
        h = layer_norm(DEEPNORM_ALPHA * h + ffn, ln2_g[l], ln2_b[l])
    return h[:, N_META:]


_drawn_inputs = setup_inputs


def setup_inputs(seed=0):
    import zlib

    import numpy as np

    out = dict(_drawn_inputs(seed))
    spreads = {}
    factors = {'b_gate': 8.0,
     'pool_scale': 23.589,
     'b_router_group': 8.0,
     'b_router_expert': 8.0,
     'ln2_g': 8.268,
     'ln2_b': 7.953,
     'in_ln_b': 2.848}
    for name, (base, spread) in spreads.items():
        noise = np.random.default_rng([zlib.crc32(name.encode()), seed]).standard_normal(out[name].shape)
        drawn = base * np.exp(spread * noise) if base else spread * noise
        out[name] = __import__('jax').numpy.asarray(drawn.astype(out[name].dtype))
    for name, factor in factors.items():
        out[name] = (out[name] * factor).astype(out[name].dtype)
    return out
```

```python
from contextlib import ExitStack

import concourse.bass as bass
import numpy as np
from concourse import mybir

F32 = mybir.dt.float32
F32R = mybir.dt.float32r
U32 = mybir.dt.uint32
I32 = mybir.dt.int32
ALU = mybir.AluOpType
ACT = mybir.ActivationFunctionType
AX = mybir.AxisListType.X

P = 128
D = 2048
SEQ = 512
META = 16
T = SEQ + META
TILES = 5
STARTS = [0, 128, 256, 384, T - P]
KC = D // P
HALF = T // 2
NG = 4
GD = 256
W2 = NG * GD
NE = 32
EG = 8
F = D // 4
CAP = 64
NX = 2 * T // (CAP + 1)
NB = NE + NX
NTAB = NB + 1
ALPHA = 2.0 ** 0.25
EPS = 1e-5
BIG = 1e30
EMPTY = 8192

MC = 1024
RAW, RING = 4, 2
EC = 2048
ECH = 12
ERING = 4

FCH, PCH, JCH, WCH = 16, 6, 6, 8
F0 = 0
P0 = F0 + NG * FCH
J0 = P0 + NG * PCH
W0 = J0 + KC * JCH
WEND = W0 + 4 * WCH

PADW = 8
UW = T + 2 * PADW

CONST = {}
_at = 0
for _n, _w in (("ident", P), ("ltri", P), ("e32", NE), ("r32", NE), ("slot", CAP), ("block", NTAB), ("r4", NG),
               ("valid", TILES), ("token", 2 * TILES), ("x", NX)):
    CONST[_n] = (_at, _at + _w)
    _at += _w
NCONST = _at


def shape_constants():
    k = np.zeros((P, NCONST), np.float32)

    def put(name, v):
        k[:, CONST[name][0]:CONST[name][1]] = v

    i = np.arange(P)
    put("ident", np.eye(P))
    put("ltri", i[:, None] < i[None, :])
    put("e32", np.arange(NE)[None])
    put("r32", NE - np.arange(NE)[None])
    put("slot", np.arange(CAP)[None])
    put("block", np.arange(NTAB)[None])
    put("r4", NG - np.arange(NG)[None])
    own = np.ones((P, TILES))
    own[:TILES * P - T, TILES - 1] = 0
    put("valid", own)
    tok = np.array(STARTS)[None, :] + i[:, None]
    put("token", np.concatenate([tok + 1, tok + 1 + T], 1))
    put("x", np.arange(NX)[None])
    c = np.arange(GD)
    ang = 2 * np.pi * (np.outer(c, c) % GD) / GD
    chan = np.concatenate([np.cos(ang), np.sin(ang)], 1) / np.sqrt(GD)
    n = np.arange(T)
    ang = 2 * np.pi * (np.outer(n, n) % T) / T
    pos = np.zeros((2, TILES, P, T))
    for t, s in enumerate(STARTS):
        pos[0, t] = np.cos(ang[s:s + P]) / np.sqrt(T)
        pos[1, t] = -np.sin(ang[s:s + P]) / np.sqrt(T)
    pos[:, TILES - 1, :TILES * P - T] = 0
    edge = np.zeros((NG, 2 * PADW))
    for g in range(NG):
        w = 2 ** (g + 1)
        cnt = np.clip(n + w // 2 - 1, 0, T - 1) - np.clip(n - w // 2, 0, T - 1) + 1
        edge[g] = (w / cnt)[np.r_[0:PADW, T - PADW:T]]
    return k, chan.astype(np.float32), pos.astype(np.float32), edge.astype(np.float32)


def encoder_kernel(nc, x, meta_tokens, in_ln_g, in_ln_b, w_in, b_gate, w_pool_group, pool_scale, w_branch_pool,
                   w_branch_fourier, w_out, ln1_g, ln1_b, w_router_group, b_router_group, w_router_expert,
                   b_router_expert, w_gate, w_up, w_down, ln2_g, ln2_b, k_small, k_chan, k_pos, k_edge, out):
    h0_dram = nc.dram_tensor("h0_rows", [T, D], F32).ap()
    h1_dram = nc.dram_tensor("h1_rows", [T, D], F32).ap()
    y_dram = nc.dram_tensor("expert_rows", [2 * T, D], F32).ap()

    base = (nc.sbuf_base + 31) // 32 * 32

    def sb(name, shape, dt, at):
        return nc.alloc_sbuf_tensor_at(name, shape, dt, offset=base + at)

    act_hi = sb("act_hi", [P, KC, T], F32R, 0)
    act_lo = sb("act_lo", [P, KC, T], F32R, 33792)
    mix_hi = sb("mix_hi", [P, KC, T], F32R, 67584)
    mix_lo = sb("mix_lo", [P, KC, T], F32R, 101376)
    chan_hi = mix_hi[:, 0:2, :]
    chan_lo = mix_lo[:, 0:2, :]
    freq_hi = mix_hi[:, 2:7, 0:2 * GD]
    freq_lo = mix_lo[:, 2:7, 0:2 * GD]
    raw = sb("raw", [P, RAW, MC], F32, 135168)
    whi = sb("whi", [P, RING, MC], F32R, 151552)
    wlo = sb("wlo", [P, RING, MC], F32R, 159744)
    merged = sb("merged", [P, KC, T], F32, 167936)
    consts = sb("consts", [P, NCONST], F32, 201728)
    small_at = 201728 + (4 * NCONST + 31) // 32 * 32

    def small(name, shape, dt):
        nonlocal small_at
        t = sb(name, shape, dt, small_at)
        small_at += (int(np.prod(shape[1:])) * 4 + 31) // 32 * 32
        return t

    cols = small("cols", [P, 40], F32)
    edge = small("edge", [P, NG, 2 * PADW], F32)
    rbias = small("rbias", [P, NG + NE], F32)
    gidx = small("gidx", [CAP, NTAB], U32)
    sidx = small("sidx", [CAP, NTAB], U32)
    gatew = small("gatew", [CAP, NTAB], F32)
    steer = small("steer", [1, NX + 1], I32)
    assert small_at <= 204992
    stage = sb("stage", [P, 3, UW], F32, 204992)
    rows = sb("rows", [P, TILES, D], F32, 67584)
    resid = sb("resid", [P, 2, TILES, 512], F32, 108544)
    gb = sb("gb", [P, 2, D], F32, 167936)
    colsrc = sb("colsrc", [40, P], F32, 184320)
    stats = sb("stats", [P, TILES, 4, 6], F32, 129024)
    mv = sb("mv", [P, TILES, 2], F32, 129536)
    std = sb("std", [P, TILES], F32, 129600)
    rstd = sb("rstd", [P, TILES], F32, 129632)
    nmr = sb("nmr", [P, TILES], F32, 129664)
    h1T = sb("h1T", [P, 2, KC, P], F32, 0)
    wrout = sb("wrout", [P, KC, NG + NE], F32, 16384)
    rt = 18944

    def rbuf(name, shape, dt=F32):
        nonlocal rt
        t = sb(name, shape, dt, rt)
        rt += (int(np.prod(shape[1:])) * 4 + 31) // 32 * 32
        return t

    logit = rbuf("logit", [P, TILES, NG + NE])
    gmax = rbuf("gmax", [P, TILES])
    gdif = rbuf("gdif", [P, TILES, NG])
    gexp = rbuf("gexp", [P, TILES, NG])
    gsum = rbuf("gsum", [P, TILES])
    gprob = rbuf("gprob", [P, TILES])
    gone = rbuf("gone", [P, TILES, NG])
    gpick = rbuf("gpick", [P, TILES])
    masked = rbuf("masked", [P, TILES, NE])
    masked2 = rbuf("masked2", [P, TILES, NE])
    emax = rbuf("emax", [P, 2, TILES])
    epick = rbuf("epick", [P, 2, TILES])
    etmp = rbuf("etmp", [P, TILES, NE])
    one = rbuf("one", [P, 2, TILES, NE])
    anyone = rbuf("anyone", [P, TILES, NE])
    ones = rbuf("ones", [P, P])
    ediff = rbuf("ediff", [P, TILES])
    eexp = rbuf("eexp", [P, TILES])
    esum = rbuf("esum", [P, TILES])
    gate = rbuf("gate", [P, 2, TILES])
    posn = rbuf("posn", [P, TILES, NE])
    count = rbuf("count", [P, NE])
    over = rbuf("over", [P, 8, NE])
    nover = rbuf("nover", [P, NE])
    cum = rbuf("cum", [P, NE])
    excl = rbuf("excl", [P, NE])
    prod = rbuf("prod", [P, 2, TILES, NE])
    apos = rbuf("apos", [P, 2, TILES])
    aexp = rbuf("aexp", [P, 2, TILES])
    aexc = rbuf("aexc", [P, 2, TILES])
    step8 = rbuf("step8", [P, 8, 2 * TILES])
    turn = rbuf("turn", [P, 2, TILES])
    turn1 = rbuf("turn1", [P, 2, TILES])
    aslot = rbuf("aslot", [P, 2, TILES])
    ablock = rbuf("ablock", [P, 2, TILES])
    slot1 = rbuf("slot1", [P, 2 * TILES, CAP])
    block1 = rbuf("block1", [P, 2 * TILES, NTAB])
    block2 = rbuf("block2", [P, 2 * TILES, 2, NTAB])
    table = rbuf("table", [CAP, 2, NTAB])
    none = rbuf("none", [CAP, NTAB])
    sidxf = rbuf("sidxf", [CAP, NTAB])
    second = rbuf("second", [CAP, NTAB])
    gidxf = rbuf("gidxf", [CAP, NTAB])
    below = rbuf("below", [P, NX, NE])
    steerf = rbuf("steerf", [P, NX + 1])
    assert rt <= 67584
    ehi = sb("ehi", [P, ERING, EC], F32R, 0)
    elo = sb("elo", [P, ERING, EC], F32R, 32768)
    hrow = sb("hrow", [P, F], F32, 65536)
    SLOTS = [184320, 192512, 135168, 143360, 151552, 159744, 108544, 116736, 124928, 67584, 75776, 83968]
    eraw = [sb(f"eraw{i}", [P, EC], F32, at) for i, at in enumerate(SLOTS)]
    xrow = sb("xrow", [P, D], F32, 92160)
    yrow = sb("yrow", [CAP, D], F32, 100352)
    xT_hi = sb("xT_hi", [P, KC, P], F32R, 167936)
    xT_lo = sb("xT_lo", [P, KC, P], F32R, 176128)
    hT_hi = sb("hT_hi", [P, 4, P], F32R, 204992)
    hT_lo = sb("hT_lo", [P, 4, P], F32R, 207040)
    gcol = sb("gcol", [CAP, 1], F32, 211200)
    srow = sb("srow", [P, F], F32, 209088)
    gcur = sb("gcur", [CAP, 1], U32, 211136)
    scur = sb("scur", [CAP, 1], U32, 211168)
    fin_h = sb("fin_h", [P, TILES, D], F32, 0)
    fin_y = sb("fin_y", [P, 2, TILES, D], F32, 40960)

    ident = consts[:, 0:P]

    def const(name, parts=P):
        a, b = CONST[name]
        return consts[0:parts, a:b]

    ctx = ExitStack()
    with ctx:
        ps = ctx.enter_context(nc.psum_tensor("ps", [P, 8, 512], F32))

        def sem(name):
            return ctx.enter_context(nc.semaphore(name))

        s_small = sem("s_small")
        s_wr = sem("s_wr")
        s_row = [sem(f"s_row{t}") for t in range(TILES)]
        s_gb = sem("s_gb")
        s_gb2 = sem("s_gb2")
        s_raw = [sem(f"s_raw{i}") for i in range(RAW)]
        s_res = [sem(f"s_res{i}") for i in range(2)]
        s_eraw = [sem(f"s_eraw{i}") for i in range(ECH)]
        s_h0 = sem("s_h0")
        s_h1 = sem("s_h1")
        s_out = sem("s_out")
        hi_done = sem("hi_done")
        lo_done = sem("lo_done")
        used = sem("used")
        ln_mv = [sem(f"ln_mv{i}") for i in range(3)]
        ln_std = [sem(f"ln_std{i}") for i in range(3)]
        ln_norm = [sem(f"ln_norm{i}") for i in range(3)]
        ln_g = [sem(f"ln_g{i}") for i in range(3)]
        ln_done = [sem(f"ln_done{i}") for i in range(3)]
        tr_ready = sem("tr_ready")
        tr_hi = sem("tr_hi")
        tr_lo = sem("tr_lo")
        cols_ready = sem("cols_ready")
        cols_done = sem("cols_done")
        fu_hi = sem("fu_hi")
        fu_lo = sem("fu_lo")
        fv_ready = sem("fv_ready")
        fv_hi = sem("fv_hi")
        fv_lo = sem("fv_lo")
        fo_ready = sem("fo_ready")
        fo_hi = sem("fo_hi")
        fo_lo = sem("fo_lo")
        pad_zero = sem("pad_zero")
        pu_copied = sem("pu_copied")
        pw_step = sem("pw_step")
        pw_done = sem("pw_done")
        pd_hi = sem("pd_hi")
        pd_lo = sem("pd_lo")
        pm_hi = sem("pm_hi")
        pm_lo = sem("pm_lo")
        gate_done = sem("gate_done")
        mul_done = sem("mul_done")
        merge_done = sem("merge_done")
        mt_hi = sem("mt_hi")
        mt_lo = sem("mt_lo")
        acc_ready = sem("acc_ready")
        acc_free = sem("acc_free")
        bn_done = sem("bn_done")
        s_ln0 = sem("s_ln0")
        s_ln2 = sem("s_ln2")
        s_agg = [sem(f"s_agg{i}") for i in range(3)]
        rt_ready = sem("rt_ready")
        rt_done = sem("rt_done")
        lg_ready = sem("lg_ready")
        lg_done = sem("lg_done")
        r_step = sem("r_step")
        r_gexp = sem("r_gexp")
        r_eexp = sem("r_eexp")
        r_any = sem("r_any")
        r_pos = sem("r_pos")
        r_hot = sem("r_hot")
        r_table = sem("r_table")
        r_done = sem("r_done")
        pad_cols = sem("pad_cols")
        ehi_done = sem("ehi_done")
        elo_done = sem("elo_done")
        eused = sem("eused")
        idx_g = sem("idx_g")
        idx_s = sem("idx_s")
        gathered = sem("gathered")
        scattered = sem("scattered")
        xt_ready = sem("xt_ready")
        xt_hi = sem("xt_hi")
        xt_lo = sem("xt_lo")
        silu_done = sem("silu_done")
        h_done = sem("h_done")
        ht_ready = sem("ht_ready")
        ht_hi = sem("ht_hi")
        ht_lo = sem("ht_lo")
        y_ready = sem("y_ready")
        y_done = sem("y_done")
        gcol_done = sem("gcol_done")
        moe_end = sem("moe_end")
        s_fh = [sem(f"s_fh{t}") for t in range(TILES)]
        s_fy = [sem(f"s_fy{t}") for t in range(TILES)]
        f_sum = sem("f_sum")

        block = ctx.enter_context(nc.Block())

        def win_half(col, half):
            return w_in[0, 1024 * half:1024 * (half + 1), col].rearrange("(k p) n -> p k n", p=P)

        def past(eng, sem, value):
            if not isinstance(value, int) or value > 0:
                eng.wait_ge(sem, value)

        def at(start, size=P):
            return bass.ds(start, size)

        def raw3(i, n, w):
            return raw[:, i, 0:n * w].rearrange("p (k n) -> p k n", n=w)

        def used_cols(bank):
            return bank.rearrange("p (c n) -> p c n", n=P)[:, :, 0:CAP]

        def own_rows(t):
            lo = t * P
            return lo, min(T, lo + P), lo - STARTS[t]

        def dynamic_weights(e, i):
            if i < 8:
                w = w_gate if i < 4 else w_up
                return w[0, bass.ds(e, 1), 512 * (i % 4):512 * (i % 4 + 1), :].rearrange("a (k p) n -> p (a k) n", p=P)
            return w_down[0, bass.ds(e, 1), P * (i - 8):P * (i - 7), :].rearrange("a p n -> p (a n)")

        def eraw_view(i):
            return eraw[i][:, :].rearrange("p (k n) -> p k n", n=F) if i < 8 else eraw[i][:, :]

        @block.sync
        def _(sp):
            x_rows = x.rearrange("b s d -> (b s) d")
            sp.dma_start(rows[0:META, 0, :], meta_tokens).then_inc(s_row[0], 16)
            sp.dma_start(rows[META:P, 0, :], x_rows[0:P - META, :]).then_inc(s_row[0], 16)
            for t in range(1, TILES):
                sp.dma_start(rows[:, t, :], x_rows[STARTS[t] - META:STARTS[t] - META + P, :]).then_inc(s_row[t], 16)

            def chunk(n, slot, dst, src):
                if isinstance(n, int) and n < RAW:
                    pass
                else:
                    sp.wait_ge(lo_done, n - RAW + 1)
                sp.dma_start(dst, src).then_inc(s_raw[slot], 16)

            def fourier_group(g, first):
                for i in range(4):
                    n = F0 + i if first else F0 + FCH * g + i
                    chunk(n, i % RAW, raw3(i % RAW, 8, P), win_half(at(W2 + GD * g + P * (i // 2)), i % 2))
                for i in range(4, 6):
                    chunk(F0 + FCH * g + i, i % RAW, raw[:, i % RAW, 0:512], k_chan[P * (i - 4):P * (i - 3), :])
                for i in range(6, FCH):
                    t, cs = divmod(i - 6, 2)
                    chunk(F0 + FCH * g + i, i % RAW, raw[:, i % RAW, 0:T], k_pos[cs, t])

            fourier_group(0, True)
            with sp.Fori(1, NG) as g:
                fourier_group(g, False)
            for g in range(NG):
                for i in range(PCH):
                    n = P0 + PCH * g + i
                    if i < 4:
                        chunk(n, n % RAW, raw3(n % RAW, 8, P), win_half(at(GD * g + P * (i // 2)), i % 2))
                    else:
                        chunk(n, n % RAW, raw[:, n % RAW, 0:GD], w_pool_group[0, g, P * (i - 4):P * (i - 3), :])
            with sp.Fori(0, KC // 2) as jj:
                for b in range(2):
                    sp.to_reg(4 * (P * (2 * jj + b)))
                    for i in range(JCH):
                        j = 2 * jj + b
                        slot = (J0 + JCH * b + i) % RAW
                        if i < 4:
                            src = win_half(at(2 * W2 + D * (i // 2) + P * j), i % 2)
                        else:
                            w = (w_branch_pool, w_branch_fourier)[i - 4]
                            src = w[0, :, at(P * j)].rearrange("(k p) n -> p k n", p=P)
                        chunk(J0 + JCH * b + i + 2 * JCH * jj, slot, raw3(slot, 8, P), src)
            with sp.Fori(0, 4) as n:
                for i in range(WCH):
                    slot = (W0 + i) % RAW
                    chunk(W0 + i + WCH * n, slot, raw3(slot, 2, 512),
                          w_out[0, 2 * P * i:2 * P * (i + 1), at(512 * n, 512)].rearrange("(k p) n -> p k n", p=P))

            for i in range(ECH):
                if i == 0:
                    sp.wait_ge(mt_lo, KC // 2)
                if i == 2:
                    sp.wait_ge(used, WEND)
                if i == 6:
                    sp.wait_ge(acc_free, 5 + 20)
                    sp.wait_ge(ln_done[1], TILES)
                if 9 <= i:
                    sp.wait_ge(rt_ready, 4 * (i - 8))
                    sp.wait_ge(s_h1, 16 * TILES)
                sp.dma_start(eraw_view(i), dynamic_weights(0, i)).then_inc(s_eraw[i], 16)
            with sp.Fori(1, NE) as e:
                for i in range(ECH):
                    sp.wait_ge(elo_done, ECH * e - ECH + i + 1)
                    sp.dma_start(eraw_view(i), dynamic_weights(e, i)).then_inc(s_eraw[i], 16)
            sp.wait_ge(r_done, 1)
            n_over = sp.value_load(steer[0:1, NX:NX + 1], min_val=0, max_val=NX)
            with sp.Fori(0, NX) as b:
                with sp.If(b < n_over):
                    e = sp.value_load(steer[0:1, at(b, 1)], min_val=0, max_val=NE - 1)
                    for i in range(ECH):
                        sp.wait_ge(elo_done, ECH * (b + NE) - ECH + i + 1)
                        sp.dma_start(eraw_view(i), dynamic_weights(e, i)).then_inc(s_eraw[i], 16)
                sp.nop()

            sp.wait_ge(moe_end, 4)
            for i, v in enumerate((ln2_g, ln2_b)):
                sp.dma_start(gb[:, i, :], v.broadcast_to([P, D])).then_inc(s_gb2, 16)
            for t in range(TILES):
                s = STARTS[t]
                sp.dma_start(fin_h[:, t, :], h1_dram[s:s + P, :]).then_inc(s_fh[t], 16)
                for a in range(2):
                    sp.dma_start(fin_y[:, a, t, :], y_dram[a * T + s:a * T + s + P, :]).then_inc(s_fy[t], 16)
            out_rows = out.rearrange("b s d -> (b s) d")
            for t in range(TILES):
                lo, hi, r = own_rows(t)
                skip = META if t == 0 else 0
                sp.wait_ge(ln_done[2], t + 1)
                sp.dma_start(out_rows[lo + skip - META:hi - META, :], fin_h[r + skip:r + hi - lo, t, :]).then_inc(s_out, 16)
            sp.wait_ge(s_out, 16 * TILES)

        @block.gpsimd
        def _(pool):
            pool.dma_start(consts[:, :], k_small).then_inc(s_small, 16)
            pool.dma_start(colsrc[0:32, :], b_gate.rearrange("a (j p) -> (a j) p", p=P)).then_inc(s_small, 16)
            pool.dma_start(colsrc[32:40, :], pool_scale.rearrange("a (j p) -> (a j) p", p=P)).then_inc(s_small, 16)
            pool.dma_start(edge[:, :, :].rearrange("p g w -> p (g w)"), k_edge.broadcast_to([P, NG * 2 * PADW])).then_inc(s_small, 16)
            pool.dma_start(rbias[:, 0:NG], b_router_group.broadcast_to([P, NG])).then_inc(s_small, 16)
            pool.dma_start(rbias[:, NG:NG + NE], b_router_expert.broadcast_to([P, NE])).then_inc(s_small, 16)
            for i, v in enumerate((in_ln_g, in_ln_b)):
                pool.dma_start(gb[:, i, :], v.broadcast_to([P, D])).then_inc(s_gb, 16)
            for t in range(TILES):
                lo, hi, r = own_rows(t)
                pool.wait_ge(ln_done[0], t + 1)
                pool.dma_start(h0_dram[lo:hi, :], rows[r:r + hi - lo, t, :]).then_inc(s_h0, 16)
            pool.wait_ge(s_h0, 16 * TILES)

            def residual(n):
                for t in range(TILES):
                    s = STARTS[t]
                    pool.dma_start(resid[:, n % 2, t, :], h0_dram[s:s + P, 512 * n:512 * (n + 1)]).then_inc(s_res[n % 2], 16)

            pool.wait_ge(used, W0)
            residual(0)
            residual(1)
            pool.wait_ge(mt_lo, KC // 2)
            for i, v in enumerate((ln1_g, ln1_b)):
                pool.dma_start(gb[:, i, :], v.broadcast_to([P, D])).then_inc(s_gb, 16)
            for n in (2, 3):
                pool.wait_ge(acc_free, 5 + 5 * (n - 1))
                residual(n)
            pool.wait_ge(used, WEND)
            pool.dma_start(wrout[:, :, 0:NG], w_router_group[0].rearrange("(k p) n -> p k n", p=P)).then_inc(s_wr, 16)
            pool.dma_start(wrout[:, :, NG:NG + NE], w_router_expert[0].rearrange("(k p) n -> p k n", p=P)).then_inc(s_wr, 16)
            for t in range(TILES):
                lo, hi, r = own_rows(t)
                pool.wait_ge(ln_done[1], t + 1)
                pool.dma_start(h1_dram[lo:hi, :], rows[r:r + hi - lo, t, :]).then_inc(s_h1, 16)
            pool.wait_ge(s_h1, 16 * TILES)
            pool.wait_ge(rt_ready, 4 * TILES)
            pool.memset(xrow[:, :], 0.0).then_inc(pad_cols, 1)
            pool.memset(xT_hi[:, :, CAP:P].bitcast(F32), 0.0).then_inc(pad_cols, 1)
            pool.memset(xT_lo[:, :, CAP:P].bitcast(F32), 0.0).then_inc(pad_cols, 1)
            pool.memset(hT_hi[:, :, CAP:P].bitcast(F32), 0.0).then_inc(pad_cols, 1)
            pool.memset(hT_lo[:, :, CAP:P].bitcast(F32), 0.0).then_inc(pad_cols, 1)
            pool.wait_ge(pad_cols, 5)
            pool.wait_ge(r_done, 1)

            origin_reg = pool.alloc_register("origin")
            pool.reg_mov(origin_reg, 0)

            def gather(b):
                origin = pool.snap(origin_reg, min_val=0, max_val=1)
                pool.tensor_copy(gcur[:, :], gidx[:, at(b, 1)]).then_inc(idx_g, 1)
                pool.wait_ge(idx_g, b + 1)
                pool.indirect_dma_start(xrow[0:CAP, :], None, h1_dram, bass.IndirectOffsetOnAxis(gcur[:, :], 0),
                                        bounds_check=origin + (T - 1), oob_is_err=False).then_inc(gathered, 16)

            def moe_block(b):
                pool.wait_ge(xt_ready, 4 * b + 4)
                pool.wait_ge(gathered, 16 * b + 16)
                gather(b + 1)
                past(pool, scattered, 16 * b)
                origin = pool.snap(origin_reg, min_val=0, max_val=1)
                pool.tensor_copy(scur[:, :], sidx[:, at(b, 1)]).then_inc(idx_s, 1)
                pool.wait_ge(idx_s, b + 1)
                pool.wait_ge(y_done, 4 * b + 4)
                pool.indirect_dma_start(y_dram, bass.IndirectOffsetOnAxis(scur[:, :], 0), yrow[:, :], None,
                                        bounds_check=origin + (2 * T - 1), oob_is_err=False).then_inc(scattered, 16)

            gather(0)
            moe_block(0)
            with pool.Fori(1, NE) as b:
                moe_block(b)
            n_over = pool.value_load(steer[0:1, NX:NX + 1], min_val=0, max_val=NX)
            with pool.Fori(0, NX) as b:
                with pool.If(b < n_over):
                    moe_block(b + NE)
                pool.nop()
            pool.wait_ge(gathered, 16 * (n_over + (NE + 1)))
            pool.wait_ge(scattered, 16 * n_over + 16 * NE)
            pool.sem_inc(moe_end, 1)

        @block.scalar
        def _(act):
            def copy(dst, src, done, **kw):
                act.activation(dst, src, ACT.Copy, **kw).then_inc(done, 1)

            def layernorm(i):
                buf = rows if i < 2 else fin_h
                act.wait_ge(ln_mv[i], 1)
                act.activation(std[:, :], std[:, :], ACT.Sqrt).then_inc(ln_std[i], 1)
                act.wait_ge(ln_mv[i], 3)
                for t in range(TILES):
                    act.activation(buf[:, t, :], buf[:, t, :], ACT.Identity, bias=nmr[:, t:t + 1],
                                   scale=rstd[:, t:t + 1]).then_inc(ln_norm[i], 1)

            layernorm(0)
            act.wait_ge(cols_ready, 1)
            copy(cols[:, :], ps[:, 7, 0:40], cols_done)
            for t in range(TILES):
                for q in range(4):
                    act.wait_ge(tr_ready, 4 * t + q + 1)
                    copy(act_hi[:, 4 * q:4 * q + 4, STARTS[t]:STARTS[t] + P],
                         ps[:, q, :].rearrange("p (c n) -> p c n", n=P), tr_hi)

            def hi(base, i, loops, per, width=MC):
                n = base + i
                slot = n % RAW
                act.wait_ge(s_raw[slot], 16 * (n // RAW + 1) + (16 * per // RAW) * loops)
                if not (isinstance(loops, int) and n < RING):
                    act.wait_ge(used, n - RING + 1 + per * loops)
                copy(whi[:, n % RING, 0:width], raw[:, slot, 0:width], hi_done)

            def fourier_group(g):
                def u_evac(m):
                    act.wait_ge(used, F0 + 2 * m + 2 + FCH * g)
                    copy(chan_hi[:, m, :].rearrange("p (h n) -> p h n", h=2), ps[:, 2 * m:2 * m + 2, 0:HALF], fu_hi)

                for i in range(4):
                    hi(F0, i, g, FCH)
                u_evac(0)
                hi(F0, 4, g, FCH, 512)
                hi(F0, 5, g, FCH, 512)
                u_evac(1)
                hi(F0, 6, g, FCH, T)
                for t in range(TILES):
                    if t < TILES - 1:
                        act.wait_ge(fv_ready, 4 * g + t + 1)
                    else:
                        act.wait_ge(used, F0 + 6 + FCH * g)
                    copy(freq_hi[:, t, :], ps[:, (4 + t) % 8, :], fv_hi)
                for i in range(7, FCH):
                    hi(F0, i, g, FCH, T)
                for m in range(2):
                    if m == 0:
                        act.wait_ge(fo_ready, g + 1)
                    else:
                        act.wait_ge(used, F0 + FCH + FCH * g)
                    copy(mix_hi[:, at(8 + 2 * g + m, 1), :].rearrange("p a (h n) -> p (a h) n", h=2),
                         ps[:, 2 + 2 * m:4 + 2 * m, 0:HALF], fo_hi)

            fourier_group(0)
            with act.Fori(1, NG) as g:
                fourier_group(g)

            act.wait_ge(pad_zero, 1)
            for g in range(NG):
                for i in range(PCH):
                    hi(P0 + PCH * g, i, 0, 0, MC if i < 4 else GD)
                    if i in (3, 5):
                        m = (i - 3) // 2
                        n = 2 * g + m
                        act.wait_ge(used, P0 + PCH * g + 2 * m + 2)
                        if n:
                            act.wait_ge(pd_lo, n)
                        copy(stage[:, 0, PADW:PADW + T].rearrange("p (h n) -> p h n", h=2),
                             ps[:, 2 * m:2 * m + 2, 0:HALF], pu_copied)
                        act.wait_ge(pw_done, n + 1)
                        copy(mix_hi[:, n, :], stage[:, 1 + g % 2, 0:T], pd_hi)
                for m in range(2):
                    n = 2 * g + m
                    act.wait_ge(used, P0 + PCH * (g + 1))
                    act.activation(mix_hi[:, n, :].rearrange("p (h n) -> p h n", h=2), ps[:, 4 + 2 * m:6 + 2 * m, 0:HALF],
                                   ACT.Copy, scale=cols[:, 32 + n:33 + n]).then_inc(pm_hi, 1)

            act.wait_ge(pm_lo, 2 * NG)

            def gate_columns(jj):
                for b in range(2):
                    for i in range(JCH):
                        hi(J0 + JCH * b, i, jj, 2 * JCH)
                        if i in (3, 5):
                            a = (i - 3) // 2
                            act.wait_ge(used, J0 + JCH * b + 2 * a + 2 + 2 * JCH * jj)
                            past(act, mul_done, 4 * jj + 2 * b)
                            act.wait_ge(cols_done, 1)
                            act.activation(stage[:, a, 0:T].rearrange("p (h n) -> p h n", h=2),
                                           ps[:, 2 * a:2 * a + 2, 0:HALF], ACT.Sigmoid,
                                           bias=cols[:, at(16 * a + 2 * jj + b, 1)]).then_inc(gate_done, 1)

            gate_columns(0)
            with act.Fori(1, KC // 2) as jj:
                gate_columns(jj)

            def merged_hi(q):
                act.wait_ge(merge_done, 2 * q + 2)
                copy(act_hi[:, 2 * q:2 * q + 2, :], merged[:, 2 * q:2 * q + 2, :], mt_hi)

            act.wait_ge(used, J0 + JCH * (KC - 1) + 4)
            for q in range(6):
                merged_hi(q)
            hi(W0, 0, 0, 0)
            merged_hi(6)
            hi(W0, 1, 0, 0)
            merged_hi(7)
            for i in range(2, WCH):
                hi(W0, i, 0, 0)
            with act.Fori(1, 4) as n:
                for i in range(WCH):
                    hi(W0, i, n, WCH)

            layernorm(1)
            act.wait_ge(used, WEND)
            for t in range(TILES):
                for q in range(4):
                    act.wait_ge(rt_ready, 4 * t + q + 1)
                    if t >= 2 and q == 0:
                        act.wait_ge(lg_ready, t - 1)
                    copy(h1T[:, t % 2, 4 * q:4 * q + 4, :], ps[:, q, :].rearrange("p (c n) -> p c n", n=P), rt_done)
            act.wait_ge(r_gexp, 1)
            act.activation(gexp[:, :, :], gdif[:, :, :], ACT.Exp).then_inc(r_gexp, 1)
            act.wait_ge(r_eexp, 1)
            act.activation(eexp[:, :], ediff[:, :], ACT.Exp).then_inc(r_eexp, 1)
            act.wait_ge(r_done, 1)
            act.wait_ge(pad_cols, 5)

            def ehi_chunk(b, i):
                act.wait_ge(s_eraw[i], 16 * b + 16)
                act.wait_ge(eused, ECH * b + i + 1)
                copy(ehi[:, i % ERING, :], eraw[i][:, :], ehi_done)

            def xt_evac(b, q):
                act.wait_ge(xt_ready, 4 * b + q + 1)
                copy(xT_hi[:, 4 * q:4 * q + 4, 0:CAP], used_cols(ps[:, 6 + q % 2, :]), xt_hi)

            def y_evac(b):
                past(act, scattered, 16 * b)
                act.wait_ge(gcol_done, b + 1)
                for n in range(4):
                    if n < 3:
                        act.wait_ge(y_ready, 3 * b + n + 1)
                    else:
                        act.wait_ge(eused, ECH * b + ECH + ERING)
                    act.activation(yrow[:, 512 * n:512 * (n + 1)], ps[0:CAP, 2 + n, :], ACT.Copy,
                                   scale=gcol[:, :]).then_inc(y_done, 1)

            def moe_block(b, first=False):
                for i in range(4):
                    ehi_chunk(b, i)
                if not first:
                    y_evac(0 if isinstance(b, int) else b - 1)
                for i in range(4, 8):
                    ehi_chunk(b, i)
                act.wait_ge(eused, ECH * b + 4 + ERING)
                past(act, h_done, b)
                act.activation(srow[:, :], ps[:, 0, :], ACT.Silu).then_inc(silu_done, 1)
                for i in range(8, 12):
                    ehi_chunk(b, i)
                xt_evac(b + 1, 0)
                xt_evac(b + 1, 1)
                act.wait_ge(ht_ready, b + 1)
                copy(hT_hi[:, :, 0:CAP], used_cols(ps[:, 1, :]), ht_hi)
                xt_evac(b + 1, 2)
                xt_evac(b + 1, 3)

            for q in range(4):
                xt_evac(0, q)
            moe_block(0, True)
            with act.Fori(1, NE) as b:
                moe_block(b)
            n_over = act.value_load(steer[0:1, NX:NX + 1], min_val=0, max_val=NX)
            with act.Fori(0, NX) as b:
                with act.If(b < n_over):
                    moe_block(b + NE)
                act.nop()
            y_evac(n_over + (NE - 1))
            act.wait_ge(y_done, 4 * n_over + 4 * NE)
            act.wait_ge(xt_hi, 4 * n_over + 4 * (NE + 1))
            act.sem_inc(moe_end, 1)
            layernorm(2)

        @block.vector
        def _(dve):
            def lo_of(dst, src, hi, done):
                dve.tensor_tensor(dst, src, hi, ALU.subtract).then_inc(done, 1)

            def piece_stats(buf, t, n, done):
                dve.bn_stats(stats[:, t, n, :], buf[:, t, 512 * n:512 * (n + 1)]).then_inc(done, 1)

            def layernorm(i, n_stats, s_stats):
                buf = rows if i < 2 else fin_h
                dve.wait_ge(s_stats, n_stats)
                for t in range(TILES):
                    dve.bn_aggr(mv[:, t, :], stats[:, t, :, :].rearrange("p a b -> p (a b)")).then_inc(s_agg[i], 1)
                dve.wait_ge(s_agg[i], TILES)
                dve.tensor_scalar(std[:, :], mv[:, :, 1], EPS, None, ALU.add).then_inc(ln_mv[i], 1)
                dve.wait_ge(ln_std[i], 1)
                dve.reciprocal(rstd[:, :], std[:, :]).then_inc(ln_mv[i], 1)
                dve.wait_ge(ln_mv[i], 2)
                dve.scalar_tensor_tensor(out=nmr[:, :], in0=mv[:, :, 0], scalar=-1.0, in1=rstd[:, :],
                                         op0=ALU.mult, op1=ALU.mult).then_inc(ln_mv[i], 1)
                if i < 2:
                    dve.wait_ge(s_gb, 32 * (i + 1))
                else:
                    dve.wait_ge(s_gb2, 32)
                for t in range(TILES):
                    dve.wait_ge(ln_norm[i], t + 1)
                    dve.tensor_tensor(buf[:, t, :], buf[:, t, :], gb[:, 0, :], ALU.mult).then_inc(ln_g[i], 1)
                    dve.wait_ge(ln_g[i], t + 1)
                    dve.tensor_tensor(buf[:, t, :], buf[:, t, :], gb[:, 1, :], ALU.add).then_inc(ln_done[i], 1)

            dve.sem_inc(acc_free, 5)
            for t in range(TILES):
                dve.wait_ge(s_row[t], 32 if t == 0 else 16)
                for n in range(4):
                    piece_stats(rows, t, n, s_ln0)
            layernorm(0, 4 * TILES, s_ln0)
            for t in range(TILES):
                for q in range(4):
                    dve.wait_ge(tr_hi, 4 * t + q + 1)
                    sl = slice(STARTS[t], STARTS[t] + P)
                    lo_of(act_lo[:, 4 * q:4 * q + 4, sl], ps[:, q, :].rearrange("p (c n) -> p c n", n=P),
                          act_hi[:, 4 * q:4 * q + 4, sl], tr_lo)

            def lo(base, i, loops, per, width=MC):
                n = base + i
                dve.wait_ge(hi_done, n + 1 + per * loops)
                lo_of(wlo[:, n % RING, 0:width], raw[:, n % RAW, 0:width], whi[:, n % RING, 0:width], lo_done)

            def fourier_group(g):
                def u_evac(m):
                    dve.wait_ge(fu_hi, 2 * g + m + 1)
                    lo_of(chan_lo[:, m, :].rearrange("p (h n) -> p h n", h=2), ps[:, 2 * m:2 * m + 2, 0:HALF],
                          chan_hi[:, m, :].rearrange("p (h n) -> p h n", h=2), fu_lo)

                for i in range(4):
                    lo(F0, i, g, FCH)
                u_evac(0)
                lo(F0, 4, g, FCH, 512)
                lo(F0, 5, g, FCH, 512)
                u_evac(1)
                lo(F0, 6, g, FCH, T)
                for t in range(TILES):
                    dve.wait_ge(fv_hi, TILES * g + t + 1)
                    lo_of(freq_lo[:, t, :], ps[:, (4 + t) % 8, :], freq_hi[:, t, :], fv_lo)
                for i in range(7, FCH):
                    lo(F0, i, g, FCH, T)
                for m in range(2):
                    dve.wait_ge(fo_hi, 2 * g + m + 1)
                    v = [z[:, at(8 + 2 * g + m, 1), :].rearrange("p a (h n) -> p (a h) n", h=2) for z in (mix_lo, mix_hi)]
                    lo_of(v[0], ps[:, 2 + 2 * m:4 + 2 * m, 0:HALF], v[1], fo_lo)

            fourier_group(0)
            with dve.Fori(1, NG) as g:
                fourier_group(g)

            dve.memset(stage[:, 0, :], 0.0).then_inc(pad_zero, 1)
            steps = 0

            def pstep(ins):
                nonlocal steps
                steps += 1
                ins.then_inc(pw_step, 1)
                dve.wait_ge(pw_step, steps)

            def window(g, n):
                w = 2 ** (g + 1)
                dve.wait_ge(pu_copied, n + 1)
                src, width, shift = 0, UW, 1
                for s in range(g + 1):
                    dst = 2 - s % 2
                    width -= shift
                    pstep(dve.tensor_tensor(stage[:, dst, 0:width], stage[:, src, 0:width],
                                            stage[:, src, shift:shift + width], ALU.add))
                    src, shift = dst, shift * 2
                a = PADW - w // 2
                res = stage[:, src, a:a + T]
                for k, c in ((0, 0), (1, T - PADW)):
                    pstep(dve.tensor_tensor(res[:, c:c + PADW], res[:, c:c + PADW],
                                            edge[:, g, PADW * k:PADW * (k + 1)], ALU.mult))
                dst = 3 - src
                dve.scalar_tensor_tensor(out=stage[:, dst, 0:T], in0=res, scalar=1.0 / w,
                                         in1=stage[:, 0, PADW:PADW + T], op0=ALU.mult,
                                         op1=ALU.subtract).then_inc(pw_done, 1)
                assert dst == 1 + g % 2, (g, src, dst)
                dve.wait_ge(pd_hi, n + 1)
                lo_of(mix_lo[:, n, :], stage[:, dst, 0:T], mix_hi[:, n, :], pd_lo)

            dve.wait_ge(s_small, 16 * 6)
            for g in range(NG):
                for i in range(PCH):
                    lo(P0 + PCH * g, i, 0, 0, MC if i < 4 else GD)
                    if i in (3, 5):
                        window(g, 2 * g + (i - 3) // 2)
                for m in range(2):
                    n = 2 * g + m
                    dve.wait_ge(pm_hi, n + 1)
                    dve.scalar_tensor_tensor(out=mix_lo[:, n, :].rearrange("p (h n) -> p h n", h=2),
                                             in0=ps[:, 4 + 2 * m:6 + 2 * m, 0:HALF], scalar=cols[:, 32 + n:33 + n],
                                             in1=mix_hi[:, n, :].rearrange("p (h n) -> p h n", h=2),
                                             op0=ALU.mult, op1=ALU.subtract).then_inc(pm_lo, 1)

            def gate_half(a, dst, jj, b):
                dve.wait_ge(used, J0 + JCH * b + 5 + a + 2 * JCH * jj)
                dve.wait_ge(gate_done, 4 * jj + 2 * b + a + 1)
                dve.tensor_tensor(dst, halved(stage[:, a, 0:T]), ps[:, 4 + 2 * a:6 + 2 * a, 0:HALF],
                                  ALU.mult).then_inc(mul_done, 1)

            def halved(ap):
                return ap.rearrange("p (h n) -> p h n", h=2)

            def column(jj, b):
                return merged[:, at(2 * jj + b, 1), :].rearrange("p a (h n) -> p (a h) n", h=2)

            def finish_column(jj, b):
                gate_half(1, halved(stage[:, 2, 0:T]), jj, b)
                dve.wait_ge(mul_done, 4 * jj + 2 * b + 2)
                dve.tensor_tensor(column(jj, b), column(jj, b), halved(stage[:, 2, 0:T]), ALU.add).then_inc(merge_done, 1)

            def gate_columns(jj):
                for b in range(2):
                    lo(J0 + JCH * b, 0, jj, 2 * JCH)
                    if b or not isinstance(jj, int):
                        finish_column(jj if b else jj - 1, 1 - b)
                    for i in range(1, JCH):
                        lo(J0 + JCH * b, i, jj, 2 * JCH)
                    past(dve, merge_done, 2 * jj + b)
                    gate_half(0, column(jj, b), jj, b)

            gate_columns(0)
            with dve.Fori(1, KC // 2) as jj:
                gate_columns(jj)

            def merged_lo(q):
                dve.wait_ge(mt_hi, q + 1)
                lo_of(act_lo[:, 2 * q:2 * q + 2, :], merged[:, 2 * q:2 * q + 2, :], act_hi[:, 2 * q:2 * q + 2, :], mt_lo)

            for q in range(6):
                merged_lo(q)
            lo(W0, 0, 0, 0)
            finish_column(KC // 2 - 1, 1)
            merged_lo(6)
            lo(W0, 1, 0, 0)
            merged_lo(7)
            for n in range(4):
                for i in range(2 if n == 0 else 0, WCH):
                    lo(W0 + WCH * n, i, 0, 0)
                dve.wait_ge(s_res[n % 2], 16 * TILES * (n // 2 + 1))
                for t in range(TILES):
                    if t < TILES - 1:
                        dve.wait_ge(acc_ready, 4 * n + t + 1)
                    else:
                        dve.wait_ge(used, W0 + WCH * (n + 1))
                    dve.scalar_tensor_tensor(out=rows[:, t, 512 * n:512 * (n + 1)], in0=resid[:, n % 2, t, :],
                                             scalar=ALPHA, in1=ps[:, t, :], op0=ALU.mult,
                                             op1=ALU.add).then_inc(acc_free, 1)
                    dve.wait_ge(acc_free, 5 + 5 * n + t + 1)
                    piece_stats(rows, t, n, bn_done)
            layernorm(1, 4 * TILES, bn_done)

            dve.wait_ge(used, WEND)
            for t in range(TILES):
                dve.wait_ge(lg_ready, t + 1)
                dve.tensor_tensor(logit[:, t, :], ps[:, 4 + t % 4, 0:NG + NE], rbias[:, :], ALU.add).then_inc(lg_done, 1)
            dve.wait_ge(lg_done, TILES)
            rsteps = 0

            def r(ins):
                nonlocal rsteps
                rsteps += 1
                ins.then_inc(r_step, 1)
                dve.wait_ge(r_step, rsteps)

            def wide(ap, n):
                shape = list(ap.shape)
                return ap.unsqueeze(len(shape)).broadcast_to(shape + [n])

            def over_tiles(ap, n):
                return ap.unsqueeze(1).broadcast_to([ap.shape[0], n, ap.shape[1]])

            gl, el = logit[:, :, 0:NG], logit[:, :, NG:NG + NE]
            r(dve.memset(ones[:, :], 1.0))
            r(dve.tensor_reduce(gmax[:, :], gl, AX, ALU.max))
            dve.tensor_tensor(gdif[:, :, :], gl, wide(gmax[:, :], NG), ALU.subtract).then_inc(r_gexp, 1)
            r(dve.tensor_tensor(gone[:, :, :], gl, wide(gmax[:, :], NG), ALU.is_equal))
            r(dve.tensor_tensor(gone[:, :, :], gone[:, :, :], over_tiles(const("r4"), TILES), ALU.mult))
            r(dve.tensor_reduce(gpick[:, :], gone[:, :, :], AX, ALU.max))
            r(dve.tensor_tensor(gone[:, :, :], gone[:, :, :], wide(gpick[:, :], NG), ALU.is_equal))
            r(dve.tensor_scalar(gone[:, :, :], gone[:, :, :], -1.0, BIG, ALU.add, ALU.mult))
            for t in range(TILES):
                r(dve.tensor_tensor(masked[:, t, :].rearrange("p (g e) -> p g e", e=EG),
                                    el[:, t, :].rearrange("p (g e) -> p g e", e=EG), wide(gone[:, t, :], EG), ALU.add))
            for a in range(2):
                src = (masked, masked2)[a]
                r(dve.tensor_reduce(emax[:, a, :], src[:, :, :], AX, ALU.max))
                r(dve.tensor_tensor(etmp[:, :, :], src[:, :, :], wide(emax[:, a, :], NE), ALU.is_equal))
                r(dve.tensor_tensor(etmp[:, :, :], etmp[:, :, :], over_tiles(const("r32"), TILES), ALU.mult))
                r(dve.tensor_reduce(epick[:, a, :], etmp[:, :, :], AX, ALU.max))
                r(dve.tensor_tensor(one[:, a, :, :], etmp[:, :, :], wide(epick[:, a, :], NE), ALU.is_equal))
                if a == 0:
                    r(dve.scalar_tensor_tensor(out=masked2[:, :, :], in0=one[:, 0, :, :], scalar=-2 * BIG,
                                               in1=masked[:, :, :], op0=ALU.mult, op1=ALU.add))
                r(dve.tensor_tensor(one[:, a, :, :], one[:, a, :, :], wide(const("valid"), NE), ALU.mult))
            dve.tensor_tensor(ediff[:, :], emax[:, 1, :], emax[:, 0, :], ALU.subtract).then_inc(r_eexp, 1)
            dve.tensor_tensor(anyone[:, :, :], one[:, 0, :, :], one[:, 1, :, :], ALU.add).then_inc(r_any, 1)
            dve.wait_ge(r_gexp, 2)
            r(dve.tensor_reduce(gsum[:, :], gexp[:, :, :], AX, ALU.add))
            dve.wait_ge(r_eexp, 2)
            r(dve.tensor_scalar(esum[:, :], eexp[:, :], 1.0, None, ALU.add))
            r(dve.tensor_tensor(gsum[:, :], gsum[:, :], esum[:, :], ALU.mult))
            r(dve.reciprocal(gprob[:, :], gsum[:, :]))
            r(dve.tensor_tensor(gate[:, 0, :], gprob[:, :], const("valid"), ALU.mult))
            r(dve.tensor_tensor(gate[:, 1, :], gate[:, 0, :], eexp[:, :], ALU.mult))
            dve.wait_ge(r_pos, 1)
            r(dve.tensor_copy(posn[:, :, :], ps[:, 5, 0:TILES * NE].rearrange("p (t e) -> p t e", e=NE)))
            r(dve.tensor_copy(count[:, :], ps[:, 5, TILES * NE:TILES * NE + NE]))
            for k in range(8):
                r(dve.tensor_scalar(over[:, k, :], count[:, :], float(CAP * (k + 1)), None, ALU.is_gt))
            r(dve.tensor_reduce(nover[:, :], over[:, :, :].rearrange("p k e -> p e k"), AX, ALU.add))
            r(dve.tensor_tensor_scan(cum[:, :], ones[:, 0:NE], nover[:, :], 0.0, ALU.mult, ALU.add))
            r(dve.tensor_tensor(excl[:, :], cum[:, :], nover[:, :], ALU.subtract))

            def pick(dst, values):
                for a in range(2):
                    v = values if len(values.shape) == 3 else over_tiles(values, TILES)
                    r(dve.tensor_tensor(prod[:, a, :, :], one[:, a, :, :], v, ALU.mult))
                r(dve.tensor_reduce(dst[:, :, :], prod[:, :, :, :], AX, ALU.add))

            pick(apos, posn[:, :, :])
            pick(aexp, const("e32"))
            pick(aexc, excl[:, :])
            flat = lambda b: b[:, :, :].rearrange("p a t -> p (a t)")
            for k in range(8):
                r(dve.tensor_scalar(step8[:, k, :], flat(apos), float(CAP * (k + 1)), None, ALU.is_ge))
            r(dve.tensor_reduce(flat(turn), step8[:, :, :].rearrange("p k n -> p n k"), AX, ALU.add))
            r(dve.scalar_tensor_tensor(out=flat(aslot), in0=flat(turn), scalar=-float(CAP), in1=flat(apos),
                                       op0=ALU.mult, op1=ALU.add))
            r(dve.tensor_scalar(flat(turn1), flat(turn), 1.0, None, ALU.min))
            r(dve.scalar_tensor_tensor(out=flat(ablock), in0=flat(aexc), scalar=float(NE - 1), in1=flat(aexp),
                                       op0=ALU.add, op1=ALU.subtract))
            r(dve.tensor_tensor(flat(ablock), flat(ablock), flat(turn1), ALU.mult))
            r(dve.tensor_tensor(flat(ablock), flat(ablock), flat(aexp), ALU.add))
            r(dve.tensor_tensor(flat(ablock), flat(ablock), flat(turn), ALU.add))
            r(dve.tensor_tensor(slot1[:, :, :], over_tiles(const("slot"), 2 * TILES), wide(flat(aslot), CAP), ALU.is_equal))
            r(dve.tensor_tensor(block1[:, :, :], over_tiles(const("block"), 2 * TILES), wide(flat(ablock), NTAB), ALU.is_equal))
            for a in range(2):
                r(dve.tensor_tensor(block1[:, TILES * a:TILES * (a + 1), :], block1[:, TILES * a:TILES * (a + 1), :],
                                    wide(const("valid"), NTAB), ALU.mult))
            r(dve.tensor_tensor(block2[:, :, 0, :], block1[:, :, :], wide(const("token"), NTAB), ALU.mult))
            dve.tensor_tensor(block2[:, :, 1, :], block1[:, :, :], wide(flat(gate), NTAB), ALU.mult).then_inc(r_hot, 1)
            for k in range(NX):
                r(dve.tensor_scalar(below[:, k, :], cum[:, :], float(k), None, ALU.is_le))
            r(dve.tensor_reduce(steerf[:, 0:NX], below[:, :, :], AX, ALU.add))
            r(dve.tensor_scalar(steerf[:, 0:NX], steerf[:, 0:NX], float(NE - 1), None, ALU.min))
            r(dve.tensor_copy(steerf[:, NX:NX + 1], cum[:, NE - 1:NE]))
            r(dve.tensor_copy(steer[:, :], steerf[0:1, :]))
            dve.wait_ge(r_table, 1)
            r(dve.tensor_copy(table[:, :, :], ps[0:CAP, 6, 0:2 * NTAB].rearrange("p (a n) -> p a n", a=2)))
            r(dve.tensor_scalar(none[:, :], table[:, 0, :], 0.0, float(EMPTY), ALU.is_equal, ALU.mult))
            r(dve.scalar_tensor_tensor(out=sidxf[:, :], in0=table[:, 0, :], scalar=-1.0, in1=none[:, :],
                                       op0=ALU.add, op1=ALU.add))
            r(dve.tensor_scalar(second[:, :], sidxf[:, :], float(T), -float(T), ALU.is_ge, ALU.mult))
            r(dve.tensor_tensor(gidxf[:, :], sidxf[:, :], second[:, :], ALU.add))
            r(dve.tensor_copy(gidx[:, :], gidxf[:, :]))
            r(dve.tensor_copy(sidx[:, :], sidxf[:, :]))
            r(dve.tensor_copy(gatew[:, :], table[:, 1, :]))
            dve.sem_inc(r_done, 1)
            dve.wait_ge(pad_cols, 5)

            def elo_chunk(b, i):
                dve.wait_ge(ehi_done, ECH * b + i + 1)
                lo_of(elo[:, i % ERING, :], eraw[i][:, :], ehi[:, i % ERING, :], elo_done)

            def xt_evac(b, q):
                dve.wait_ge(xt_hi, 4 * b + q + 1)
                lo_of(xT_lo[:, 4 * q:4 * q + 4, 0:CAP], used_cols(ps[:, 6 + q % 2, :]),
                      xT_hi[:, 4 * q:4 * q + 4, 0:CAP], xt_lo)

            def moe_block(b):
                for i in range(11):
                    elo_chunk(b, i)
                dve.wait_ge(silu_done, b + 1)
                dve.wait_ge(eused, ECH * b + 8 + ERING)
                past(dve, ht_lo, b)
                dve.tensor_tensor(hrow[:, :], srow[:, :], ps[:, 1, :], ALU.mult).then_inc(h_done, 1)
                elo_chunk(b, 11)
                xt_evac(b + 1, 0)
                xt_evac(b + 1, 1)
                dve.wait_ge(ht_hi, b + 1)
                lo_of(hT_lo[:, :, 0:CAP], used_cols(ps[:, 1, :]), hT_hi[:, :, 0:CAP], ht_lo)
                xt_evac(b + 1, 2)
                xt_evac(b + 1, 3)
                past(dve, y_done, 4 * b)
                dve.tensor_scalar(gcol[:, :], gatew[:, at(b, 1)], 1.0, None, ALU.mult).then_inc(gcol_done, 1)

            for q in range(4):
                xt_evac(0, q)
            moe_block(0)
            with dve.Fori(1, NE) as b:
                moe_block(b)
            n_over = dve.value_load(steer[0:1, NX:NX + 1], min_val=0, max_val=NX)
            with dve.Fori(0, NX) as b:
                with dve.If(b < n_over):
                    moe_block(b + NE)
                dve.nop()
            dve.wait_ge(xt_lo, 4 * n_over + 4 * (NE + 1))
            dve.wait_ge(elo_done, ECH * n_over + ECH * NE)
            dve.sem_inc(moe_end, 1)

            for t in range(TILES):
                dve.wait_ge(s_fh[t], 16)
                dve.wait_ge(s_fy[t], 32)
                dve.scalar_tensor_tensor(out=fin_h[:, t, :], in0=fin_h[:, t, :], scalar=ALPHA, in1=fin_y[:, 0, t, :],
                                         op0=ALU.mult, op1=ALU.add).then_inc(f_sum, 1)
                dve.wait_ge(f_sum, 2 * t + 1)
                dve.tensor_tensor(fin_h[:, t, :], fin_h[:, t, :], fin_y[:, 1, t, :], ALU.add).then_inc(f_sum, 1)
                dve.wait_ge(f_sum, 2 * t + 2)
                for n in range(4):
                    piece_stats(fin_h, t, n, s_ln2)
            layernorm(2, 4 * TILES, s_ln2)

        @block.tensor
        def _(pe):
            def product(outs, l_hi, l_lo, r_hi, r_lo, start, stop):
                last = None
                for k, (l, r) in enumerate(((l_hi, r_hi), (l_hi, r_lo), (l_lo, r_hi))):
                    for o, rr in zip(outs, r, strict=True):
                        last = pe.matmul(o, l, rr, start=start and k == 0, stop=stop and k == 2)
                return last

            def halves(buf, k):
                return [buf[:, k, 0:HALF], buf[:, k, HALF:T]]

            pe.wait_ge(s_small, 16 * 6)
            pe.transpose(ps[:, 7, 0:40], colsrc[:, :], ident[0:40, 0:40]).then_inc(cols_ready, 1)
            for t in range(TILES):
                pe.wait_ge(ln_done[0], t + 1)
                for q in range(4):
                    if t:
                        pe.wait_ge(tr_lo, 4 * (t - 1) + q + 1)
                    for c in range(4):
                        k = 4 * q + c
                        last = pe.transpose(ps[:, q, P * c:P * (c + 1)], rows[:, t, P * k:P * (k + 1)], ident)
                    last.then_inc(tr_ready, 1)
            pe.wait_ge(tr_lo, 4 * TILES)
            pe.wait_ge(s_h0, 16 * TILES)

            def project(base, i0, loops, per, bank):
                for half in range(2):
                    n = base + i0 + half
                    pe.wait_ge(lo_done, n + 1 + per * loops)
                    for k in range(8):
                        last = product([ps[:, bank, 0:HALF], ps[:, bank + 1, 0:HALF]],
                                       whi[:, n % RING, P * k:P * (k + 1)], wlo[:, n % RING, P * k:P * (k + 1)],
                                       halves(act_hi, 8 * half + k), halves(act_lo, 8 * half + k),
                                       half == 0 and k == 0, half == 1 and k == 7)
                    last.then_inc(used, 1)
                return last

            def fourier_group(g):
                for m in range(2):
                    if m == 0:
                        past(pe, fv_lo, TILES * g)
                    else:
                        past(pe, fo_lo, 2 * g)
                    project(F0, 2 * m, g, FCH, 2 * m)
                for m in range(2):
                    n = F0 + 4 + m
                    pe.wait_ge(lo_done, n + 1 + FCH * g)
                    pe.wait_ge(fu_lo, 2 * g + m + 1)
                    for t, s in enumerate(STARTS):
                        last = product([ps[:, (4 + t) % 8, :]], chan_hi[:, m, s:s + P], chan_lo[:, m, s:s + P],
                                       [whi[:, n % RING, 0:512]], [wlo[:, n % RING, 0:512]], m == 0, m == 1)
                        if m == 1 and t < TILES - 1:
                            last.then_inc(fv_ready, 1)
                    last.then_inc(used, 1)
                for t in range(TILES):
                    pe.wait_ge(fv_lo, TILES * g + max(t + 1, 2))
                    for cs in range(2):
                        n = F0 + 6 + 2 * t + cs
                        pe.wait_ge(lo_done, n + 1 + FCH * g)
                        for m in range(2):
                            c = GD * cs + P * m
                            last = product([ps[:, 2 + 2 * m, 0:HALF], ps[:, 3 + 2 * m, 0:HALF]],
                                           freq_hi[:, t, c:c + P], freq_lo[:, t, c:c + P],
                                           [whi[:, n % RING, 0:HALF], whi[:, n % RING, HALF:T]],
                                           [wlo[:, n % RING, 0:HALF], wlo[:, n % RING, HALF:T]],
                                           t == 0 and cs == 0, t == TILES - 1 and cs == 1)
                            if t == TILES - 1 and cs == 1 and m == 0:
                                last.then_inc(fo_ready, 1)
                        last.then_inc(used, 1)

            fourier_group(0)
            with pe.Fori(1, NG) as g:
                fourier_group(g)
            pe.wait_ge(fo_lo, 2 * NG)

            def pool_group(g):
                for m in range(2):
                    past(pe, pu_copied, 2 * g)
                    project(P0, 2 * m, g, PCH, 2 * m)
                past(pe, pm_lo, 2 * g)
                for k in range(2):
                    n = P0 + 4 + k
                    pe.wait_ge(lo_done, n + 1 + PCH * g)
                    pe.wait_ge(pd_lo, 2 * g + k + 1)
                    hi = [mix_hi[:, at(2 * g + k, 1), h * HALF:(h + 1) * HALF].rearrange("p a n -> p (a n)") for h in range(2)]
                    lo = [mix_lo[:, at(2 * g + k, 1), h * HALF:(h + 1) * HALF].rearrange("p a n -> p (a n)") for h in range(2)]
                    for m in range(2):
                        last = product([ps[:, 4 + 2 * m, 0:HALF], ps[:, 5 + 2 * m, 0:HALF]],
                                       whi[:, n % RING, P * m:P * (m + 1)], wlo[:, n % RING, P * m:P * (m + 1)],
                                       hi, lo, k == 0, k == 1)
                    last.then_inc(used, 1)

            pool_group(0)
            with pe.Fori(1, NG) as g:
                pool_group(g)
            pe.wait_ge(pm_lo, 2 * NG)

            def gate_column(j):
                for a in range(2):
                    past(pe, gate_done, 2 * j)
                    project(J0, 2 * a, j, JCH, 2 * a)
                for a in range(2):
                    n = J0 + 4 + a
                    pe.wait_ge(lo_done, n + 1 + JCH * j)
                    past(pe, mul_done, 2 * j)
                    for k in range(8):
                        last = product([ps[:, 4 + 2 * a, 0:HALF], ps[:, 5 + 2 * a, 0:HALF]],
                                       whi[:, n % RING, P * k:P * (k + 1)], wlo[:, n % RING, P * k:P * (k + 1)],
                                       halves(mix_hi, 8 * a + k), halves(mix_lo, 8 * a + k), k == 0, k == 7)
                    last.then_inc(used, 1)

            gate_column(0)
            with pe.Fori(1, KC) as j:
                gate_column(j)

            pe.wait_ge(mul_done, 2 * KC)
            def out_block(n):
                for i in range(WCH):
                    c = W0 + i
                    if isinstance(n, int):
                        pe.wait_ge(mt_lo, i + 1)
                    pe.wait_ge(lo_done, c + 1 + WCH * n)
                    for t, s in enumerate(STARTS):
                        if i == 0:
                            pe.wait_ge(acc_free, 5 * n + t + 1)
                        for kk in range(2):
                            k = 2 * i + kk
                            last = product([ps[:, t, :]], act_hi[:, k, s:s + P], act_lo[:, k, s:s + P],
                                           [whi[:, c % RING, 512 * kk:512 * (kk + 1)]],
                                           [wlo[:, c % RING, 512 * kk:512 * (kk + 1)]],
                                           i == 0 and kk == 0, i == WCH - 1 and kk == 1)
                        if i == WCH - 1 and t < TILES - 1:
                            last.then_inc(acc_ready, 1)
                    last.then_inc(used, 1)

            out_block(0)
            with pe.Fori(1, 4) as n:
                out_block(n)

            pe.wait_ge(acc_free, 5 + 20)
            pe.wait_ge(s_wr, 32)
            for t in range(TILES):
                pe.wait_ge(ln_done[1], t + 1)
                for q in range(4):
                    if t:
                        pe.wait_ge(rt_done, 4 * (t - 1) + q + 1)
                    for c in range(4):
                        k = 4 * q + c
                        last = pe.transpose(ps[:, q, P * c:P * (c + 1)], rows[:, t, P * k:P * (k + 1)], ident)
                    last.then_inc(rt_ready, 1)
                pe.wait_ge(rt_done, 4 * t + 4)
                if t == 4:
                    pe.wait_ge(lg_done, 1)
                for k in range(KC):
                    last = pe.matmul(ps[:, 4 + t % 4, 0:NG + NE], h1T[:, t % 2, k, :], wrout[:, k, :],
                                     start=k == 0, stop=k == KC - 1)
                last.then_inc(lg_ready, 1)
            pe.wait_ge(r_any, 1)
            pe.wait_ge(lg_done, TILES)
            for t in range(TILES):
                for s in range(t + 1):
                    pe.matmul(ps[:, 5, NE * t:NE * (t + 1)], const("ltri") if s == t else ones[:, :], anyone[:, s, :],
                              start=s == 0, stop=s == t)
            for s in range(TILES):
                last = pe.matmul(ps[:, 5, NE * TILES:NE * (TILES + 1)], ones[:, :], anyone[:, s, :],
                                 start=s == 0, stop=s == TILES - 1)
            last.then_inc(r_pos, 1)
            pe.wait_ge(r_hot, 1)
            for n in range(2 * TILES):
                last = pe.matmul(ps[0:CAP, 6, 0:2 * NTAB], slot1[:, n, :],
                                 block2[:, n, :, :].rearrange("p a n -> p (a n)"), start=n == 0, stop=n == 2 * TILES - 1)
            last.then_inc(r_table, 1)
            pe.wait_ge(r_done, 1)
            pe.sem_inc(eused, ERING)

            def xt(b, q):
                if q == 0:
                    pe.wait_ge(gathered, 16 * b + 16)
                past(pe, xt_lo, 4 * b + q - 1 if q else 4 * b)
                pe.wait_ge(pad_cols, 5)
                for c in range(4):
                    k = 4 * q + c
                    last = pe.transpose(ps[:, 6 + q % 2, P * c:P * (c + 1)], xrow[:, P * k:P * (k + 1)], ident)
                last.then_inc(xt_ready, 1)

            def moe_block(b):
                pe.wait_ge(xt_lo, 4 * b + 4)
                for i in range(8):
                    pe.wait_ge(elo_done, ECH * b + i + 1)
                    if i == 0:
                        past(pe, silu_done, b)
                    if i == 4:
                        past(pe, ht_lo, b)
                    for kk in range(4):
                        k = 4 * (i % 4) + kk
                        last = product([ps[:, i // 4, :]], xT_hi[:, k, :], xT_lo[:, k, :],
                                       [ehi[:, i % ERING, F * kk:F * (kk + 1)]],
                                       [elo[:, i % ERING, F * kk:F * (kk + 1)]], k == 0, k == KC - 1)
                    last.then_inc(eused, 1)
                xt(b + 1, 0)
                xt(b + 1, 1)
                pe.wait_ge(h_done, b + 1)
                pe.wait_ge(pad_cols, 5)
                for c in range(4):
                    last = pe.transpose(ps[:, 1, P * c:P * (c + 1)], hrow[:, P * c:P * (c + 1)], ident)
                last.then_inc(ht_ready, 1)
                for i in range(8, 12):
                    if i == 8:
                        pe.wait_ge(ht_lo, b + 1)
                    if i in (9, 10):
                        xt(b + 1, i - 7)
                    pe.wait_ge(elo_done, ECH * b + i + 1)
                    for n in range(4):
                        if i == 8:
                            past(pe, y_done, 4 * b)
                        last = product([ps[:, 2 + n, :]], hT_hi[:, i - 8, :], hT_lo[:, i - 8, :],
                                       [ehi[:, i % ERING, 512 * n:512 * (n + 1)]],
                                       [elo[:, i % ERING, 512 * n:512 * (n + 1)]], i == 8, i == 11)
                        if i == 11 and n < 3:
                            last.then_inc(y_ready, 1)
                    last.then_inc(eused, 1)

            for q in range(4):
                xt(0, q)
            moe_block(0)
            with pe.Fori(1, NE) as b:
                moe_block(b)
            n_over = pe.value_load(steer[0:1, NX:NX + 1], min_val=0, max_val=NX)
            with pe.Fori(0, NX) as b:
                with pe.If(b < n_over):
                    moe_block(b + NE)
                pe.nop()
            pe.wait_ge(eused, ECH * n_over + (ECH * NE + ERING))
            pe.sem_inc(moe_end, 1)


_INS = ["x", "meta_tokens", "in_ln_g", "in_ln_b", "w_in", "b_gate", "w_pool_group", "pool_scale", "w_branch_pool",
        "w_branch_fourier", "w_out", "ln1_g", "ln1_b", "w_router_group", "b_router_group", "w_router_expert",
        "b_router_expert", "w_gate", "w_up", "w_down", "ln2_g", "ln2_b"]


def kernel(**inputs):
    import concourse.bacc as _bacc
    from concourse.bass_utils import run_bass_kernel_spmd as _run

    nc = _bacc.Bacc("TRN2", target_bir_lowering=False, num_devices=1)
    small, chan, pos, edge = shape_constants()
    arrays, args = {}, []

    def add(name, a):
        arrays[name] = a
        args.append(nc.dram_tensor(name, a.shape, mybir.dt.from_np(a.dtype), kind="ExternalInput").ap())

    for name in _INS:
        a = np.ascontiguousarray(inputs[name])
        if a.ndim == 1:
            a = a.reshape(1, -1)
        add(f"in_{name}", a)
    add("k_small", small)
    add("k_chan", chan)
    add("k_pos", pos)
    add("k_edge", edge.reshape(1, -1))
    args.append(nc.dram_tensor("out", (1, SEQ, D), F32, kind="ExternalOutput").ap())
    encoder_kernel(nc, *args)
    r = _run(nc, [arrays], core_ids=[0])
    return r.results[0]["out"]
```

```python
from contextlib import ExitStack

import concourse.bass as bass
import numpy as np
from concourse import mybir

F32 = mybir.dt.float32
F32R = mybir.dt.float32r
U32 = mybir.dt.uint32
I32 = mybir.dt.int32
ALU = mybir.AluOpType
ACT = mybir.ActivationFunctionType
AX = mybir.AxisListType.X

P = 128
D = 2048
SEQ = 512
META = 16
T = SEQ + META
TILES = 5
STARTS = [0, 128, 256, 384, T - P]
KC = D // P
HALF = T // 2
NG = 4
GD = 256
W2 = NG * GD
NE = 32
EG = 8
F = D // 4
CAP = 64
NX = 2 * T // (CAP + 1)
NB = NE + NX
NTAB = NB + 1
ALPHA = 2.0 ** 0.25
EPS = 1e-5
BIG = 1e30
EMPTY = 8192

MC = 1024
RAW, RING = 4, 2
EC = 2048
ECH = 12
ERING = 4

FCH, PCH, JCH, WCH = 16, 6, 6, 8
F0 = 0
P0 = F0 + NG * FCH
J0 = P0 + NG * PCH
W0 = J0 + KC * JCH
WEND = W0 + 4 * WCH

PADW = 8
UW = T + 2 * PADW

CONST = {}
_at = 0
for _n, _w in (("ident", P), ("ltri", P), ("r32", NE), ("slot", CAP), ("block", NTAB), ("r4", NG), ("steps", 8),
               ("valid", TILES), ("token", 2 * TILES), ("x", NX)):
    CONST[_n] = (_at, _at + _w)
    _at += _w
NCONST = _at


def shape_constants():
    k = np.zeros((P, NCONST), np.float32)

    def put(name, v):
        k[:, CONST[name][0]:CONST[name][1]] = v

    i = np.arange(P)
    put("ident", np.eye(P))
    put("ltri", i[:, None] < i[None, :])
    put("r32", NE - np.arange(NE)[None])
    put("slot", np.arange(CAP)[None])
    put("block", np.arange(NTAB)[None])
    put("r4", NG - np.arange(NG)[None])
    own = np.ones((P, TILES))
    own[:TILES * P - T, TILES - 1] = 0
    put("valid", own)
    tok = np.array(STARTS)[None, :] + i[:, None]
    put("token", np.concatenate([(tok + 1) * own, (tok + 1 + T) * own], 1))
    put("x", np.arange(NX)[None])
    put("steps", CAP * np.arange(1, 9)[None])
    c = np.arange(GD)
    ang = 2 * np.pi * (np.outer(c, c) % GD) / GD
    chan = np.concatenate([np.cos(ang), np.sin(ang)], 1) / np.sqrt(GD)
    n = np.arange(T)
    ang = 2 * np.pi * (np.outer(n, n) % T) / T
    pos = np.zeros((2, TILES, P, T))
    for t, s in enumerate(STARTS):
        pos[0, t] = np.cos(ang[s:s + P]) / np.sqrt(T)
        pos[1, t] = -np.sin(ang[s:s + P]) / np.sqrt(T)
    pos[:, TILES - 1, :TILES * P - T] = 0
    edge = np.zeros((NG, 2 * PADW))
    for g in range(NG):
        w = 2 ** (g + 1)
        cnt = np.clip(n + w // 2 - 1, 0, T - 1) - np.clip(n - w // 2, 0, T - 1) + 1
        edge[g] = (w / cnt)[np.r_[0:PADW, T - PADW:T]]
    return k, chan.astype(np.float32), pos.astype(np.float32), edge.astype(np.float32)


def encoder_kernel(nc, x, meta_tokens, in_ln_g, in_ln_b, w_in, b_gate, w_pool_group, pool_scale, w_branch_pool,
                   w_branch_fourier, w_out, ln1_g, ln1_b, w_router_group, b_router_group, w_router_expert,
                   b_router_expert, w_gate, w_up, w_down, ln2_g, ln2_b, k_small, k_chan, k_pos, k_edge, out):
    h0_dram = nc.dram_tensor("h0_rows", [T, D], F32).ap()
    h1_dram = nc.dram_tensor("h1_rows", [T, D], F32).ap()
    y_dram = nc.dram_tensor("expert_rows", [2 * T, D], F32).ap()

    base = (nc.sbuf_base + 31) // 32 * 32

    def sb(name, shape, dt, at):
        return nc.alloc_sbuf_tensor_at(name, shape, dt, offset=base + at)

    act_hi = sb("act_hi", [P, KC, T], F32R, 0)
    act_lo = sb("act_lo", [P, KC, T], F32R, 33792)
    mix_hi = sb("mix_hi", [P, KC, T], F32R, 67584)
    mix_lo = sb("mix_lo", [P, KC, T], F32R, 101376)
    chan_hi = mix_hi[:, 0:2, :]
    chan_lo = mix_lo[:, 0:2, :]
    freq_hi = mix_hi[:, 2:7, 0:2 * GD]
    freq_lo = mix_lo[:, 2:7, 0:2 * GD]
    raw = sb("raw", [P, RAW, MC], F32, 135168)
    whi = sb("whi", [P, RING, MC], F32R, 151552)
    wlo = sb("wlo", [P, RING, MC], F32R, 159744)
    merged = sb("merged", [P, KC, T], F32, 167936)
    consts = sb("consts", [P, NCONST], F32, 201728)
    small_at = 201728 + (4 * NCONST + 31) // 32 * 32

    def small(name, shape, dt):
        nonlocal small_at
        t = sb(name, shape, dt, small_at)
        small_at += (int(np.prod(shape[1:])) * 4 + 31) // 32 * 32
        return t

    cols = small("cols", [P, 40], F32)
    edge = small("edge", [P, NG, 2 * PADW], F32)
    rbias = small("rbias", [P, NG + NE], F32)
    gidx = small("gidx", [CAP, NTAB], U32)
    sidx = small("sidx", [CAP, NTAB], U32)
    gatew = small("gatew", [CAP, NTAB], F32)
    steer = small("steer", [1, NX + 2], I32)
    assert small_at <= 204992
    stage = sb("stage", [P, 3, UW], F32, 204992)
    rows = sb("rows", [P, TILES, D], F32, 67584)
    resid = sb("resid", [P, 2, TILES, 512], F32, 108544)
    gb = sb("gb", [P, 2, D], F32, 167936)
    colsrc = sb("colsrc", [40, P], F32, 184320)
    stats = sb("stats", [P, TILES, 4, 6], F32, 211520)
    mv = sb("mv", [P, TILES, 2], F32, 212000)
    std = sb("std", [P, TILES], F32, 212064)
    rstd = sb("rstd", [P, TILES], F32, 212096)
    nmr = sb("nmr", [P, TILES], F32, 212128)
    h1T = sb("h1T", [P, 2, KC, P], F32, 0)
    wrout = sb("wrout", [P, KC, NG + NE], F32, 204992)
    logit = sb("logit", [P, TILES, NG + NE], F32, 207296)
    rt = [167936, 100352]

    def rbuf(name, shape, dt=F32, area=0):
        t = sb(name, shape, dt, rt[area])
        rt[area] += (int(np.prod(shape[1:])) * 4 + 31) // 32 * 32
        return t

    gmax = rbuf("gmax", [P, TILES])
    gdif = rbuf("gdif", [P, TILES, NG])
    gexp = rbuf("gexp", [P, TILES, NG])
    gsum = rbuf("gsum", [P, TILES])
    gprob = rbuf("gprob", [P, TILES])
    gone = rbuf("gone", [P, TILES, NG])
    gpick = rbuf("gpick", [P, TILES])
    masked = rbuf("masked", [P, TILES, NE])
    masked2 = rbuf("masked2", [P, TILES, NE])
    emax = rbuf("emax", [P, 2, TILES])
    epick = rbuf("epick", [P, 2, TILES])
    etmp = rbuf("etmp", [P, TILES, NE])
    one = rbuf("one", [P, 2, TILES, NE])
    anyone = rbuf("anyone", [P, TILES, NE])
    ones = rbuf("ones", [P, P])
    ediff = rbuf("ediff", [P, TILES])
    eexp = rbuf("eexp", [P, TILES])
    esum = rbuf("esum", [P, TILES])
    gate = rbuf("gate", [P, 2, TILES])
    posn = rbuf("posn", [P, TILES, NE])
    earlier = rbuf("earlier", [P, TILES + 1, NE])
    over = rbuf("over", [P, 8, NE])
    nover = rbuf("nover", [P, NE])
    cum = rbuf("cum", [P, NE])
    excl = rbuf("excl", [P, NE])
    prod = rbuf("prod", [P, 2, TILES, NE])
    apos = rbuf("apos", [P, 2, TILES])
    aexp = rbuf("aexp", [P, 2, TILES])
    aexc = rbuf("aexc", [P, 2, TILES])
    step8 = rbuf("step8", [P, 8, 2 * TILES])
    turn = rbuf("turn", [P, 2, TILES])
    turn1 = rbuf("turn1", [P, 2, TILES])
    aslot = rbuf("aslot", [P, 2, TILES])
    ablock = rbuf("ablock", [P, 2, TILES])
    slot1 = rbuf("slot1", [P, 2 * TILES, CAP], area=1)
    block1 = rbuf("block1", [P, 2 * TILES, NTAB], area=1)
    block2 = rbuf("block2", [P, 2 * TILES, 2, NTAB])
    table = rbuf("table", [CAP, 2, NTAB])
    none = rbuf("none", [CAP, NTAB])
    sidxf = rbuf("sidxf", [CAP, NTAB])
    second = rbuf("second", [CAP, NTAB])
    gidxf = rbuf("gidxf", [CAP, NTAB])
    below = rbuf("below", [P, NX, NE], area=1)
    steerf = rbuf("steerf", [P, NX + 2])
    assert rt[0] <= 184320 and rt[1] <= 108544, rt
    ehi = sb("ehi", [P, ERING, EC], F32R, 0)
    elo = sb("elo", [P, ERING, EC], F32R, 32768)
    hrow = sb("hrow", [P, F], F32, 65536)
    SLOTS = [184320, 192512, 135168, 143360, 151552, 159744, 108544, 116736, 124928, 67584, 75776, 83968]
    eraw = [sb(f"eraw{i}", [P, EC], F32, at) for i, at in enumerate(SLOTS)]
    xrow = sb("xrow", [P, D], F32, 92160)
    yrow = sb("yrow", [CAP, D], F32, 100352)
    xT_hi = sb("xT_hi", [P, KC, P], F32R, 167936)
    xT_lo = sb("xT_lo", [P, KC, P], F32R, 176128)
    hT_hi = sb("hT_hi", [P, 4, P], F32R, 204992)
    hT_lo = sb("hT_lo", [P, 4, P], F32R, 207040)
    gcol = sb("gcol", [CAP, 1], F32, 211200)
    srow = sb("srow", [P, F], F32, 209088)
    gcur = sb("gcur", [CAP, 1], U32, 211136)
    scur = sb("scur", [CAP, 1], U32, 211168)
    fin_rows = [P, P, P, P, T - 4 * P]
    fin_order = [4, 0, 1, 2, 3]
    fin_h = [eraw[t][0:fin_rows[t], :] for t in range(TILES)]
    fin_g, fin_b = eraw[5], eraw[6]
    fin_ring = sb("fin_ring", [P, 8, D], F32, 0)
    fin_y = [[fin_ring[:, 2 * t + a, :] for a in range(2)] for t in range(4)]
    fin_y.append([eraw[7][0:fin_rows[4], :], eraw[8][0:fin_rows[4], :]])
    fin_small = sb("fin_small", [P, 6, TILES], F32, 212128)
    fin_eps = sb("fin_eps", [P, 1], F32, 212256)
    ident = consts[:, 0:P]

    def const(name, parts=P):
        a, b = CONST[name]
        return consts[0:parts, a:b]

    ctx = ExitStack()
    with ctx:
        ps = ctx.enter_context(nc.psum_tensor("ps", [P, 8, 512], F32))

        def sem(name):
            return ctx.enter_context(nc.semaphore(name))

        s_small = sem("s_small")
        s_wr = sem("s_wr")
        s_row = [sem(f"s_row{t}") for t in range(TILES)]
        s_gb0 = [sem(f"s_gb0_{i}") for i in range(2)]
        s_gb1 = sem("s_gb1")
        s_gb2 = sem("s_gb2")
        s_raw = [sem(f"s_raw{i}") for i in range(RAW)]
        s_res = [sem(f"s_res{i}") for i in range(2)]
        s_eraw = [sem(f"s_eraw{i}") for i in range(ECH)]
        s_h0 = sem("s_h0")
        s_h1 = sem("s_h1")
        s_out = sem("s_out")
        hi_done = sem("hi_done")
        lo_done = sem("lo_done")
        used = sem("used")
        ln_var = [sem(f"ln_var{i}") for i in range(2)]
        ln_mv = [sem(f"ln_mv{i}") for i in range(2)]
        ln_std = [sem(f"ln_std{i}") for i in range(2)]
        ln_norm = [sem(f"ln_norm{i}") for i in range(2)]
        ln_g = [sem(f"ln_g{i}") for i in range(2)]
        ln_done = [[sem(f"ln_done{i}_{t}") for t in range(TILES)] for i in range(2)]
        tr_ready = sem("tr_ready")
        tr_hi = sem("tr_hi")
        tr_lo = sem("tr_lo")
        cols_ready = sem("cols_ready")
        cols_done = sem("cols_done")
        fu_hi = sem("fu_hi")
        fu_lo = sem("fu_lo")
        fv_ready = sem("fv_ready")
        fv_hi = sem("fv_hi")
        fv_lo = sem("fv_lo")
        fo_ready = sem("fo_ready")
        fo_hi = sem("fo_hi")
        fo_lo = sem("fo_lo")
        pad_zero = sem("pad_zero")
        pu_copied = sem("pu_copied")
        pw_step = sem("pw_step")
        pw_done = sem("pw_done")
        pd_hi = sem("pd_hi")
        pd_lo = sem("pd_lo")
        pm_hi = sem("pm_hi")
        pm_lo = sem("pm_lo")
        gate_done = sem("gate_done")
        mul_done = sem("mul_done")
        merge_done = sem("merge_done")
        mt_hi = sem("mt_hi")
        mt_lo = sem("mt_lo")
        acc_ready = sem("acc_ready")
        acc_free = sem("acc_free")
        bn_done = sem("bn_done")
        s_ln0 = sem("s_ln0")
        s_agg = [sem(f"s_agg{i}") for i in range(2)]
        rt_ready = sem("rt_ready")
        rt_done = sem("rt_done")
        lg_ready = sem("lg_ready")
        lg_done = sem("lg_done")
        r_step = sem("r_step")
        r_gexp = sem("r_gexp")
        r_eexp = sem("r_eexp")
        r_any = sem("r_any")
        r_pos = sem("r_pos")
        r_hot = sem("r_hot")
        r_table = sem("r_table")
        r_done = sem("r_done")
        pad_cols = sem("pad_cols")
        ehi_done = sem("ehi_done")
        elo_done = sem("elo_done")
        eused = sem("eused")
        idx_g = sem("idx_g")
        idx_s = sem("idx_s")
        gathered = sem("gathered")
        scattered = sem("scattered")
        xt_ready = sem("xt_ready")
        xt_hi = sem("xt_hi")
        xt_lo = sem("xt_lo")
        silu_done = sem("silu_done")
        h_done = sem("h_done")
        ht_ready = sem("ht_ready")
        ht_hi = sem("ht_hi")
        ht_lo = sem("ht_lo")
        y_ready = sem("y_ready")
        y_done = sem("y_done")
        gcol_done = sem("gcol_done")
        moe_end = sem("moe_end")
        s_fh = [sem(f"s_fh{t}") for t in range(TILES)]
        s_fy = [sem(f"s_fy{t}") for t in range(TILES)]
        f_eps = sem("f_eps")
        f_sum = sem("f_sum")
        f_mean = sem("f_mean")
        f_sq = sem("f_sq")
        f_std = sem("f_std")
        f_mv = sem("f_mv")
        f_norm = sem("f_norm")
        f_g = sem("f_g")
        f_done = [sem(f"f_done{t}") for t in range(TILES)]

        block = ctx.enter_context(nc.Block())

        def win_half(col, half):
            return w_in[0, 1024 * half:1024 * (half + 1), col].rearrange("(k p) n -> p k n", p=P)

        def past(eng, sem, value):
            if not isinstance(value, int) or value > 0:
                eng.wait_ge(sem, value)

        def at(start, size=P):
            return bass.ds(start, size)

        def raw3(i, n, w):
            return raw[:, i, 0:n * w].rearrange("p (k n) -> p k n", n=w)

        def add_b(eng, i, t):
            eng.wait_ge(ln_g[i], t + 1)
            eng.tensor_tensor(rows[:, t, :], rows[:, t, :], gb[:, 1, :], ALU.add).then_inc(ln_done[i][t], 1)

        def fin_add_b(eng, j, t):
            eng.wait_ge(f_g, j + 1)
            eng.tensor_tensor(fin_h[t], fin_h[t], fin_b[0:fin_rows[t], :], ALU.add).then_inc(f_done[t], 1)

        def u_chunk(g):
            return P0 + (PCH * g - 2 if g else 0)

        def g_chunk(g):
            return u_chunk(g + 1) + 4 if g < NG - 1 else J0

        GATE0 = J0 - 2

        def used_cols(bank):
            return bank.rearrange("p (c n) -> p c n", n=P)[:, :, 0:CAP]

        def own_rows(t):
            lo = t * P
            return lo, min(T, lo + P), lo - STARTS[t]

        TR_BANK = [0, 4, 0, 4, 4]

        def own_columns(t):
            lo, hi, _ = own_rows(t)
            return slice(lo, hi)

        def own_part(t, q):
            _, _, r = own_rows(t)
            return ps[:, q + TR_BANK[t], :].rearrange("p (c n) -> p c n", n=P)[:, :, r:]

        def gate_up(e, i):
            w = w_gate if i < 4 else w_up
            return w[0, bass.ds(e, 1), 512 * (i % 4):512 * (i % 4 + 1), :].rearrange("a (k p) n -> p (a k) n", p=P)

        def down(e, i):
            return w_down[0, bass.ds(e, 1), P * i:P * (i + 1), :].rearrange("a p n -> p (a n)")

        def number(b, i):
            return i if isinstance(b, int) and b == 0 else ECH * b + (i - 4)

        def place(b, i):
            if isinstance(b, int) and b == 0:
                return i, 1
            return (i + 8) % ECH, b + (i + 8) // ECH

        def eraw_gate(slot):
            return eraw[slot][:, :].rearrange("p (k n) -> p k n", n=F)

        @block.sync
        def _(sp):
            x_rows = x.rearrange("b s d -> (b s) d")
            sp.dma_start(rows[0:META, 0, :], meta_tokens).then_inc(s_row[0], 16)
            sp.dma_start(rows[META:P, 0, :], x_rows[0:P - META, :]).then_inc(s_row[0], 16)
            for t in range(1, TILES):
                sp.dma_start(rows[:, t, :], x_rows[STARTS[t] - META:STARTS[t] - META + P, :]).then_inc(s_row[t], 16)
                if t == 1:
                    for i, v in enumerate((in_ln_g, in_ln_b)):
                        sp.dma_start(gb[:, i, :], v.broadcast_to([P, D])).then_inc(s_gb0[i], 16)
            sp.wait_ge(s_small, 16 * 6)

            def chunk(n, slot, dst, src):
                if isinstance(n, int) and n < RAW:
                    pass
                else:
                    sp.wait_ge(lo_done, n - RAW + 1)
                sp.dma_start(dst, src).then_inc(s_raw[slot], 16)

            def store_rows(dst, i, done):
                for t in range(TILES):
                    lo, hi, r = own_rows(t)
                    sp.wait_ge(ln_done[i][t], 1)
                    sp.dma_start(dst[lo:hi, :], rows[r:r + hi - lo, t, :]).then_inc(done, 16)

            def fourier_group(g, first):
                for i in range(4):
                    n = F0 + i if first else F0 + FCH * g + i
                    chunk(n, i % RAW, raw3(i % RAW, 8, P), win_half(at(W2 + GD * g + P * (i // 2)), i % 2))
                if first:
                    store_rows(h0_dram, 0, s_h0)
                for i in range(4, 6):
                    chunk(F0 + FCH * g + i, i % RAW, raw[:, i % RAW, 0:512], k_chan[P * (i - 4):P * (i - 3), :])
                for i in range(6, FCH):
                    t, cs = divmod(i - 6, 2)
                    chunk(F0 + FCH * g + i, i % RAW, raw[:, i % RAW, 0:T], k_pos[cs, t])

            fourier_group(0, True)
            with sp.Fori(1, NG) as g:
                fourier_group(g, False)
            def u_chunks(g):
                for i in range(4):
                    n = u_chunk(g) + i
                    chunk(n, n % RAW, raw3(n % RAW, 8, P), win_half(at(GD * g + P * (i // 2)), i % 2))

            def g_chunks(g):
                for k in range(2):
                    n = g_chunk(g) + k
                    chunk(n, n % RAW, raw[:, n % RAW, 0:GD], w_pool_group[0, g, P * k:P * (k + 1), :])

            u_chunks(0)
            for g in range(1, NG):
                u_chunks(g)
                g_chunks(g - 1)

            def column_chunks(jj, b):
                if not isinstance(jj, int):
                    sp.to_reg(4 * (P * (2 * jj + b)))
                for i in range(JCH):
                    j = 2 * jj + b
                    n = J0 + JCH * b + i + 2 * JCH * jj
                    slot = (J0 + JCH * b + i) % RAW
                    if isinstance(j, int) and j == 0 and i < 2:
                        n = GATE0 + i
                        slot = n % RAW
                    if i < 4:
                        src = win_half(at(2 * W2 + D * (i // 2) + P * j), i % 2)
                    else:
                        w = (w_branch_pool, w_branch_fourier)[i - 4]
                        src = w[0, :, at(P * j)].rearrange("(k p) n -> p k n", p=P)
                    chunk(n, slot, raw3(slot, 8, P), src)
                    if isinstance(j, int) and j == 0 and i == 1:
                        g_chunks(NG - 1)

            column_chunks(0, 0)
            column_chunks(0, 1)
            with sp.Fori(1, KC // 2) as jj:
                for b in range(2):
                    column_chunks(jj, b)
            with sp.Fori(0, 4) as n:
                for i in range(WCH):
                    slot = (W0 + i) % RAW
                    chunk(W0 + i + WCH * n, slot, raw3(slot, 2, 512),
                          w_out[0, 2 * P * i:2 * P * (i + 1), at(512 * n, 512)].rearrange("(k p) n -> p k n", p=P))

            def expert_chunk(b, i, dst, src):
                slot, _ = place(b, i)
                past(sp, elo_done, number(b, i) - ECH + 1)
                sp.dma_start(dst(slot), src).then_inc(s_eraw[slot], 16)

            def down_chunks(b, e, places):
                for i in places:
                    expert_chunk(b, i, lambda slot: eraw[slot][:, :], down(e, i % 4))

            def round_chunks(b, e, e_down):
                for i in range(8):
                    expert_chunk(b, i, eraw_gate, gate_up(e, i))
                down_chunks(b, e_down, range(8, 12))

            for n in range(ECH):
                if n == 0:
                    sp.wait_ge(mt_lo, KC // 2)
                if n == 2:
                    sp.wait_ge(used, WEND)
                if n == 6:
                    sp.wait_ge(acc_free, 5 + 20)
                if n == 9:
                    store_rows(h1_dram, 1, s_h1)
                if 9 <= n:
                    sp.wait_ge(rt_ready, 4 * (n - 8))
                    sp.wait_ge(s_h1, 16 * TILES)
                b, i = divmod(n, 8)
                expert_chunk(b, i, eraw_gate, gate_up(b, i))
            for i in range(4, 8):
                expert_chunk(1, i, eraw_gate, gate_up(1, i))
            down_chunks(1, 0, range(8, 12))
            with sp.Fori(2, NE) as b:
                round_chunks(b, b, b - 1)
            sp.wait_ge(r_done, 1)
            n_over = sp.value_load(steer[0:1, NX + 1:NX + 2], min_val=0, max_val=NX)
            with sp.If(n_over > 0):
                with sp.Fori(0, NX) as x_block:
                    with sp.If(x_block < n_over):
                        e_down = sp.value_load(steer[0:1, at(x_block, 1)], min_val=0, max_val=NE - 1)
                        e = sp.value_load(steer[0:1, at(x_block + 1, 1)], min_val=0, max_val=NE - 1)
                        round_chunks(x_block + NE, e, e_down)
                    sp.nop()
            sp.nop()
            e_last = sp.value_load(steer[0:1, at(n_over, 1)], min_val=0, max_val=NE - 1)
            down_chunks(n_over + NE, e_last, range(4))

            sp.wait_ge(elo_done, number(n_over + NE, 0))
            sp.dma_start(fin_g[:, :], ln2_g.broadcast_to([P, D])).then_inc(s_gb2, 16)
            sp.dma_start(fin_b[:, :], ln2_b.broadcast_to([P, D])).then_inc(s_gb2, 16)
            for t in fin_order:
                sp.dma_start(fin_h[t], h1_dram[P * t:P * t + fin_rows[t], :]).then_inc(s_fh[t], 16)
            sp.wait_ge(moe_end, 4)
            for t in fin_order:
                for a in range(2):
                    s = a * T + P * t
                    sp.dma_start(fin_y[t][a], y_dram[s:s + fin_rows[t], :]).then_inc(s_fy[t], 16)
            out_rows = out.rearrange("b s d -> (b s) d")
            for t in fin_order:
                skip = META if t == 0 else 0
                sp.wait_ge(f_done[t], 1)
                sp.dma_start(out_rows[P * t + skip - META:P * t + fin_rows[t] - META, :], fin_h[t][skip:, :]).then_inc(s_out, 16)
            sp.wait_ge(s_out, 16 * TILES)

        @block.gpsimd
        def _(pool):
            pool.dma_start(consts[:, :], k_small).then_inc(s_small, 16)
            pool.dma_start(colsrc[0:32, :], b_gate.rearrange("a (j p) -> (a j) p", p=P)).then_inc(s_small, 16)
            pool.dma_start(colsrc[32:40, :], pool_scale.rearrange("a (j p) -> (a j) p", p=P)).then_inc(s_small, 16)
            pool.dma_start(edge[:, :, :].rearrange("p g w -> p (g w)"), k_edge.broadcast_to([P, NG * 2 * PADW])).then_inc(s_small, 16)
            pool.dma_start(rbias[:, 0:NG], b_router_group.broadcast_to([P, NG])).then_inc(s_small, 16)
            pool.dma_start(rbias[:, NG:NG + NE], b_router_expert.broadcast_to([P, NE])).then_inc(s_small, 16)
            pool.wait_ge(s_gb0[1], 16)
            for t in range(TILES - 1):
                add_b(pool, 0, t)

            pool.memset(stage[:, 0, :], 0.0).then_inc(pad_zero, 1)
            pool.wait_ge(s_small, 16 * 6)
            steps = 0

            def pstep(ins):
                nonlocal steps
                steps += 1
                ins.then_inc(pw_step, 1)
                pool.wait_ge(pw_step, steps)

            for n in range(2 * NG):
                g = n // 2
                w = 2 ** (g + 1)
                pool.wait_ge(pu_copied, n + 1)
                src, width, shift = 0, UW, 1
                for s in range(g + 1):
                    dst = 2 - s % 2
                    width -= shift
                    pstep(pool.tensor_tensor(stage[:, dst, 0:width], stage[:, src, 0:width],
                                             stage[:, src, shift:shift + width], ALU.add))
                    src, shift = dst, shift * 2
                a = PADW - w // 2
                res = stage[:, src, a:a + T]
                for k, c in ((0, 0), (1, T - PADW)):
                    pstep(pool.tensor_tensor(res[:, c:c + PADW], res[:, c:c + PADW],
                                             edge[:, g, PADW * k:PADW * (k + 1)], ALU.mult))
                pstep(pool.tensor_scalar(res, res, 1.0 / w, None, ALU.mult))
                dst = 3 - src
                assert dst == 1 + g % 2, (g, src, dst)
                pool.tensor_tensor(stage[:, dst, 0:T], res, stage[:, 0, PADW:PADW + T], ALU.subtract).then_inc(pw_done, 1)

            def residual(n):
                for t in range(TILES):
                    s = STARTS[t]
                    pool.dma_start(resid[:, n % 2, t, :], h0_dram[s:s + P, 512 * n:512 * (n + 1)]).then_inc(s_res[n % 2], 16)

            pool.wait_ge(used, W0)
            pool.wait_ge(s_h0, 16 * TILES)
            residual(0)
            residual(1)
            pool.wait_ge(mt_lo, KC // 2)
            for i, v in enumerate((ln1_g, ln1_b)):
                pool.dma_start(gb[:, i, :], v.broadcast_to([P, D])).then_inc(s_gb1, 16)
            pool.wait_ge(merge_done, KC)
            pool.dma_start(wrout[:, :, 0:NG], w_router_group[0].rearrange("(k p) n -> p k n", p=P)).then_inc(s_wr, 16)
            pool.dma_start(wrout[:, :, NG:NG + NE], w_router_expert[0].rearrange("(k p) n -> p k n", p=P)).then_inc(s_wr, 16)
            for n in (2, 3):
                pool.wait_ge(acc_free, 5 + 5 * (n - 1))
                residual(n)
            pool.wait_ge(s_gb1, 32)
            for t in (1, 3):
                add_b(pool, 1, t)
            pool.wait_ge(s_h1, 16 * TILES)
            pool.wait_ge(rt_ready, 4 * TILES)
            pool.memset(xrow[:, :], 0.0).then_inc(pad_cols, 1)
            for i in range(ERING):
                pool.wait_ge(ehi_done, i + 1)
                pool.tensor_tensor(elo[:, i, :], eraw[i][:, :], ehi[:, i, :], ALU.subtract).then_inc(elo_done, 1)
            pool.wait_ge(pad_cols, 1)
            pool.wait_ge(r_done, 1)

            origin_reg = pool.alloc_register("origin")
            pool.reg_mov(origin_reg, 0)

            def gather(b):
                origin = pool.snap(origin_reg, min_val=0, max_val=1)
                pool.tensor_copy(gcur[:, :], gidx[:, at(b, 1)]).then_inc(idx_g, 1)
                pool.wait_ge(idx_g, b + 1)
                pool.indirect_dma_start(xrow[0:CAP, :], None, h1_dram, bass.IndirectOffsetOnAxis(gcur[:, :], 0),
                                        bounds_check=origin + (T - 1), oob_is_err=False).then_inc(gathered, 16)

            def next_gather(b):
                pool.wait_ge(xt_ready, 4 * b + 4)
                pool.wait_ge(gathered, 16 * b + 16)
                gather(b + 1)

            def scatter(b):
                past(pool, scattered, 16 * b)
                origin = pool.snap(origin_reg, min_val=0, max_val=1)
                pool.tensor_copy(scur[:, :], sidx[:, at(b, 1)]).then_inc(idx_s, 1)
                pool.wait_ge(idx_s, b + 1)
                pool.wait_ge(y_done, 4 * b + 4)
                pool.indirect_dma_start(y_dram, bass.IndirectOffsetOnAxis(scur[:, :], 0), yrow[:, :], None,
                                        bounds_check=origin + (2 * T - 1), oob_is_err=False).then_inc(scattered, 16)

            def moe_round(b):
                next_gather(b)
                if not (isinstance(b, int) and b < 2):
                    scatter(b - 2)

            gather(0)
            for pads in (xT_hi, xT_lo, hT_hi, hT_lo):
                pool.memset(pads[:, :, CAP:P].bitcast(F32), 0.0).then_inc(pad_cols, 1)
            for b in range(3):
                moe_round(b)
            with pool.Fori(3, NE) as b:
                moe_round(b)
            n_over = pool.value_load(steer[0:1, NX + 1:NX + 2], min_val=0, max_val=NX)
            with pool.If(n_over > 0):
                with pool.Fori(0, NX) as x_block:
                    with pool.If(x_block < n_over):
                        moe_round(x_block + NE)
                    pool.nop()
            pool.nop()
            scatter(n_over + (NE - 2))
            scatter(n_over + (NE - 1))
            pool.wait_ge(gathered, 16 * (n_over + (NE + 1)))
            pool.wait_ge(scattered, 16 * n_over + 16 * NE)
            pool.sem_inc(moe_end, 1)

            pool.wait_ge(s_gb2, 32)
            for j, t in enumerate(fin_order[:-1]):
                fin_add_b(pool, j, t)

        @block.scalar
        def _(act):
            def copy(dst, src, done, **kw):
                act.activation(dst, src, ACT.Copy, **kw).then_inc(done, 1)

            def ln_root(i, t):
                act.wait_ge(ln_var[i], t + 1)
                act.activation(std[:, t:t + 1], std[:, t:t + 1], ACT.Sqrt).then_inc(ln_std[i], 1)

            def ln_normal(i, t):
                act.wait_ge(ln_mv[i], 2 * t + 2)
                act.activation(rows[:, t, :], rows[:, t, :], ACT.Identity, bias=nmr[:, t:t + 1],
                               scale=rstd[:, t:t + 1]).then_inc(ln_norm[i], 1)

            def layernorm(i):
                for t in range(TILES):
                    ln_root(i, t)
                    ln_normal(i, t)

            def h0_evac(t):
                for q in range(4):
                    act.wait_ge(tr_ready, 4 * t + q + 1)
                    copy(act_hi[:, 4 * q:4 * q + 4, own_columns(t)], own_part(t, q), tr_hi)

            def hi(base, i, loops, per, width=MC):
                n = base + i
                slot = n % RAW
                act.wait_ge(s_raw[slot], 16 * (n // RAW + 1) + (16 * per // RAW) * loops)
                if not (isinstance(loops, int) and n < RING):
                    act.wait_ge(used, n - RING + 1 + per * loops)
                copy(whi[:, n % RING, 0:width], raw[:, slot, 0:width], hi_done)

            for t in range(TILES):
                ln_root(0, t)
                ln_normal(0, t)
                if t == 2:
                    act.wait_ge(cols_ready, 1)
                    copy(cols[:, :], ps[:, 7, 0:40], cols_done)
                if t >= 3:
                    h0_evac(t - 3)
            hi(F0, 0, 0, FCH)
            h0_evac(2)
            hi(F0, 1, 0, FCH)
            h0_evac(3)
            h0_evac(4)
            act.wait_ge(s_h0, 16 * TILES)

            def fourier_out(g):
                for m in range(2):
                    if m == 0:
                        act.wait_ge(fo_ready, g + 1)
                    else:
                        act.wait_ge(used, F0 + FCH + FCH * g)
                    copy(mix_hi[:, at(8 + 2 * g + m, 1), :].rearrange("p a (h n) -> p (a h) n", h=2),
                         ps[:, 2 + 2 * m:4 + 2 * m, 0:HALF], fo_hi)

            def fourier_group(g):
                def u_evac(m):
                    act.wait_ge(used, F0 + 2 * m + 2 + FCH * g)
                    copy(chan_hi[:, m, :].rearrange("p (h n) -> p h n", h=2), ps[:, 2 * m:2 * m + 2, 0:HALF], fu_hi)

                if not isinstance(g, int):
                    hi(F0, 0, g, FCH)
                    fourier_out(g - 1)
                    hi(F0, 1, g, FCH)
                for i in range(2, 4):
                    hi(F0, i, g, FCH)
                u_evac(0)
                hi(F0, 4, g, FCH, 512)
                hi(F0, 5, g, FCH, 512)
                u_evac(1)
                hi(F0, 6, g, FCH, T)
                for t in range(TILES):
                    if t < TILES - 1:
                        act.wait_ge(fv_ready, 4 * g + t + 1)
                    else:
                        act.wait_ge(used, F0 + 6 + FCH * g)
                    copy(freq_hi[:, t, :], ps[:, (4 + t) % 8, :], fv_hi)
                for i in range(7, FCH):
                    hi(F0, i, g, FCH, T)

            fourier_group(0)
            with act.Fori(1, NG) as g:
                fourier_group(g)

            def u_evac(n):
                act.wait_ge(used, u_chunk(n // 2) + 2 * (n % 2) + 2)
                if n:
                    act.wait_ge(pd_lo, n)
                m = n % 2
                copy(stage[:, 0, PADW:PADW + T].rearrange("p (h n) -> p h n", h=2),
                     ps[:, 2 * m:2 * m + 2, 0:HALF], pu_copied)

            def window_hi(n):
                act.wait_ge(pw_done, n + 1)
                copy(mix_hi[:, n, :], stage[:, 1 + (n // 2) % 2, 0:T], pd_hi)

            def pool_out(g):
                act.wait_ge(used, g_chunk(g) + 2)
                act.wait_ge(cols_done, 1)
                for m in range(2):
                    n = 2 * g + m
                    act.activation(mix_hi[:, n, :].rearrange("p (h n) -> p h n", h=2), ps[:, 4 + 2 * m:6 + 2 * m, 0:HALF],
                                   ACT.Copy, scale=cols[:, 32 + n:33 + n]).then_inc(pm_hi, 1)

            act.wait_ge(pad_zero, 1)
            for g in range(NG):
                u, gc = u_chunk(g), g_chunk(g - 1)
                hi(u, 0, 0, 0)
                if g == 0:
                    fourier_out(NG - 1)
                if g >= 2:
                    pool_out(g - 2)
                hi(u, 1, 0, 0)
                hi(u, 2, 0, 0)
                if g >= 1:
                    window_hi(2 * g - 1)
                hi(u, 3, 0, 0)
                u_evac(2 * g)
                if g >= 1:
                    hi(gc, 0, 0, 0, GD)
                window_hi(2 * g)
                if g >= 1:
                    hi(gc, 1, 0, 0, GD)
                u_evac(2 * g + 1)
            hi(GATE0, 0, 0, 0)
            pool_out(NG - 2)
            hi(GATE0, 1, 0, 0)
            hi(J0, 0, 0, 0, GD)
            window_hi(2 * NG - 1)
            hi(J0, 1, 0, 0, GD)

            def gate_columns(jj):
                for b in range(2):
                    first = isinstance(jj, int) and b == 0
                    for i in range(2 if first else 0, JCH):
                        hi(J0 + JCH * b, i, jj, 2 * JCH)
                        if first and i == 2:
                            pool_out(NG - 1)
                        if i in (3, 5):
                            a = (i - 3) // 2
                            act.wait_ge(used, J0 + JCH * b + 2 * a + 2 + 2 * JCH * jj)
                            past(act, mul_done, 4 * jj + 2 * b)
                            act.wait_ge(cols_done, 1)
                            act.activation(stage[:, a, 0:T].rearrange("p (h n) -> p h n", h=2),
                                           ps[:, 2 * a:2 * a + 2, 0:HALF], ACT.Sigmoid,
                                           bias=cols[:, at(16 * a + 2 * jj + b, 1)]).then_inc(gate_done, 1)

            gate_columns(0)
            with act.Fori(1, KC // 2) as jj:
                gate_columns(jj)

            def merged_hi(q):
                act.wait_ge(merge_done, 2 * q + 2)
                copy(act_hi[:, 2 * q:2 * q + 2, :], merged[:, 2 * q:2 * q + 2, :], mt_hi)

            act.wait_ge(used, J0 + JCH * (KC - 1) + 4)
            for q in range(4):
                merged_hi(q)
            hi(W0, 0, 0, 0)
            for q in range(4, 7):
                merged_hi(q)
            hi(W0, 1, 0, 0)
            merged_hi(7)
            for i in range(2, WCH):
                hi(W0, i, 0, 0)
            with act.Fori(1, 4) as n:
                for i in range(WCH):
                    hi(W0, i, n, WCH)

            layernorm(1)
            act.wait_ge(used, WEND)
            for t in range(TILES):
                for q in range(4):
                    act.wait_ge(rt_ready, 4 * t + q + 1)
                    if t >= 2 and q == 0:
                        act.wait_ge(lg_ready, t - 1)
                    copy(h1T[:, t % 2, 4 * q:4 * q + 4, :], ps[:, q, :].rearrange("p (c n) -> p c n", n=P), rt_done)
            act.wait_ge(r_gexp, 1)
            act.activation(gexp[:, :, :], gdif[:, :, :], ACT.Exp).then_inc(r_gexp, 1)
            def first_ehi(i):
                act.wait_ge(s_eraw[i], 16)
                act.wait_ge(eused, i + 1)
                copy(ehi[:, i, :], eraw[i][:, :], ehi_done)

            for i in range(3):
                first_ehi(i)
            act.wait_ge(r_eexp, 1)
            act.activation(eexp[:, :], ediff[:, :], ACT.Exp).then_inc(r_eexp, 1)
            first_ehi(3)
            act.wait_ge(r_done, 1)
            act.wait_ge(pad_cols, 5)

            def ehi_chunk(b, i):
                n = number(b, i)
                slot, landed = place(b, i)
                act.wait_ge(s_eraw[slot], 16 * landed)
                act.wait_ge(eused, n + 1)
                copy(ehi[:, i % ERING, :], eraw[slot][:, :], ehi_done)

            def xt_evac(b, q):
                act.wait_ge(xt_ready, 4 * b + q + 1)
                copy(xT_hi[:, 4 * q:4 * q + 4, 0:CAP], used_cols(ps[:, 6 + q % 2, :]), xt_hi)

            def ht_evac(b):
                act.wait_ge(ht_ready, b + 1)
                copy(hT_hi[:, :, 0:CAP], used_cols(ps[:, 1, :]), ht_hi)

            def y_evac(b, last):
                past(act, scattered, 16 * b)
                act.wait_ge(gcol_done, b + 1)
                for n in range(4):
                    if n < 3:
                        act.wait_ge(y_ready, 3 * b + n + 1)
                    else:
                        act.wait_ge(eused, last + (1 + ERING))
                    act.activation(yrow[:, 512 * n:512 * (n + 1)], ps[0:CAP, 2 + n, :], ACT.Copy,
                                   scale=gcol[:, :]).then_inc(y_done, 1)

            def moe_round(b):
                if not (isinstance(b, int) and b < 1):
                    for i in range(4):
                        ehi_chunk(b, i)
                if not (isinstance(b, int) and b < 2):
                    y_evac(b - 2, number(b - 1, ECH - 1))
                if not (isinstance(b, int) and b < 1):
                    ht_evac(b - 1)
                for i in range(4, 8):
                    ehi_chunk(b, i)
                act.wait_ge(eused, number(b, 3) + (1 + ERING))
                past(act, h_done, b)
                act.activation(srow[:, :], ps[:, 0, :], ACT.Silu).then_inc(silu_done, 1)
                if not (isinstance(b, int) and b < 1):
                    for i in range(8, 12):
                        ehi_chunk(b, i)
                for q in range(4):
                    xt_evac(b + 1, q)

            for q in range(4):
                xt_evac(0, q)
            for b in range(3):
                moe_round(b)
            with act.Fori(3, NE) as b:
                moe_round(b)
            n_over = act.value_load(steer[0:1, NX + 1:NX + 2], min_val=0, max_val=NX)
            with act.If(n_over > 0):
                with act.Fori(0, NX) as x_block:
                    with act.If(x_block < n_over):
                        moe_round(x_block + NE)
                    act.nop()
            act.nop()
            end = n_over + NE
            ht_evac(end - 1)
            ehi_chunk(end, 0)
            y_evac(end - 2, number(end, -1))
            for i in range(1, 4):
                ehi_chunk(end, i)
            y_evac(end - 1, number(end, 3))
            act.wait_ge(y_done, 4 * n_over + 4 * NE)
            act.wait_ge(xt_hi, 4 * n_over + 4 * (NE + 1))
            act.sem_inc(moe_end, 1)

            act.wait_ge(f_eps, 1)
            for j, t in enumerate(fin_order):
                _, nmean, sq, sd, rs, nm = [fin_small[0:fin_rows[t], k, t:t + 1] for k in range(6)]
                act.wait_ge(f_mean, j + 1)
                act.activation(fin_y[t][0], fin_h[t], ACT.Square, bias=nmean, accum_out=sq).then_inc(f_sq, 1)
                act.wait_ge(f_sq, j + 1)
                act.activation(sd, sq, ACT.Sqrt, bias=fin_eps[0:fin_rows[t], :], scale=1.0 / D).then_inc(f_std, 1)
                act.wait_ge(f_mv, 2 * j + 2)
                act.activation(fin_h[t], fin_h[t], ACT.Identity, bias=nm, scale=rs).then_inc(f_norm, 1)

        @block.vector
        def _(dve):
            def lo_of(dst, src, hi, done):
                dve.tensor_tensor(dst, src, hi, ALU.subtract).then_inc(done, 1)

            def piece_stats(t, n, done):
                dve.bn_stats(stats[:, t, n, :], rows[:, t, 512 * n:512 * (n + 1)]).then_inc(done, 1)

            def ln_variance(i, t):
                dve.bn_aggr(mv[:, t, :], stats[:, t, :, :].rearrange("p a b -> p (a b)")).then_inc(s_agg[i], 1)
                dve.wait_ge(s_agg[i], t + 1)
                dve.tensor_scalar(std[:, t:t + 1], mv[:, t, 1:2], EPS, None, ALU.add).then_inc(ln_var[i], 1)

            def ln_scale(i, t):
                dve.wait_ge(ln_std[i], t + 1)
                dve.reciprocal(rstd[:, t:t + 1], std[:, t:t + 1]).then_inc(ln_mv[i], 1)
                dve.wait_ge(ln_mv[i], 2 * t + 1)
                dve.scalar_tensor_tensor(out=nmr[:, t:t + 1], in0=mv[:, t, 0:1], scalar=-1.0, in1=rstd[:, t:t + 1],
                                         op0=ALU.mult, op1=ALU.mult).then_inc(ln_mv[i], 1)

            def mult_g(i, t):
                dve.wait_ge(ln_norm[i], t + 1)
                dve.tensor_tensor(rows[:, t, :], rows[:, t, :], gb[:, 0, :], ALU.mult).then_inc(ln_g[i], 1)

            def h0_evac(t):
                sl = own_columns(t)
                for q in range(4):
                    dve.wait_ge(tr_hi, 4 * t + q + 1)
                    lo_of(act_lo[:, 4 * q:4 * q + 4, sl], own_part(t, q), act_hi[:, 4 * q:4 * q + 4, sl], tr_lo)

            def lo(base, i, loops, per, width=MC):
                n = base + i
                dve.wait_ge(hi_done, n + 1 + per * loops)
                lo_of(wlo[:, n % RING, 0:width], raw[:, n % RAW, 0:width], whi[:, n % RING, 0:width], lo_done)

            dve.sem_inc(acc_free, 5)
            for t in range(TILES):
                dve.wait_ge(s_row[t], 32 if t == 0 else 16)
                for n in range(4):
                    piece_stats(t, n, s_ln0)
                dve.wait_ge(s_ln0, 4 * t + 4)
                ln_variance(0, t)
                if t == 1:
                    dve.wait_ge(s_gb0[0], 16)
                if t:
                    mult_g(0, t - 1)
                ln_scale(0, t)
            h0_evac(0)
            mult_g(0, TILES - 1)
            dve.wait_ge(s_gb0[1], 16)
            add_b(dve, 0, TILES - 1)
            h0_evac(1)
            lo(F0, 0, 0, FCH)
            h0_evac(2)
            lo(F0, 1, 0, FCH)
            h0_evac(3)
            h0_evac(4)

            def fourier_out(g):
                for m in range(2):
                    dve.wait_ge(fo_hi, 2 * g + m + 1)
                    v = [z[:, at(8 + 2 * g + m, 1), :].rearrange("p a (h n) -> p (a h) n", h=2) for z in (mix_lo, mix_hi)]
                    lo_of(v[0], ps[:, 2 + 2 * m:4 + 2 * m, 0:HALF], v[1], fo_lo)

            def fourier_group(g):
                def u_evac(m):
                    dve.wait_ge(fu_hi, 2 * g + m + 1)
                    lo_of(chan_lo[:, m, :].rearrange("p (h n) -> p h n", h=2), ps[:, 2 * m:2 * m + 2, 0:HALF],
                          chan_hi[:, m, :].rearrange("p (h n) -> p h n", h=2), fu_lo)

                if not isinstance(g, int):
                    lo(F0, 0, g, FCH)
                    fourier_out(g - 1)
                    lo(F0, 1, g, FCH)
                for i in range(2, 4):
                    lo(F0, i, g, FCH)
                u_evac(0)
                lo(F0, 4, g, FCH, 512)
                lo(F0, 5, g, FCH, 512)
                u_evac(1)
                lo(F0, 6, g, FCH, T)
                for t in range(TILES):
                    dve.wait_ge(fv_hi, TILES * g + t + 1)
                    lo_of(freq_lo[:, t, :], ps[:, (4 + t) % 8, :], freq_hi[:, t, :], fv_lo)
                for i in range(7, FCH):
                    lo(F0, i, g, FCH, T)

            fourier_group(0)
            with dve.Fori(1, NG) as g:
                fourier_group(g)

            def window_lo(n):
                dve.wait_ge(pd_hi, n + 1)
                lo_of(mix_lo[:, n, :], stage[:, 1 + (n // 2) % 2, 0:T], mix_hi[:, n, :], pd_lo)

            def pool_out(g):
                for m in range(2):
                    n = 2 * g + m
                    dve.wait_ge(pm_hi, n + 1)
                    dve.scalar_tensor_tensor(out=mix_lo[:, n, :].rearrange("p (h n) -> p h n", h=2),
                                             in0=ps[:, 4 + 2 * m:6 + 2 * m, 0:HALF], scalar=cols[:, 32 + n:33 + n],
                                             in1=mix_hi[:, n, :].rearrange("p (h n) -> p h n", h=2),
                                             op0=ALU.mult, op1=ALU.subtract).then_inc(pm_lo, 1)

            for g in range(NG):
                u, gc = u_chunk(g), g_chunk(g - 1)
                lo(u, 0, 0, 0)
                if g == 0:
                    fourier_out(NG - 1)
                if g >= 2:
                    pool_out(g - 2)
                lo(u, 1, 0, 0)
                lo(u, 2, 0, 0)
                if g >= 1:
                    window_lo(2 * g - 1)
                lo(u, 3, 0, 0)
                if g >= 1:
                    lo(gc, 0, 0, 0, GD)
                window_lo(2 * g)
                if g >= 1:
                    lo(gc, 1, 0, 0, GD)
            lo(GATE0, 0, 0, 0)
            pool_out(NG - 2)
            lo(GATE0, 1, 0, 0)
            lo(J0, 0, 0, 0, GD)
            window_lo(2 * NG - 1)
            lo(J0, 1, 0, 0, GD)

            def gate_half(a, dst, jj, b):
                dve.wait_ge(used, J0 + JCH * b + 5 + a + 2 * JCH * jj)
                dve.wait_ge(gate_done, 4 * jj + 2 * b + a + 1)
                dve.tensor_tensor(dst, halved(stage[:, a, 0:T]), ps[:, 4 + 2 * a:6 + 2 * a, 0:HALF],
                                  ALU.mult).then_inc(mul_done, 1)

            def halved(ap):
                return ap.rearrange("p (h n) -> p h n", h=2)

            def column(jj, b):
                return merged[:, at(2 * jj + b, 1), :].rearrange("p a (h n) -> p (a h) n", h=2)

            def finish_column(jj, b):
                gate_half(1, halved(stage[:, 2, 0:T]), jj, b)
                dve.wait_ge(mul_done, 4 * jj + 2 * b + 2)
                dve.tensor_tensor(column(jj, b), column(jj, b), halved(stage[:, 2, 0:T]), ALU.add).then_inc(merge_done, 1)

            def gate_columns(jj):
                for b in range(2):
                    if isinstance(jj, int) and b == 0:
                        lo(J0, 2, 0, 0)
                        pool_out(NG - 1)
                        rest = range(3, JCH)
                    else:
                        lo(J0 + JCH * b, 0, jj, 2 * JCH)
                        finish_column(jj if b else jj - 1, 1 - b)
                        rest = range(1, JCH)
                    for i in rest:
                        lo(J0 + JCH * b, i, jj, 2 * JCH)
                    past(dve, merge_done, 2 * jj + b)
                    gate_half(0, column(jj, b), jj, b)

            gate_columns(0)
            with dve.Fori(1, KC // 2) as jj:
                gate_columns(jj)

            def merged_lo(q):
                dve.wait_ge(mt_hi, q + 1)
                lo_of(act_lo[:, 2 * q:2 * q + 2, :], merged[:, 2 * q:2 * q + 2, :], act_hi[:, 2 * q:2 * q + 2, :], mt_lo)

            merged_lo(0)
            merged_lo(1)
            lo(W0, 0, 0, 0)
            finish_column(KC // 2 - 1, 1)
            merged_lo(2)
            merged_lo(3)
            lo(W0, 1, 0, 0)
            for q in range(4, 8):
                merged_lo(q)
            for n in range(4):
                for i in range(2 if n == 0 else 1, WCH):
                    lo(W0 + WCH * n, i, 0, 0)
                if n < 3:
                    lo(W0 + WCH * (n + 1), 0, 0, 0)
                dve.wait_ge(s_res[n % 2], 16 * TILES * (n // 2 + 1))
                for t in range(TILES):
                    if t < TILES - 1:
                        dve.wait_ge(acc_ready, 4 * n + t + 1)
                    else:
                        dve.wait_ge(used, W0 + WCH * (n + 1))
                    dve.scalar_tensor_tensor(out=rows[:, t, 512 * n:512 * (n + 1)], in0=resid[:, n % 2, t, :],
                                             scalar=ALPHA, in1=ps[:, t, :], op0=ALU.mult,
                                             op1=ALU.add).then_inc(acc_free, 1)
                    dve.wait_ge(acc_free, 5 + 5 * n + t + 1)
                    piece_stats(t, n, bn_done)
                    if n == 3:
                        dve.wait_ge(bn_done, 4 * TILES - (TILES - 1 - t))
                        ln_variance(1, t)
                        if t >= 1:
                            ln_scale(1, t - 1)
                        if t == 2:
                            dve.wait_ge(s_gb1, 32)
                        if t >= 2:
                            mult_g(1, t - 2)
                        if t == 2:
                            add_b(dve, 1, 0)
            ln_scale(1, TILES - 1)
            add_b(dve, 1, 2)
            mult_g(1, 3)
            mult_g(1, 4)
            add_b(dve, 1, 4)

            dve.wait_ge(used, WEND)
            for t in range(TILES):
                dve.wait_ge(lg_ready, t + 1)
                dve.tensor_tensor(logit[:, t, :], ps[:, 4 + t % 4, 0:NG + NE], rbias[:, :], ALU.add).then_inc(lg_done, 1)
            dve.wait_ge(lg_done, TILES)
            rsteps = 0

            def r(ins):
                nonlocal rsteps
                rsteps += 1
                ins.then_inc(r_step, 1)
                dve.wait_ge(r_step, rsteps)

            def wide(ap, n):
                shape = list(ap.shape)
                return ap.unsqueeze(len(shape)).broadcast_to(shape + [n])

            def over_tiles(ap, n):
                return ap.unsqueeze(1).broadcast_to([ap.shape[0], n, ap.shape[1]])

            gl, el = logit[:, :, 0:NG], logit[:, :, NG:NG + NE]
            r(dve.memset(ones[:, :], 1.0))
            r(dve.tensor_reduce(gmax[:, :], gl, AX, ALU.max))
            dve.tensor_tensor(gdif[:, :, :], gl, wide(gmax[:, :], NG), ALU.subtract).then_inc(r_gexp, 1)
            r(dve.tensor_tensor(gone[:, :, :], gl, wide(gmax[:, :], NG), ALU.is_equal))
            r(dve.tensor_tensor(gone[:, :, :], gone[:, :, :], over_tiles(const("r4"), TILES), ALU.mult))
            r(dve.tensor_reduce(gpick[:, :], gone[:, :, :], AX, ALU.max))
            r(dve.tensor_tensor(gone[:, :, :], gone[:, :, :], wide(gpick[:, :], NG), ALU.is_equal))
            r(dve.tensor_scalar(gone[:, :, :], gone[:, :, :], -1.0, BIG, ALU.add, ALU.mult))
            r(dve.tensor_tensor(masked[:, :, :].rearrange("p t (g e) -> p t g e", e=EG),
                                el.rearrange("p t (g e) -> p t g e", e=EG), wide(gone[:, :, :], EG), ALU.add))
            for a in range(2):
                src = (masked, masked2)[a]
                r(dve.tensor_reduce(emax[:, a, :], src[:, :, :], AX, ALU.max))
                r(dve.tensor_tensor(etmp[:, :, :], src[:, :, :], wide(emax[:, a, :], NE), ALU.is_equal))
                r(dve.tensor_tensor(etmp[:, :, :], etmp[:, :, :], over_tiles(const("r32"), TILES), ALU.mult))
                r(dve.tensor_reduce(epick[:, a, :], etmp[:, :, :], AX, ALU.max))
                r(dve.tensor_tensor(one[:, a, :, :], etmp[:, :, :], wide(epick[:, a, :], NE), ALU.is_equal))
                if a == 0:
                    r(dve.scalar_tensor_tensor(out=masked2[:, :, :], in0=one[:, 0, :, :], scalar=-2 * BIG,
                                               in1=masked[:, :, :], op0=ALU.mult, op1=ALU.add))
                r(dve.tensor_tensor(one[:, a, :, :], one[:, a, :, :], wide(const("valid"), NE), ALU.mult))
            dve.tensor_tensor(ediff[:, :], emax[:, 1, :], emax[:, 0, :], ALU.subtract).then_inc(r_eexp, 1)
            dve.tensor_tensor(anyone[:, :, :], one[:, 0, :, :], one[:, 1, :, :], ALU.add).then_inc(r_any, 1)
            dve.wait_ge(r_gexp, 2)
            r(dve.tensor_reduce(gsum[:, :], gexp[:, :, :], AX, ALU.add))
            dve.wait_ge(r_eexp, 2)
            r(dve.tensor_scalar(esum[:, :], eexp[:, :], 1.0, None, ALU.add))
            r(dve.tensor_tensor(gsum[:, :], gsum[:, :], esum[:, :], ALU.mult))
            r(dve.reciprocal(gprob[:, :], gsum[:, :]))
            r(dve.tensor_tensor(gate[:, 0, :], gprob[:, :], const("valid"), ALU.mult))
            r(dve.tensor_tensor(gate[:, 1, :], gate[:, 0, :], eexp[:, :], ALU.mult))
            dve.wait_ge(r_pos, 1)
            r(dve.tensor_copy(earlier[:, 1, :], ps[:, 6, 0:NE]))
            for t in range(1, TILES):
                r(dve.tensor_tensor(earlier[:, t + 1, :], earlier[:, t, :], ps[:, 6, NE * t:NE * (t + 1)], ALU.add))
            r(dve.tensor_copy(posn[:, 0, :], ps[:, 5, 0:NE]))
            r(dve.tensor_tensor(posn[:, 1:TILES, :], ps[:, 5, NE:TILES * NE].rearrange("p (t e) -> p t e", e=NE),
                                earlier[:, 1:TILES, :], ALU.add))
            count = earlier[:, TILES, :]
            r(dve.tensor_tensor(over[:, :, :], over_tiles(count, 8), wide(const("steps"), NE), ALU.is_gt))
            r(dve.tensor_reduce(nover[:, :], over[:, :, :].rearrange("p k e -> p e k"), AX, ALU.add))
            r(dve.tensor_tensor_scan(cum[:, :], ones[:, 0:NE], nover[:, :], 0.0, ALU.mult, ALU.add))
            r(dve.tensor_tensor(excl[:, :], cum[:, :], nover[:, :], ALU.subtract))

            def flat(b):
                return b[:, :, :].rearrange("p a t -> p (a t)")

            def pick(dst, values):
                for a in range(2):
                    v = values if len(values.shape) == 3 else over_tiles(values, TILES)
                    r(dve.tensor_tensor(prod[:, a, :, :], one[:, a, :, :], v, ALU.mult))
                r(dve.tensor_reduce(dst[:, :, :], prod[:, :, :, :], AX, ALU.add))

            pick(apos, posn[:, :, :])
            r(dve.tensor_scalar(flat(aexp), flat(epick), -1.0, float(NE), ALU.mult, ALU.add))
            pick(aexc, excl[:, :])
            r(dve.tensor_tensor(step8[:, :, :], over_tiles(flat(apos), 8), wide(const("steps"), 2 * TILES), ALU.is_ge))
            r(dve.tensor_reduce(flat(turn), step8[:, :, :].rearrange("p k n -> p n k"), AX, ALU.add))
            r(dve.scalar_tensor_tensor(out=flat(aslot), in0=flat(turn), scalar=-float(CAP), in1=flat(apos),
                                       op0=ALU.mult, op1=ALU.add))
            r(dve.tensor_scalar(flat(turn1), flat(turn), 1.0, None, ALU.min))
            r(dve.scalar_tensor_tensor(out=flat(ablock), in0=flat(aexc), scalar=float(NE - 1), in1=flat(aexp),
                                       op0=ALU.add, op1=ALU.subtract))
            r(dve.tensor_tensor(flat(ablock), flat(ablock), flat(turn1), ALU.mult))
            r(dve.tensor_tensor(flat(ablock), flat(ablock), flat(aexp), ALU.add))
            r(dve.tensor_tensor(flat(ablock), flat(ablock), flat(turn), ALU.add))
            dve.wait_ge(s_h1, 16 * TILES)
            r(dve.tensor_tensor(slot1[:, :, :], over_tiles(const("slot"), 2 * TILES), wide(flat(aslot), CAP), ALU.is_equal))
            r(dve.tensor_tensor(block1[:, :, :], over_tiles(const("block"), 2 * TILES), wide(flat(ablock), NTAB), ALU.is_equal))
            r(dve.tensor_tensor(block2[:, :, 0, :], block1[:, :, :], wide(const("token"), NTAB), ALU.mult))
            dve.tensor_tensor(block2[:, :, 1, :], block1[:, :, :], wide(flat(gate), NTAB), ALU.mult).then_inc(r_hot, 1)
            r(dve.tensor_tensor(below[:, :, :], over_tiles(cum[:, :], NX), wide(const("x"), NE), ALU.is_le))
            r(dve.memset(steerf[:, 0:1], float(NE - 1)))
            r(dve.tensor_reduce(steerf[:, 1:NX + 1], below[:, :, :], AX, ALU.add))
            r(dve.tensor_scalar(steerf[:, 1:NX + 1], steerf[:, 1:NX + 1], float(NE - 1), None, ALU.min))
            r(dve.tensor_copy(steerf[:, NX + 1:NX + 2], cum[:, NE - 1:NE]))
            r(dve.tensor_copy(steer[:, :], steerf[0:1, :]))
            dve.wait_ge(r_table, 1)
            r(dve.tensor_copy(table[:, :, :], ps[0:CAP, 6, 0:2 * NTAB].rearrange("p (a n) -> p a n", a=2)))
            r(dve.tensor_scalar(none[:, :], table[:, 0, :], 0.0, float(EMPTY), ALU.is_equal, ALU.mult))
            r(dve.scalar_tensor_tensor(out=sidxf[:, :], in0=table[:, 0, :], scalar=-1.0, in1=none[:, :],
                                       op0=ALU.add, op1=ALU.add))
            r(dve.tensor_scalar(second[:, :], sidxf[:, :], float(T), -float(T), ALU.is_ge, ALU.mult))
            r(dve.tensor_tensor(gidxf[:, :], sidxf[:, :], second[:, :], ALU.add))
            r(dve.tensor_copy(gidx[:, :], gidxf[:, :]))
            r(dve.tensor_copy(sidx[:, :], sidxf[:, :]))
            r(dve.tensor_copy(gatew[:, :], table[:, 1, :]))
            dve.sem_inc(r_done, 1)
            dve.wait_ge(pad_cols, 5)
            dve.wait_ge(elo_done, ERING)

            def elo_chunk(b, i):
                slot, _ = place(b, i)
                dve.wait_ge(ehi_done, number(b, i) + 1)
                lo_of(elo[:, i % ERING, :], eraw[slot][:, :], ehi[:, i % ERING, :], elo_done)

            def xt_evac(b, q):
                dve.wait_ge(xt_hi, 4 * b + q + 1)
                lo_of(xT_lo[:, 4 * q:4 * q + 4, 0:CAP], used_cols(ps[:, 6 + q % 2, :]),
                      xT_hi[:, 4 * q:4 * q + 4, 0:CAP], xt_lo)

            def ht_evac(b):
                dve.wait_ge(ht_hi, b + 1)
                lo_of(hT_lo[:, :, 0:CAP], used_cols(ps[:, 1, :]), hT_hi[:, :, 0:CAP], ht_lo)

            def gate_weights(b):
                past(dve, y_done, 4 * b)
                dve.tensor_scalar(gcol[:, :], gatew[:, at(b, 1)], 1.0, None, ALU.mult).then_inc(gcol_done, 1)

            def moe_round(b):
                if not (isinstance(b, int) and b < 1):
                    for i in range(4):
                        elo_chunk(b, i)
                if not (isinstance(b, int) and b < 1):
                    ht_evac(b - 1)
                for i in range(4, 8):
                    elo_chunk(b, i)
                if not (isinstance(b, int) and b < 1):
                    for i in range(8, 12):
                        elo_chunk(b, i)
                dve.wait_ge(silu_done, b + 1)
                dve.wait_ge(eused, number(b, 7) + (1 + ERING))
                past(dve, ht_lo, b)
                dve.tensor_tensor(hrow[:, :], srow[:, :], ps[:, 1, :], ALU.mult).then_inc(h_done, 1)
                for q in range(4):
                    xt_evac(b + 1, q)
                if not (isinstance(b, int) and b < 1):
                    gate_weights(b - 1)

            for q in range(4):
                xt_evac(0, q)
            moe_round(0)
            moe_round(1)
            with dve.Fori(2, NE) as b:
                moe_round(b)
            n_over = dve.value_load(steer[0:1, NX + 1:NX + 2], min_val=0, max_val=NX)
            with dve.If(n_over > 0):
                with dve.Fori(0, NX) as x_block:
                    with dve.If(x_block < n_over):
                        moe_round(x_block + NE)
                    dve.nop()
            dve.nop()
            end = n_over + NE
            ht_evac(end - 1)
            for i in range(4):
                elo_chunk(end, i)
            gate_weights(end - 1)
            dve.wait_ge(xt_lo, 4 * n_over + 4 * (NE + 1))
            dve.wait_ge(elo_done, number(end, 3) + 1)
            dve.sem_inc(moe_end, 1)

            def fin_mult_g(j):
                t = fin_order[j]
                dve.wait_ge(f_norm, j + 1)
                dve.tensor_tensor(fin_h[t], fin_h[t], fin_g[0:fin_rows[t], :], ALU.mult).then_inc(f_g, 1)

            dve.memset(fin_eps[:, :], EPS).then_inc(f_eps, 1)
            for j, t in enumerate(fin_order):
                total, nmean, _, sd, rs, nm = [fin_small[0:fin_rows[t], k, t:t + 1] for k in range(6)]
                dve.wait_ge(s_fh[t], 16)
                dve.wait_ge(s_fy[t], 32)
                dve.scalar_tensor_tensor(out=fin_h[t], in0=fin_h[t], scalar=ALPHA, in1=fin_y[t][0],
                                         op0=ALU.mult, op1=ALU.add).then_inc(f_sum, 1)
                dve.wait_ge(f_sum, 2 * j + 1)
                dve.scalar_tensor_tensor(out=fin_h[t], in0=fin_h[t], scalar=1.0, in1=fin_y[t][1],
                                         op0=ALU.mult, op1=ALU.add, accum_out=total).then_inc(f_sum, 1)
                dve.wait_ge(f_sum, 2 * j + 2)
                dve.tensor_scalar(nmean, total, -1.0 / D, None, ALU.mult).then_inc(f_mean, 1)
                if j == 1:
                    dve.wait_ge(s_gb2, 32)
                if j:
                    fin_mult_g(j - 1)
                dve.wait_ge(f_std, j + 1)
                dve.reciprocal(rs, sd).then_inc(f_mv, 1)
                dve.wait_ge(f_mv, 2 * j + 1)
                dve.tensor_tensor(nm, nmean, rs, ALU.mult).then_inc(f_mv, 1)
            fin_mult_g(TILES - 1)
            fin_add_b(dve, TILES - 1, fin_order[-1])

        @block.tensor
        def _(pe):
            def product(outs, l_hi, l_lo, r_hi, r_lo, start, stop):
                last = None
                for k, (l, r) in enumerate(((l_hi, r_hi), (l_hi, r_lo), (l_lo, r_hi))):
                    for o, rr in zip(outs, r, strict=True):
                        last = pe.matmul(o, l, rr, start=start and k == 0, stop=stop and k == 2)
                return last

            def halves(buf, k):
                return [buf[:, k, 0:HALF], buf[:, k, HALF:T]]

            pe.wait_ge(s_small, 16 * 6)
            pe.transpose(ps[:, 7, 0:40], colsrc[:, :], ident[0:40, 0:40]).then_inc(cols_ready, 1)

            def h0_transposes(t):
                pe.wait_ge(ln_done[0][t], 1)
                if t == 1:
                    pe.wait_ge(cols_done, 1)
                for q in range(4):
                    if t >= 2:
                        pe.wait_ge(tr_lo, 4 * (t - 2 if t < 4 else 3) + q + 1)
                    for c in range(4):
                        k = 4 * q + c
                        last = pe.transpose(ps[:, q + TR_BANK[t], P * c:P * (c + 1)], rows[:, t, P * k:P * (k + 1)], ident)
                    last.then_inc(tr_ready, 1)

            for t in range(4):
                h0_transposes(t)

            def project(base, i0, loops, per, bank):
                for half in range(2):
                    n = base + i0 + half
                    pe.wait_ge(lo_done, n + 1 + per * loops)
                    for k in range(8):
                        last = product([ps[:, bank, 0:HALF], ps[:, bank + 1, 0:HALF]],
                                       whi[:, n % RING, P * k:P * (k + 1)], wlo[:, n % RING, P * k:P * (k + 1)],
                                       halves(act_hi, 8 * half + k), halves(act_lo, 8 * half + k),
                                       half == 0 and k == 0, half == 1 and k == 7)
                    last.then_inc(used, 1)
                return last

            def first_project():
                for h in range(2):
                    if h == 1:
                        h0_transposes(4)
                    pe.wait_ge(tr_lo, 12 if h == 0 else 4 * TILES)
                    for half in range(2):
                        n = F0 + half
                        pe.wait_ge(lo_done, n + 1)
                        for k in range(8):
                            last = product([ps[:, h, 0:HALF]],
                                           whi[:, n, P * k:P * (k + 1)], wlo[:, n, P * k:P * (k + 1)],
                                           [halves(act_hi, 8 * half + k)[h]], [halves(act_lo, 8 * half + k)[h]],
                                           half == 0 and k == 0, half == 1 and k == 7)
                        if h == 1:
                            last.then_inc(used, 1)

            def fourier_group(g):
                for m in range(2):
                    if isinstance(g, int) and m == 0:
                        first_project()
                        continue
                    if m == 0:
                        pe.wait_ge(fv_lo, TILES * g)
                    else:
                        past(pe, fo_lo, 2 * g)
                    project(F0, 2 * m, g, FCH, 2 * m)
                for m in range(2):
                    n = F0 + 4 + m
                    pe.wait_ge(lo_done, n + 1 + FCH * g)
                    pe.wait_ge(fu_lo, 2 * g + m + 1)
                    for t, s in enumerate(STARTS):
                        last = product([ps[:, (4 + t) % 8, :]], chan_hi[:, m, s:s + P], chan_lo[:, m, s:s + P],
                                       [whi[:, n % RING, 0:512]], [wlo[:, n % RING, 0:512]], m == 0, m == 1)
                        if m == 1 and t < TILES - 1:
                            last.then_inc(fv_ready, 1)
                    last.then_inc(used, 1)
                for t in range(TILES):
                    pe.wait_ge(fv_lo, TILES * g + max(t + 1, 2))
                    for cs in range(2):
                        n = F0 + 6 + 2 * t + cs
                        pe.wait_ge(lo_done, n + 1 + FCH * g)
                        for m in range(2):
                            c = GD * cs + P * m
                            last = product([ps[:, 2 + 2 * m, 0:HALF], ps[:, 3 + 2 * m, 0:HALF]],
                                           freq_hi[:, t, c:c + P], freq_lo[:, t, c:c + P],
                                           [whi[:, n % RING, 0:HALF], whi[:, n % RING, HALF:T]],
                                           [wlo[:, n % RING, 0:HALF], wlo[:, n % RING, HALF:T]],
                                           t == 0 and cs == 0, t == TILES - 1 and cs == 1)
                            if t == TILES - 1 and cs == 1 and m == 0:
                                last.then_inc(fo_ready, 1)
                        last.then_inc(used, 1)

            fourier_group(0)
            with pe.Fori(1, NG) as g:
                fourier_group(g)

            def pool_project(g):
                for m in range(2):
                    if isinstance(g, int) and g == 0:
                        if m == 1:
                            pe.wait_ge(fo_lo, 2 * NG)
                        project(P0, 2 * m, 0, 0, 2 * m)
                    else:
                        pe.wait_ge(pu_copied, 2 * g - 1 + m)
                        project(P0 - 2, 2 * m, g, PCH, 2 * m)

            def pool_map(g, base, loops):
                past(pe, pm_lo, 2 * g)
                for k in range(2):
                    n = base + k
                    pe.wait_ge(lo_done, n + 1 + PCH * loops)
                    pe.wait_ge(pd_lo, 2 * g + k + 1)
                    hi = [mix_hi[:, at(2 * g + k, 1), h * HALF:(h + 1) * HALF].rearrange("p a n -> p (a n)") for h in range(2)]
                    lo = [mix_lo[:, at(2 * g + k, 1), h * HALF:(h + 1) * HALF].rearrange("p a n -> p (a n)") for h in range(2)]
                    for m in range(2):
                        last = product([ps[:, 4 + 2 * m, 0:HALF], ps[:, 5 + 2 * m, 0:HALF]],
                                       whi[:, n % RING, P * m:P * (m + 1)], wlo[:, n % RING, P * m:P * (m + 1)],
                                       hi, lo, k == 0, k == 1)
                    last.then_inc(used, 1)

            pool_project(0)
            pool_project(1)
            pool_map(0, g_chunk(0), 0)
            with pe.Fori(2, NG) as g:
                pool_project(g)
                pool_map(g - 1, g_chunk(0) - PCH, g)

            def gate_column(j):
                for a in range(2):
                    past(pe, gate_done, 2 * j)
                    if isinstance(j, int) and a == 0:
                        project(GATE0, 0, 0, 0, 0)
                        pool_map(NG - 1, J0, 0)
                    else:
                        project(J0, 2 * a, j, JCH, 2 * a)
                for a in range(2):
                    n = J0 + 4 + a
                    pe.wait_ge(lo_done, n + 1 + JCH * j)
                    past(pe, mul_done, 2 * j)
                    if isinstance(j, int):
                        pe.wait_ge(pm_lo, 2 * NG)
                    for k in range(8):
                        last = product([ps[:, 4 + 2 * a, 0:HALF], ps[:, 5 + 2 * a, 0:HALF]],
                                       whi[:, n % RING, P * k:P * (k + 1)], wlo[:, n % RING, P * k:P * (k + 1)],
                                       halves(mix_hi, 8 * a + k), halves(mix_lo, 8 * a + k), k == 0, k == 7)
                    last.then_inc(used, 1)

            gate_column(0)
            with pe.Fori(1, KC) as j:
                gate_column(j)

            def out_block(n):
                for i in range(WCH):
                    c = W0 + i
                    if isinstance(n, int):
                        pe.wait_ge(mt_lo, i + 1)
                    pe.wait_ge(lo_done, c + 1 + WCH * n)
                    for t, s in enumerate(STARTS):
                        if i == 0:
                            pe.wait_ge(acc_free, 5 * n + t + 1)
                            if isinstance(n, int) and t == 4:
                                pe.wait_ge(mul_done, 2 * KC)
                        for kk in range(2):
                            k = 2 * i + kk
                            last = product([ps[:, t, :]], act_hi[:, k, s:s + P], act_lo[:, k, s:s + P],
                                           [whi[:, c % RING, 512 * kk:512 * (kk + 1)]],
                                           [wlo[:, c % RING, 512 * kk:512 * (kk + 1)]],
                                           i == 0 and kk == 0, i == WCH - 1 and kk == 1)
                        if i == WCH - 1 and t < TILES - 1:
                            last.then_inc(acc_ready, 1)
                    last.then_inc(used, 1)

            out_block(0)
            with pe.Fori(1, 4) as n:
                out_block(n)

            pe.wait_ge(acc_free, 5 + 20)
            def logits(t):
                pe.wait_ge(rt_done, 4 * t + 4)
                if t == 0:
                    pe.wait_ge(s_wr, 32)
                if t == 4:
                    pe.wait_ge(lg_done, 1)
                for k in range(KC):
                    last = pe.matmul(ps[:, 4 + t % 4, 0:NG + NE], h1T[:, t % 2, k, :], wrout[:, k, :],
                                     start=k == 0, stop=k == KC - 1)
                last.then_inc(lg_ready, 1)

            for t in range(TILES):
                pe.wait_ge(ln_done[1][t], 1)
                for q in range(4):
                    if t:
                        pe.wait_ge(rt_done, 4 * (t - 1) + q + 1)
                    for c in range(4):
                        k = 4 * q + c
                        last = pe.transpose(ps[:, q, P * c:P * (c + 1)], rows[:, t, P * k:P * (k + 1)], ident)
                    last.then_inc(rt_ready, 1)
                if t:
                    logits(t - 1)
            logits(TILES - 1)
            pe.wait_ge(lg_done, TILES)
            pe.sem_inc(eused, ERING)
            pe.wait_ge(r_any, 1)
            every = anyone[:, :, :].rearrange("p t e -> p (t e)")
            pe.matmul(ps[:, 5, 0:TILES * NE], const("ltri"), every, start=True, stop=True)
            pe.matmul(ps[:, 6, 0:TILES * NE], ones[:, :], every, start=True, stop=True).then_inc(r_pos, 1)
            pe.wait_ge(r_hot, 1)
            for n in range(2 * TILES):
                last = pe.matmul(ps[0:CAP, 6, 0:2 * NTAB], slot1[:, n, :],
                                 block2[:, n, :, :].rearrange("p a n -> p (a n)"), start=n == 0, stop=n == 2 * TILES - 1)
            last.then_inc(r_table, 1)

            def xt(b, q):
                if q == 0:
                    pe.wait_ge(gathered, 16 * b + 16)
                past(pe, xt_lo, 4 * b + q - 1 if q else 4 * b)
                pe.wait_ge(pad_cols, 1)
                for c in range(4):
                    k = 4 * q + c
                    last = pe.transpose(ps[:, 6 + q % 2, P * c:P * (c + 1)], xrow[:, P * k:P * (k + 1)], ident)
                last.then_inc(xt_ready, 1)

            def ht(b):
                pe.wait_ge(h_done, b + 1)
                pe.wait_ge(pad_cols, 5)
                for c in range(4):
                    last = pe.transpose(ps[:, 1, P * c:P * (c + 1)], hrow[:, P * c:P * (c + 1)], ident)
                last.then_inc(ht_ready, 1)

            def down_product(b, i, k):
                pe.wait_ge(elo_done, number(b, i) + 1)
                for n in range(4):
                    last = product([ps[:, 2 + n, :]], hT_hi[:, k, :], hT_lo[:, k, :],
                                   [ehi[:, i % ERING, 512 * n:512 * (n + 1)]],
                                   [elo[:, i % ERING, 512 * n:512 * (n + 1)]], k == 0, k == 3)
                    if k == 3 and n < 3:
                        last.then_inc(y_ready, 1)
                last.then_inc(eused, 1)

            def moe_round(b):
                follows = not (isinstance(b, int) and b < 1)
                pe.wait_ge(xt_lo, 4 * b + 4)
                for i in range(8):
                    if i == 0:
                        past(pe, silu_done, b)
                    if i == 2 and follows:
                        ht(b - 1)
                    if i == 4:
                        past(pe, ht_lo, b)
                    pe.wait_ge(elo_done, number(b, i) + 1)
                    for kk in range(4):
                        k = 4 * (i % 4) + kk
                        last = product([ps[:, i // 4, :]], xT_hi[:, k, :], xT_lo[:, k, :],
                                       [ehi[:, i % ERING, F * kk:F * (kk + 1)]],
                                       [elo[:, i % ERING, F * kk:F * (kk + 1)]], k == 0, k == KC - 1)
                    last.then_inc(eused, 1)
                xt(b + 1, 0)
                xt(b + 1, 1)
                if follows:
                    past(pe, y_done, 4 * (b - 1))
                    down_product(b, 8, 0)
                xt(b + 1, 2)
                xt(b + 1, 3)
                if follows:
                    for k in range(1, 4):
                        down_product(b, 8 + k, k)

            for q in range(4):
                xt(0, q)
            moe_round(0)
            moe_round(1)
            with pe.Fori(2, NE) as b:
                moe_round(b)
            n_over = pe.value_load(steer[0:1, NX + 1:NX + 2], min_val=0, max_val=NX)
            with pe.If(n_over > 0):
                with pe.Fori(0, NX) as x_block:
                    with pe.If(x_block < n_over):
                        moe_round(x_block + NE)
                    pe.nop()
            pe.nop()
            end = n_over + NE
            ht(end - 1)
            pe.wait_ge(ht_lo, end)
            pe.wait_ge(y_done, 4 * (end - 1))
            for k in range(4):
                down_product(end, k, k)
            pe.wait_ge(eused, number(end, 3) + (1 + ERING))
            pe.sem_inc(moe_end, 1)


_INS = ["x", "meta_tokens", "in_ln_g", "in_ln_b", "w_in", "b_gate", "w_pool_group", "pool_scale", "w_branch_pool",
        "w_branch_fourier", "w_out", "ln1_g", "ln1_b", "w_router_group", "b_router_group", "w_router_expert",
        "b_router_expert", "w_gate", "w_up", "w_down", "ln2_g", "ln2_b"]


def kernel(**inputs):
    import concourse.bacc as _bacc
    from concourse.bass_utils import run_bass_kernel_spmd as _run

    nc = _bacc.Bacc("TRN2", target_bir_lowering=False, num_devices=1)
    small, chan, pos, edge = shape_constants()
    arrays, args = {}, []

    def add(name, a):
        arrays[name] = a
        args.append(nc.dram_tensor(name, a.shape, mybir.dt.from_np(a.dtype), kind="ExternalInput").ap())

    for name in _INS:
        a = np.ascontiguousarray(inputs[name])
        if a.ndim == 1:
            a = a.reshape(1, -1)
        add(f"in_{name}", a)
    add("k_small", small)
    add("k_chan", chan)
    add("k_pos", pos)
    add("k_edge", edge.reshape(1, -1))
    args.append(nc.dram_tensor("out", (1, SEQ, D), F32, kind="ExternalOutput").ap())
    encoder_kernel(nc, *args)
    r = _run(nc, [arrays], core_ids=[0])
    return r.results[0]["out"]
```

```python
from contextlib import ExitStack

import concourse.bass as bass
import numpy as np
from concourse import mybir

F32 = mybir.dt.float32
F32R = mybir.dt.float32r
U32 = mybir.dt.uint32
I32 = mybir.dt.int32
ALU = mybir.AluOpType
ACT = mybir.ActivationFunctionType
AX = mybir.AxisListType.X

P = 128
D = 2048
SEQ = 512
META = 16
T = SEQ + META
TILES = 5
STARTS = [0, 128, 256, 384, T - P]
KC = D // P
HALF = T // 2
HC = HALF + 2
NG = 4
GD = 256
W2 = NG * GD
NE = 32
EG = 8
F = D // 4
CAP = 64
NX = 2 * T // (CAP + 1)
NB = NE + NX
NTAB = NB + 1
ALPHA = 2.0 ** 0.25
EPS = 1e-5
BIG = 1e30
EMPTY = 8192

MC = 1024
RAW, RING = 4, 2
EC = 2048
ECH = 12
ERING = 4

FCH, PCH, JCH, WCH = 12, 6, 6, 4
F0 = 0
P0 = F0 + NG * FCH
J0 = P0 + NG * PCH
W0 = J0 + KC * JCH
PAIRS = KC // 2
WEND = W0 + PAIRS * WCH

PADW = 8
UW = T + 2 * PADW

CONST = {}
_at = 0
for _n, _w in (("ident", P), ("ltri", P), ("r32", NE), ("slot", CAP), ("block", NTAB), ("r4", NG), ("steps", 8),
               ("valid", TILES), ("token", 2 * TILES), ("x", NX)):
    CONST[_n] = (_at, _at + _w)
    _at += _w
NCONST = _at


def shape_constants():
    k = np.zeros((P, NCONST), np.float32)

    def put(name, v):
        k[:, CONST[name][0]:CONST[name][1]] = v

    i = np.arange(P)
    put("ident", np.eye(P))
    put("ltri", i[:, None] < i[None, :])
    put("r32", NE - np.arange(NE)[None])
    put("slot", np.arange(CAP)[None])
    put("block", np.arange(NTAB)[None])
    put("r4", NG - np.arange(NG)[None])
    own = np.ones((P, TILES))
    own[:TILES * P - T, TILES - 1] = 0
    put("valid", own)
    tok = np.array(STARTS)[None, :] + i[:, None]
    put("token", np.concatenate([(tok + 1) * own, (tok + 1 + T) * own], 1))
    put("x", np.arange(NX)[None])
    put("steps", CAP * np.arange(1, 9)[None])
    c = np.arange(GD)
    ang = 2 * np.pi * (np.outer(c, c) % GD) / GD
    chan = np.concatenate([np.cos(ang), np.sin(ang)], 1) / np.sqrt(GD)
    n = np.arange(T)
    ang = 2 * np.pi * (np.outer(n, n) % T) / T
    pos = np.zeros((TILES, P, 2, HC))
    for t, s in enumerate(STARTS):
        pos[t, :, 0] = np.cos(ang[s:s + P, :HC]) / np.sqrt(T)
        pos[t, :, 1] = -np.sin(ang[s:s + P, :HC]) / np.sqrt(T)
    pos[TILES - 1, :TILES * P - T] = 0
    edge = np.zeros((NG, 2 * PADW))
    for g in range(NG):
        w = 2 ** (g + 1)
        cnt = np.clip(n + w // 2 - 1, 0, T - 1) - np.clip(n - w // 2, 0, T - 1) + 1
        edge[g] = (w / cnt)[np.r_[0:PADW, T - PADW:T]]
    return k, chan.astype(np.float32), pos.reshape(TILES, P, 2 * HC).astype(np.float32), edge.astype(np.float32)


def encoder_kernel(nc, x, meta_tokens, in_ln_g, in_ln_b, w_in, b_gate, w_pool_group, pool_scale, w_branch_pool,
                   w_branch_fourier, w_out, ln1_g, ln1_b, w_router_group, b_router_group, w_router_expert,
                   b_router_expert, w_gate, w_up, w_down, ln2_g, ln2_b, k_small, k_chan, k_pos, k_edge, out):
    h0_dram = nc.dram_tensor("h0_rows", [T, D], F32).ap()
    h1_dram = nc.dram_tensor("h1_rows", [T, D], F32).ap()
    y_dram = nc.dram_tensor("expert_rows", [2 * T, D], F32).ap()

    base = (nc.sbuf_base + 31) // 32 * 32

    def sb(name, shape, dt, at):
        return nc.alloc_sbuf_tensor_at(name, shape, dt, offset=base + at)

    act_hi = sb("act_hi", [P, KC, T], F32R, 0)
    act_lo = sb("act_lo", [P, KC, T], F32R, 33792)
    mix_hi = sb("mix_hi", [P, KC, T], F32R, 67584)
    mix_lo = sb("mix_lo", [P, KC, T], F32R, 101376)
    chan_hi = mix_hi[:, 0:2, :]
    chan_lo = mix_lo[:, 0:2, :]
    freq_hi = mix_hi[:, 2:7, 0:2 * GD]
    freq_lo = mix_lo[:, 2:7, 0:2 * GD]
    raw = sb("raw", [P, RAW, MC], F32, 135168)
    whi = sb("whi", [P, RING, MC], F32R, 151552)
    wlo = sb("wlo", [P, RING, MC], F32R, 159744)
    merged = sb("merged", [P, KC, T], F32, 167936)
    consts = sb("consts", [P, NCONST], F32, 201728)
    small_at = 201728 + (4 * NCONST + 31) // 32 * 32

    def small(name, shape, dt):
        nonlocal small_at
        t = sb(name, shape, dt, small_at)
        small_at += (int(np.prod(shape[1:])) * 4 + 31) // 32 * 32
        return t

    cols = small("cols", [P, 40], F32)
    edge = small("edge", [P, NG, 2 * PADW], F32)
    rbias = small("rbias", [P, NG + NE], F32)
    gidx = small("gidx", [CAP, NTAB], U32)
    sidx = small("sidx", [CAP, NTAB], U32)
    gatew = small("gatew", [CAP, NTAB], F32)
    steer = small("steer", [1, NX + 2], I32)
    assert small_at <= 204992
    stage = sb("stage", [P, 3, UW], F32, 204992)
    sine = stage[:, 0, :].rearrange("p (m n) -> p m n", m=2)
    rows = sb("rows", [P, TILES, D], F32, 67584)
    resid = sb("resid", [P, 2, TILES, 512], F32, 108544)
    gb = sb("gb", [P, 2, D], F32, 167936)
    colsrc = sb("colsrc", [40, P], F32, 184320)
    outT = sb("outT", [P, 2, T], F32, 207296)
    stats = sb("stats", [P, TILES, PAIRS, 6], F32, 211520)
    mv = sb("mv", [P, TILES, 2], F32, 212480)
    std = sb("std", [P, TILES], F32, 212544)
    rstd = sb("rstd", [P, TILES], F32, 212576)
    nmr = sb("nmr", [P, TILES], F32, 212608)
    h1T = sb("h1T", [P, 2, KC, P], F32, 0)
    wrout = sb("wrout", [P, KC, NG + NE], F32, 204992)
    logit = sb("logit", [P, TILES, NG + NE], F32, 207296)
    rt = [167936, 100352]

    def rbuf(name, shape, dt=F32, area=0):
        t = sb(name, shape, dt, rt[area])
        rt[area] += (int(np.prod(shape[1:])) * 4 + 31) // 32 * 32
        return t

    gmax = rbuf("gmax", [P, TILES])
    gdif = rbuf("gdif", [P, TILES, NG])
    gexp = rbuf("gexp", [P, TILES, NG])
    gsum = rbuf("gsum", [P, TILES])
    gprob = rbuf("gprob", [P, TILES])
    gone = rbuf("gone", [P, TILES, NG])
    gpick = rbuf("gpick", [P, TILES])
    masked = rbuf("masked", [P, TILES, NE])
    masked2 = rbuf("masked2", [P, TILES, NE])
    emax = rbuf("emax", [P, 2, TILES])
    epick = rbuf("epick", [P, 2, TILES])
    etmp = rbuf("etmp", [P, TILES, NE])
    one = rbuf("one", [P, 2, TILES, NE])
    anyone = rbuf("anyone", [P, TILES, NE])
    ones = rbuf("ones", [P, P])
    ediff = rbuf("ediff", [P, TILES])
    eexp = rbuf("eexp", [P, TILES])
    esum = rbuf("esum", [P, TILES])
    gate = rbuf("gate", [P, 2, TILES])
    posn = rbuf("posn", [P, TILES, NE])
    earlier = rbuf("earlier", [P, TILES + 1, NE])
    over = rbuf("over", [P, 8, NE])
    nover = rbuf("nover", [P, NE])
    cum = rbuf("cum", [P, NE])
    excl = rbuf("excl", [P, NE])
    prod = rbuf("prod", [P, 2, TILES, NE])
    apos = rbuf("apos", [P, 2, TILES])
    aexp = rbuf("aexp", [P, 2, TILES])
    aexc = rbuf("aexc", [P, 2, TILES])
    step8 = rbuf("step8", [P, 8, 2 * TILES])
    turn = rbuf("turn", [P, 2, TILES])
    turn1 = rbuf("turn1", [P, 2, TILES])
    aslot = rbuf("aslot", [P, 2, TILES])
    ablock = rbuf("ablock", [P, 2, TILES])
    slot1 = rbuf("slot1", [P, 2 * TILES, CAP], area=1)
    block1 = rbuf("block1", [P, 2 * TILES, NTAB], area=1)
    block2 = rbuf("block2", [P, 2 * TILES, 2, NTAB])
    table = rbuf("table", [CAP, 2, NTAB])
    none = rbuf("none", [CAP, NTAB])
    sidxf = rbuf("sidxf", [CAP, NTAB])
    second = rbuf("second", [CAP, NTAB])
    gidxf = rbuf("gidxf", [CAP, NTAB])
    below = rbuf("below", [P, NX, NE], area=1)
    steerf = rbuf("steerf", [P, NX + 2])
    assert rt[0] <= 184320 and rt[1] <= 108544, rt
    ehi = sb("ehi", [P, ERING, EC], F32R, 0)
    elo = sb("elo", [P, ERING, EC], F32R, 32768)
    hrow = sb("hrow", [P, F], F32, 65536)
    SLOTS = [184320, 192512, 135168, 143360, 151552, 159744, 108544, 116736, 124928, 67584, 75776, 83968]
    eraw = [sb(f"eraw{i}", [P, EC], F32, at) for i, at in enumerate(SLOTS)]
    xrow = sb("xrow", [P, D], F32, 92160)
    yrow = sb("yrow", [CAP, D], F32, 100352)
    xT_hi = sb("xT_hi", [P, KC, P], F32R, 167936)
    xT_lo = sb("xT_lo", [P, KC, P], F32R, 176128)
    hT_hi = sb("hT_hi", [P, 4, P], F32R, 204992)
    hT_lo = sb("hT_lo", [P, 4, P], F32R, 207040)
    gcol = sb("gcol", [CAP, 1], F32, 211200)
    srow = sb("srow", [P, F], F32, 209088)
    gcur = sb("gcur", [CAP, 1], U32, 211136)
    scur = sb("scur", [CAP, 1], U32, 211168)
    fin_rows = [P, P, P, P, T - 4 * P]
    fin_order = [4, 0, 1, 2, 3]
    fin_h = [eraw[t][0:fin_rows[t], :] for t in range(TILES)]
    fin_g, fin_b = eraw[5], eraw[6]
    fin_ring = sb("fin_ring", [P, 8, D], F32, 0)
    fin_y = [[fin_ring[:, 2 * t + a, :] for a in range(2)] for t in range(4)]
    fin_y.append([eraw[7][0:fin_rows[4], :], eraw[8][0:fin_rows[4], :]])
    fin_small = sb("fin_small", [P, 6, TILES], F32, 212128)
    fin_eps = sb("fin_eps", [P, 1], F32, 212256)
    ident = consts[:, 0:P]

    def const(name, parts=P):
        a, b = CONST[name]
        return consts[0:parts, a:b]

    ctx = ExitStack()
    with ctx:
        ps = ctx.enter_context(nc.psum_tensor("ps", [P, 8, 512], F32))

        def sem(name):
            return ctx.enter_context(nc.semaphore(name))

        s_small = sem("s_small")
        s_wr = sem("s_wr")
        s_row = [sem(f"s_row{t}") for t in range(TILES)]
        s_gb0 = [sem(f"s_gb0_{i}") for i in range(2)]
        s_gb1 = sem("s_gb1")
        s_gb2 = sem("s_gb2")
        s_raw = [sem(f"s_raw{i}") for i in range(RAW)]
        s_res = [sem(f"s_res{i}") for i in range(2)]
        s_eraw = [sem(f"s_eraw{i}") for i in range(ECH)]
        s_h0 = sem("s_h0")
        s_h1 = sem("s_h1")
        s_out = sem("s_out")
        hi_done = sem("hi_done")
        lo_done = sem("lo_done")
        used = sem("used")
        ln_var = [sem(f"ln_var{i}") for i in range(2)]
        ln_mv = [sem(f"ln_mv{i}") for i in range(2)]
        ln_std = [sem(f"ln_std{i}") for i in range(2)]
        ln_norm = [sem(f"ln_norm{i}") for i in range(2)]
        ln_g = [sem(f"ln_g{i}") for i in range(2)]
        ln_done = [[sem(f"ln_done{i}_{t}") for t in range(TILES)] for i in range(2)]
        tr_ready = sem("tr_ready")
        tr_hi = sem("tr_hi")
        tr_lo = sem("tr_lo")
        cols_ready = sem("cols_ready")
        cols_done = sem("cols_done")
        fu_hi = sem("fu_hi")
        fu_lo = sem("fu_lo")
        fv_ready = sem("fv_ready")
        fv_hi = sem("fv_hi")
        fv_lo = sem("fv_lo")
        fo_ready = sem("fo_ready")
        fo_sin = sem("fo_sin")
        fo_sum = sem("fo_sum")
        fo_hi = sem("fo_hi")
        fo_lo = sem("fo_lo")
        pad_zero = sem("pad_zero")
        pu_copied = sem("pu_copied")
        pw_step = sem("pw_step")
        pw_done = sem("pw_done")
        pd_hi = sem("pd_hi")
        pd_lo = sem("pd_lo")
        pm_hi = sem("pm_hi")
        pm_lo = sem("pm_lo")
        gate_done = sem("gate_done")
        mul_done = sem("mul_done")
        merge_done = sem("merge_done")
        mt_hi = sem("mt_hi")
        mt_lo = sem("mt_lo")
        out_copied = sem("out_copied")
        out_tr = sem("out_tr")
        acc_free = sem("acc_free")
        bn_done = sem("bn_done")
        s_ln0 = sem("s_ln0")
        s_agg = [sem(f"s_agg{i}") for i in range(2)]
        rt_ready = sem("rt_ready")
        rt_done = sem("rt_done")
        lg_ready = sem("lg_ready")
        lg_done = sem("lg_done")
        r_step = sem("r_step")
        r_gexp = sem("r_gexp")
        r_eexp = sem("r_eexp")
        r_any = sem("r_any")
        r_pos = sem("r_pos")
        r_hot = sem("r_hot")
        r_table = sem("r_table")
        r_gidx = sem("r_gidx")
        r_done = sem("r_done")
        pad_cols = sem("pad_cols")
        ehi_done = sem("ehi_done")
        elo_done = sem("elo_done")
        eused = sem("eused")
        idx_g = sem("idx_g")
        idx_s = sem("idx_s")
        gathered = sem("gathered")
        scattered = sem("scattered")
        xt_ready = sem("xt_ready")
        xt_hi = sem("xt_hi")
        xt_lo = sem("xt_lo")
        silu_done = sem("silu_done")
        h_done = sem("h_done")
        ht_ready = sem("ht_ready")
        ht_hi = sem("ht_hi")
        ht_lo = sem("ht_lo")
        y_ready = sem("y_ready")
        y_done = sem("y_done")
        gcol_done = sem("gcol_done")
        moe_end = sem("moe_end")
        s_fh = [sem(f"s_fh{t}") for t in range(TILES)]
        s_fy = [sem(f"s_fy{t}") for t in range(TILES)]
        f_eps = sem("f_eps")
        f_sum = sem("f_sum")
        f_mean = sem("f_mean")
        f_sq = sem("f_sq")
        f_std = sem("f_std")
        f_mv = sem("f_mv")
        f_norm = sem("f_norm")
        f_g = sem("f_g")
        f_pair = sem("f_pair")
        f_done = [sem(f"f_done{j}") for j in range(TILES + 1)]

        block = ctx.enter_context(nc.Block())

        def win_half(col, half):
            return w_in[0, 1024 * half:1024 * (half + 1), col].rearrange("(k p) n -> p k n", p=P)

        def past(eng, sem, value):
            if not isinstance(value, int) or value > 0:
                eng.wait_ge(sem, value)

        def at(start, size=P):
            return bass.ds(start, size)

        def raw3(i, n, w):
            return raw[:, i, 0:n * w].rearrange("p (k n) -> p k n", n=w)

        def add_b(eng, i, t):
            eng.wait_ge(ln_g[i], t + 1)
            eng.tensor_tensor(rows[:, t, :], rows[:, t, :], gb[:, 1, :], ALU.add).then_inc(ln_done[i][t], 1)

        def fin_add_b(eng, j, part=slice(0, D), done=0):
            t = fin_order[j]
            eng.wait_ge(f_g, j + 1)
            eng.tensor_tensor(fin_h[t][:, part], fin_h[t][:, part], fin_b[0:fin_rows[t], part],
                              ALU.add).then_inc(f_done[j + done], 1)

        def u_chunk(g):
            return P0 + (PCH * g - 2 if g else 0)

        def g_chunk(g):
            return u_chunk(g + 1) + 4 if g < NG - 1 else J0

        GATE0 = J0 - 2

        def used_cols(bank):
            return bank.rearrange("p (c n) -> p c n", n=P)[:, :, 0:CAP]

        def pos_part(i):
            if i < 10:
                return i - 6, slice(0, 2 * HC)
            return TILES - 1, slice(HC * (i - 10), HC * (i - 9))

        def pos_width(i):
            return 2 * HC if i < 10 else HC

        def own_rows(t):
            lo = t * P
            return lo, min(T, lo + P), lo - STARTS[t]

        def out_bank(t):
            return ps[:, 4 + t // 2, 256 * (t % 2):256 * (t % 2 + 1)]

        RT_BANK = [7, 0, 1, 2]
        TR_BANK = [0, 4, 0, 4, 4]

        def own_columns(t):
            lo, hi, _ = own_rows(t)
            return slice(lo, hi)

        def own_part(t, q):
            _, _, r = own_rows(t)
            return ps[:, q + TR_BANK[t], :].rearrange("p (c n) -> p c n", n=P)[:, :, r:]

        def gate_up(e, i):
            w = w_gate if i < 4 else w_up
            return w[0, bass.ds(e, 1), 512 * (i % 4):512 * (i % 4 + 1), :].rearrange("a (k p) n -> p (a k) n", p=P)

        def down(e, i):
            return w_down[0, bass.ds(e, 1), P * i:P * (i + 1), :].rearrange("a p n -> p (a n)")

        def number(b, i):
            return i if isinstance(b, int) and b == 0 else ECH * b + (i - 4)

        def place(b, i):
            if isinstance(b, int) and b == 0:
                return i, 1
            return (i + 8) % ECH, b + (i + 8) // ECH

        def eraw_gate(slot):
            return eraw[slot][:, :].rearrange("p (k n) -> p k n", n=F)

        @block.sync
        def _(sp):
            x_rows = x.rearrange("b s d -> (b s) d")
            sp.dma_start(rows[0:META, 0, :], meta_tokens).then_inc(s_row[0], 16)
            sp.dma_start(rows[META:P, 0, :], x_rows[0:P - META, :]).then_inc(s_row[0], 16)
            for t in range(1, TILES):
                sp.dma_start(rows[:, t, :], x_rows[STARTS[t] - META:STARTS[t] - META + P, :]).then_inc(s_row[t], 16)
                if t == 1:
                    for i, v in enumerate((in_ln_g, in_ln_b)):
                        sp.dma_start(gb[:, i, :], v.broadcast_to([P, D])).then_inc(s_gb0[i], 16)
            sp.wait_ge(s_small, 16 * 6)

            def chunk(n, slot, dst, src):
                if isinstance(n, int) and n < RAW:
                    pass
                else:
                    sp.wait_ge(lo_done, n - RAW + 1)
                sp.dma_start(dst, src).then_inc(s_raw[slot], 16)

            def store_rows(dst, i, done):
                for t in range(TILES):
                    lo, hi, r = own_rows(t)
                    sp.wait_ge(ln_done[i][t], 1)
                    sp.dma_start(dst[lo:hi, :], rows[r:r + hi - lo, t, :]).then_inc(done, 16)

            def fourier_group(g, first):
                for i in range(4):
                    n = F0 + i if first else F0 + FCH * g + i
                    chunk(n, i % RAW, raw3(i % RAW, 8, P), win_half(at(W2 + GD * g + P * (i // 2)), i % 2))
                if first:
                    store_rows(h0_dram, 0, s_h0)
                for i in range(4, 6):
                    chunk(F0 + FCH * g + i, i % RAW, raw[:, i % RAW, 0:512], k_chan[P * (i - 4):P * (i - 3), :])
                for i in range(6, FCH):
                    t, part = pos_part(i)
                    chunk(F0 + FCH * g + i, i % RAW, raw[:, i % RAW, 0:pos_width(i)], k_pos[t, :, part])

            fourier_group(0, True)
            with sp.Fori(1, NG) as g:
                fourier_group(g, False)
            def u_chunks(g):
                for i in range(4):
                    n = u_chunk(g) + i
                    chunk(n, n % RAW, raw3(n % RAW, 8, P), win_half(at(GD * g + P * (i // 2)), i % 2))

            def g_chunks(g):
                for k in range(2):
                    n = g_chunk(g) + k
                    chunk(n, n % RAW, raw[:, n % RAW, 0:GD], w_pool_group[0, g, P * k:P * (k + 1), :])

            u_chunks(0)
            for g in range(1, NG):
                u_chunks(g)
                g_chunks(g - 1)

            def column_chunks(jj, b):
                if not isinstance(jj, int):
                    sp.to_reg(4 * (P * (2 * jj + b)))
                for i in range(JCH):
                    j = 2 * jj + b
                    n = J0 + JCH * b + i + 2 * JCH * jj
                    slot = (J0 + JCH * b + i) % RAW
                    if isinstance(j, int) and j == 0 and i < 2:
                        n = GATE0 + i
                        slot = n % RAW
                    if i < 4:
                        src = win_half(at(2 * W2 + D * (i // 2) + P * j), i % 2)
                    else:
                        w = (w_branch_pool, w_branch_fourier)[i - 4]
                        src = w[0, :, at(P * j)].rearrange("(k p) n -> p k n", p=P)
                    chunk(n, slot, raw3(slot, 8, P), src)
                    if isinstance(j, int) and j == 0 and i == 1:
                        g_chunks(NG - 1)

            column_chunks(0, 0)
            column_chunks(0, 1)
            with sp.Fori(1, KC // 2) as jj:
                for b in range(2):
                    column_chunks(jj, b)
            with sp.Fori(0, PAIRS) as pair:
                for i in range(WCH):
                    slot = (W0 + i) % RAW
                    chunk(W0 + i + WCH * pair, slot, raw3(slot, 8, P),
                          w_out[0, 1024 * (i % 2):1024 * (i % 2 + 1), at(2 * P * pair + P * (i // 2))]
                          .rearrange("(k p) n -> p k n", p=P))

            def expert_chunk(b, i, dst, src):
                slot, _ = place(b, i)
                past(sp, elo_done, number(b, i) - ECH + 1)
                sp.dma_start(dst(slot), src).then_inc(s_eraw[slot], 16)

            def down_chunks(b, e, places):
                for i in places:
                    expert_chunk(b, i, lambda slot: eraw[slot][:, :], down(e, i % 4))

            def round_chunks(b, e, e_down):
                for i in range(8):
                    expert_chunk(b, i, eraw_gate, gate_up(e, i))
                down_chunks(b, e_down, range(8, 12))

            for n in range(ECH):
                if n == 0:
                    sp.wait_ge(mt_lo, KC // 2)
                if n == 2:
                    sp.wait_ge(used, WEND)
                if n == 6:
                    sp.wait_ge(acc_free, TILES * PAIRS)
                if n == 9:
                    store_rows(h1_dram, 1, s_h1)
                if 9 <= n:
                    sp.wait_ge(rt_ready, 4 * (n - 8))
                    sp.wait_ge(s_h1, 16 * TILES)
                b, i = divmod(n, 8)
                expert_chunk(b, i, eraw_gate, gate_up(b, i))
            for i in range(4, 8):
                expert_chunk(1, i, eraw_gate, gate_up(1, i))
            down_chunks(1, 0, range(8, 12))
            with sp.Fori(2, NE) as b:
                round_chunks(b, b, b - 1)
            sp.wait_ge(r_done, 1)
            n_over = sp.value_load(steer[0:1, NX + 1:NX + 2], min_val=0, max_val=NX)
            with sp.If(n_over > 0):
                with sp.Fori(0, NX) as x_block:
                    with sp.If(x_block < n_over):
                        e_down = sp.value_load(steer[0:1, at(x_block, 1)], min_val=0, max_val=NE - 1)
                        e = sp.value_load(steer[0:1, at(x_block + 1, 1)], min_val=0, max_val=NE - 1)
                        round_chunks(x_block + NE, e, e_down)
                    sp.nop()
            sp.nop()
            e_last = sp.value_load(steer[0:1, at(n_over, 1)], min_val=0, max_val=NE - 1)
            down_chunks(n_over + NE, e_last, range(4))

            sp.wait_ge(elo_done, number(n_over + NE, 0))
            sp.dma_start(fin_g[:, :], ln2_g.broadcast_to([P, D])).then_inc(s_gb2, 16)
            sp.dma_start(fin_b[:, :], ln2_b.broadcast_to([P, D])).then_inc(s_gb2, 16)
            for t in fin_order:
                sp.dma_start(fin_h[t], h1_dram[P * t:P * t + fin_rows[t], :]).then_inc(s_fh[t], 16)
            sp.wait_ge(moe_end, 4)
            for t in fin_order:
                for a in range(2):
                    s = a * T + P * t
                    sp.dma_start(fin_y[t][a], y_dram[s:s + fin_rows[t], :]).then_inc(s_fy[t], 16)
            out_rows = out.rearrange("b s d -> (b s) d")
            for j, t in enumerate(fin_order):
                skip = META if t == 0 else 0
                dst = out_rows[P * t + skip - META:P * t + fin_rows[t] - META, :]
                for k, part in enumerate([slice(0, D)] if j < TILES - 1 else [slice(0, D // 2), slice(D // 2, D)]):
                    sp.wait_ge(f_done[j + k], 1)
                    sp.dma_start(dst[:, part], fin_h[t][skip:, part]).then_inc(s_out, 16)
            sp.wait_ge(s_out, 16 * (TILES + 1))

        @block.gpsimd
        def _(pool):
            pool.dma_start(consts[:, :], k_small).then_inc(s_small, 16)
            pool.dma_start(colsrc[0:32, :], b_gate.rearrange("a (j p) -> (a j) p", p=P)).then_inc(s_small, 16)
            pool.dma_start(colsrc[32:40, :], pool_scale.rearrange("a (j p) -> (a j) p", p=P)).then_inc(s_small, 16)
            pool.dma_start(edge[:, :, :].rearrange("p g w -> p (g w)"), k_edge.broadcast_to([P, NG * 2 * PADW])).then_inc(s_small, 16)
            pool.dma_start(rbias[:, 0:NG], b_router_group.broadcast_to([P, NG])).then_inc(s_small, 16)
            pool.dma_start(rbias[:, NG:NG + NE], b_router_expert.broadcast_to([P, NE])).then_inc(s_small, 16)
            pool.wait_ge(s_gb0[1], 16)
            for t in range(TILES):
                add_b(pool, 0, t)

            pool.wait_ge(s_small, 16 * 6)
            steps = 0

            def pstep(ins):
                nonlocal steps
                steps += 1
                ins.then_inc(pw_step, 1)
                pool.wait_ge(pw_step, steps)

            pool.wait_ge(fo_lo, 2 * NG)
            pool.memset(stage[:, 0, :], 0.0).then_inc(pad_zero, 1)
            for n in range(2 * NG):
                g = n // 2
                w = 2 ** (g + 1)
                pool.wait_ge(pu_copied, n + 1)
                src, width, shift = 0, UW, 1
                for s in range(g + 1):
                    dst = 2 - s % 2
                    width -= shift
                    pstep(pool.tensor_tensor(stage[:, dst, 0:width], stage[:, src, 0:width],
                                             stage[:, src, shift:shift + width], ALU.add))
                    src, shift = dst, shift * 2
                a = PADW - w // 2
                res = stage[:, src, a:a + T]
                for k, c in ((0, 0), (1, T - PADW)):
                    pstep(pool.tensor_tensor(res[:, c:c + PADW], res[:, c:c + PADW],
                                             edge[:, g, PADW * k:PADW * (k + 1)], ALU.mult))
                pstep(pool.tensor_scalar(res, res, 1.0 / w, None, ALU.mult))
                dst = 3 - src
                assert dst == 1 + g % 2, (g, src, dst)
                pool.tensor_tensor(stage[:, dst, 0:T], res, stage[:, 0, PADW:PADW + T], ALU.subtract).then_inc(pw_done, 1)

            def residual(n):
                for t in range(TILES):
                    s = STARTS[t]
                    pool.dma_start(resid[:, n % 2, t, :], h0_dram[s:s + P, 512 * n:512 * (n + 1)]).then_inc(s_res[n % 2], 16)

            pool.wait_ge(used, W0)
            pool.wait_ge(s_h0, 16 * TILES)
            residual(0)
            residual(1)
            pool.wait_ge(mt_lo, KC // 2)
            for i, v in enumerate((ln1_g, ln1_b)):
                pool.dma_start(gb[:, i, :], v.broadcast_to([P, D])).then_inc(s_gb1, 16)
            pool.wait_ge(merge_done, KC)
            pool.dma_start(wrout[:, :, 0:NG], w_router_group[0].rearrange("(k p) n -> p k n", p=P)).then_inc(s_wr, 16)
            pool.dma_start(wrout[:, :, NG:NG + NE], w_router_expert[0].rearrange("(k p) n -> p k n", p=P)).then_inc(s_wr, 16)
            for n in (2, 3):
                pool.wait_ge(acc_free, 2 * TILES * (n - 1))
                residual(n)
            pool.wait_ge(s_gb1, 32)
            add_b(pool, 1, 3)
            pool.wait_ge(s_h1, 16 * TILES)
            pool.wait_ge(rt_ready, 4 * TILES)
            pool.memset(xrow[:, :], 0.0).then_inc(pad_cols, 1)
            for i in range(ERING):
                pool.wait_ge(ehi_done, i + 1)
                pool.tensor_tensor(elo[:, i, :], eraw[i][:, :], ehi[:, i, :], ALU.subtract).then_inc(elo_done, 1)
            pool.wait_ge(pad_cols, 1)
            pool.wait_ge(r_gidx, 1)

            origin_reg = pool.alloc_register("origin")
            pool.reg_mov(origin_reg, 0)

            def gather(b):
                origin = pool.snap(origin_reg, min_val=0, max_val=1)
                pool.tensor_copy(gcur[:, :], gidx[:, at(b, 1)]).then_inc(idx_g, 1)
                pool.wait_ge(idx_g, b + 1)
                pool.indirect_dma_start(xrow[0:CAP, :], None, h1_dram, bass.IndirectOffsetOnAxis(gcur[:, :], 0),
                                        bounds_check=origin + (T - 1), oob_is_err=False).then_inc(gathered, 16)

            def next_gather(b):
                pool.wait_ge(xt_ready, 4 * b + 4)
                pool.wait_ge(gathered, 16 * b + 16)
                gather(b + 1)

            def scatter(b):
                past(pool, scattered, 16 * b)
                origin = pool.snap(origin_reg, min_val=0, max_val=1)
                pool.tensor_copy(scur[:, :], sidx[:, at(b, 1)]).then_inc(idx_s, 1)
                pool.wait_ge(idx_s, b + 1)
                pool.wait_ge(y_done, 4 * b + 4)
                pool.indirect_dma_start(y_dram, bass.IndirectOffsetOnAxis(scur[:, :], 0), yrow[:, :], None,
                                        bounds_check=origin + (2 * T - 1), oob_is_err=False).then_inc(scattered, 16)

            def moe_round(b):
                next_gather(b)
                if not (isinstance(b, int) and b < 2):
                    scatter(b - 2)

            gather(0)
            pool.wait_ge(r_done, 1)
            for pads in (xT_hi, xT_lo, hT_hi, hT_lo):
                pool.memset(pads[:, :, CAP:P].bitcast(F32), 0.0).then_inc(pad_cols, 1)
            for b in range(3):
                moe_round(b)
            with pool.Fori(3, NE) as b:
                moe_round(b)
            n_over = pool.value_load(steer[0:1, NX + 1:NX + 2], min_val=0, max_val=NX)
            with pool.If(n_over > 0):
                with pool.Fori(0, NX) as x_block:
                    with pool.If(x_block < n_over):
                        moe_round(x_block + NE)
                    pool.nop()
            pool.nop()
            scatter(n_over + (NE - 2))
            scatter(n_over + (NE - 1))
            pool.wait_ge(gathered, 16 * (n_over + (NE + 1)))
            pool.wait_ge(scattered, 16 * n_over + 16 * NE)
            pool.sem_inc(moe_end, 1)

            for j in range(2, TILES):
                t = fin_order[j]
                pool.wait_ge(s_fy[t], 32)
                pool.tensor_tensor(fin_y[t][1], fin_y[t][0], fin_y[t][1], ALU.add).then_inc(f_pair, 1)
            pool.wait_ge(s_gb2, 32)
            for j in (2, 3):
                fin_add_b(pool, j)

        @block.scalar
        def _(act):
            def copy(dst, src, done, **kw):
                act.activation(dst, src, ACT.Copy, **kw).then_inc(done, 1)

            def ln_root(i, t):
                act.wait_ge(ln_var[i], t + 1)
                act.activation(std[:, t:t + 1], std[:, t:t + 1], ACT.Sqrt).then_inc(ln_std[i], 1)

            def ln_normal(i, t):
                act.wait_ge(ln_mv[i], 2 * t + 2)
                act.activation(rows[:, t, :], rows[:, t, :], ACT.Identity, bias=nmr[:, t:t + 1],
                               scale=rstd[:, t:t + 1]).then_inc(ln_norm[i], 1)

            def h0_evac(t):
                for q in range(4):
                    act.wait_ge(tr_ready, 4 * t + q + 1)
                    copy(act_hi[:, 4 * q:4 * q + 4, own_columns(t)], own_part(t, q), tr_hi)

            def hi(base, i, loops, per, width=MC):
                n = base + i
                slot = n % RAW
                act.wait_ge(s_raw[slot], 16 * (n // RAW + 1) + (16 * per // RAW) * loops)
                if not (isinstance(loops, int) and n < RING):
                    act.wait_ge(used, n - RING + 1 + per * loops)
                copy(whi[:, n % RING, 0:width], raw[:, slot, 0:width], hi_done)

            for t in range(TILES):
                ln_root(0, t)
                ln_normal(0, t)
                if t == 2:
                    act.wait_ge(cols_ready, 1)
                    copy(cols[:, :], ps[:, 7, 0:40], cols_done)
                if t >= 3:
                    h0_evac(t - 3)
            hi(F0, 0, 0, FCH)
            h0_evac(2)
            hi(F0, 1, 0, FCH)
            h0_evac(3)
            h0_evac(4)
            act.wait_ge(s_h0, 16 * TILES)

            def fourier_out(g):
                for m in range(2):
                    if m == 0:
                        act.wait_ge(fo_ready, g + 1)
                    else:
                        act.wait_ge(used, F0 + FCH + FCH * g)
                    copy(sine[:, m, 0:HC], ps[:, 3 + 2 * m, 0:HC], fo_sin)
                for m in range(2):
                    act.wait_ge(fo_sum, 4 * g + 2 * m + 2)
                    copy(mix_hi[:, at(8 + 2 * g + m, 1), :].rearrange("p a n -> p (a n)"), stage[:, 1 + m, 0:T], fo_hi)

            def fourier_group(g):
                def u_evac(m):
                    act.wait_ge(used, F0 + 2 * m + 2 + FCH * g)
                    copy(chan_hi[:, m, :].rearrange("p (h n) -> p h n", h=2), ps[:, 2 * m:2 * m + 2, 0:HALF], fu_hi)

                if not isinstance(g, int):
                    hi(F0, 0, g, FCH)
                    fourier_out(g - 1)
                    hi(F0, 1, g, FCH)
                for i in range(2, 4):
                    hi(F0, i, g, FCH)
                u_evac(0)
                hi(F0, 4, g, FCH, 512)
                hi(F0, 5, g, FCH, 512)
                u_evac(1)
                hi(F0, 6, g, FCH, 2 * HC)
                for t in range(TILES):
                    if t < TILES - 1:
                        act.wait_ge(fv_ready, 4 * g + t + 1)
                    else:
                        act.wait_ge(used, F0 + 6 + FCH * g)
                    copy(freq_hi[:, t, :], ps[:, (4 + t) % 8, :], fv_hi)
                for i in range(7, FCH):
                    hi(F0, i, g, FCH, pos_width(i))

            fourier_group(0)
            with act.Fori(1, NG) as g:
                fourier_group(g)

            def u_evac(n):
                act.wait_ge(used, u_chunk(n // 2) + 2 * (n % 2) + 2)
                if n == 0:
                    act.wait_ge(pad_zero, 1)
                if n:
                    act.wait_ge(pd_lo, n)
                m = n % 2
                copy(stage[:, 0, PADW:PADW + T].rearrange("p (h n) -> p h n", h=2),
                     ps[:, 2 * m:2 * m + 2, 0:HALF], pu_copied)

            def window_hi(n):
                act.wait_ge(pw_done, n + 1)
                copy(mix_hi[:, n, :], stage[:, 1 + (n // 2) % 2, 0:T], pd_hi)

            def pool_out(g):
                act.wait_ge(used, g_chunk(g) + 2)
                act.wait_ge(cols_done, 1)
                for m in range(2):
                    n = 2 * g + m
                    act.activation(mix_hi[:, n, :].rearrange("p (h n) -> p h n", h=2), ps[:, 4 + 2 * m:6 + 2 * m, 0:HALF],
                                   ACT.Copy, scale=cols[:, 32 + n:33 + n]).then_inc(pm_hi, 1)

            for g in range(NG):
                u, gc = u_chunk(g), g_chunk(g - 1)
                hi(u, 0, 0, 0)
                if g == 0:
                    fourier_out(NG - 1)
                if g >= 2:
                    pool_out(g - 2)
                hi(u, 1, 0, 0)
                hi(u, 2, 0, 0)
                if g >= 1:
                    window_hi(2 * g - 1)
                hi(u, 3, 0, 0)
                u_evac(2 * g)
                if g >= 1:
                    hi(gc, 0, 0, 0, GD)
                window_hi(2 * g)
                if g >= 1:
                    hi(gc, 1, 0, 0, GD)
                u_evac(2 * g + 1)
            hi(GATE0, 0, 0, 0)
            pool_out(NG - 2)
            hi(GATE0, 1, 0, 0)
            hi(J0, 0, 0, 0, GD)
            window_hi(2 * NG - 1)
            hi(J0, 1, 0, 0, GD)

            def gate_columns(jj):
                for b in range(2):
                    first = isinstance(jj, int) and b == 0
                    for i in range(2 if first else 0, JCH):
                        hi(J0 + JCH * b, i, jj, 2 * JCH)
                        if first and i == 2:
                            pool_out(NG - 1)
                        if i in (3, 5):
                            a = (i - 3) // 2
                            act.wait_ge(used, J0 + JCH * b + 2 * a + 2 + 2 * JCH * jj)
                            past(act, mul_done, 4 * jj + 2 * b)
                            act.wait_ge(cols_done, 1)
                            act.activation(stage[:, a, 0:T].rearrange("p (h n) -> p h n", h=2),
                                           ps[:, 2 * a:2 * a + 2, 0:HALF], ACT.Sigmoid,
                                           bias=cols[:, at(16 * a + 2 * jj + b, 1)]).then_inc(gate_done, 1)

            gate_columns(0)
            with act.Fori(1, KC // 2) as jj:
                gate_columns(jj)

            def merged_hi(q):
                act.wait_ge(merge_done, 2 * q + 2)
                copy(act_hi[:, 2 * q:2 * q + 2, :], merged[:, 2 * q:2 * q + 2, :], mt_hi)

            act.wait_ge(used, J0 + JCH * (KC - 1) + 4)
            for q in range(4):
                merged_hi(q)
            hi(W0, 0, 0, 0)
            for q in range(4, 7):
                merged_hi(q)
            hi(W0, 1, 0, 0)
            merged_hi(7)

            def out_copy(j, p, c):
                act.wait_ge(used, W0 + 2 * c + 2 + WCH * p)
                if isinstance(j, int) and j < 2:
                    act.wait_ge(merge_done, KC)
                else:
                    act.wait_ge(out_tr, j - 1)
                copy(outT[:, c, :].rearrange("p (h n) -> p h n", h=2), ps[:, 2 * c:2 * c + 2, 0:HALF], out_copied)

            def out_pair(p):
                first = isinstance(p, int) and p == 0
                for i in range(2 if first else 0, WCH):
                    hi(W0, i, p, WCH)
                    if i == 1:
                        out_copy(2 * p - 1, p - 1, 1)
                    if i == 3:
                        out_copy(2 * p, p, 0)

            out_pair(0)
            out_pair(1)
            with act.Fori(2, PAIRS) as p:
                out_pair(p)
            out_copy(KC - 1, PAIRS - 1, 1)

            def h1_evac(t):
                for q in range(4):
                    act.wait_ge(rt_ready, 4 * t + q + 1)
                    if t >= 2 and q == 0:
                        act.wait_ge(lg_ready, t - 1)
                    copy(h1T[:, t % 2, 4 * q:4 * q + 4, :], ps[:, RT_BANK[q], :].rearrange("p (c n) -> p c n", n=P), rt_done)

            for t in range(3):
                ln_root(1, t)
                ln_normal(1, t)
            ln_root(1, 3)
            act.wait_ge(used, WEND)
            h1_evac(0)
            ln_normal(1, 3)
            ln_root(1, 4)
            ln_normal(1, 4)
            for t in range(1, TILES):
                h1_evac(t)
            act.wait_ge(r_gexp, 1)
            act.activation(gexp[:, :, :], gdif[:, :, :], ACT.Exp).then_inc(r_gexp, 1)
            def first_ehi(i):
                act.wait_ge(s_eraw[i], 16)
                act.wait_ge(eused, i + 1)
                copy(ehi[:, i, :], eraw[i][:, :], ehi_done)

            for i in range(3):
                first_ehi(i)
            act.wait_ge(r_eexp, 1)
            act.activation(eexp[:, :], ediff[:, :], ACT.Exp).then_inc(r_eexp, 1)
            first_ehi(3)
            act.wait_ge(r_done, 1)
            act.wait_ge(pad_cols, 5)

            def ehi_chunk(b, i):
                n = number(b, i)
                slot, landed = place(b, i)
                act.wait_ge(s_eraw[slot], 16 * landed)
                act.wait_ge(eused, n + 1)
                copy(ehi[:, i % ERING, :], eraw[slot][:, :], ehi_done)

            def xt_evac(b, q):
                act.wait_ge(xt_ready, 4 * b + q + 1)
                copy(xT_hi[:, 4 * q:4 * q + 4, 0:CAP], used_cols(ps[:, 6 + q % 2, :]), xt_hi)

            def ht_evac(b):
                act.wait_ge(ht_ready, b + 1)
                copy(hT_hi[:, :, 0:CAP], used_cols(ps[:, 1, :]), ht_hi)

            def y_evac(b, last):
                past(act, scattered, 16 * b)
                act.wait_ge(gcol_done, b + 1)
                for n in range(4):
                    if n < 3:
                        act.wait_ge(y_ready, 3 * b + n + 1)
                    else:
                        act.wait_ge(eused, last + (1 + ERING))
                    act.activation(yrow[:, 512 * n:512 * (n + 1)], ps[0:CAP, 2 + n, :], ACT.Copy,
                                   scale=gcol[:, :]).then_inc(y_done, 1)

            def moe_round(b):
                if not (isinstance(b, int) and b < 1):
                    for i in range(4):
                        ehi_chunk(b, i)
                if not (isinstance(b, int) and b < 2):
                    y_evac(b - 2, number(b - 1, ECH - 1))
                if not (isinstance(b, int) and b < 1):
                    ht_evac(b - 1)
                for i in range(4, 8):
                    ehi_chunk(b, i)
                act.wait_ge(eused, number(b, 3) + (1 + ERING))
                past(act, h_done, b)
                act.activation(srow[:, :], ps[:, 0, :], ACT.Silu).then_inc(silu_done, 1)
                if not (isinstance(b, int) and b < 1):
                    for i in range(8, 12):
                        ehi_chunk(b, i)
                for q in range(4):
                    xt_evac(b + 1, q)

            for q in range(4):
                xt_evac(0, q)
            for b in range(3):
                moe_round(b)
            with act.Fori(3, NE) as b:
                moe_round(b)
            n_over = act.value_load(steer[0:1, NX + 1:NX + 2], min_val=0, max_val=NX)
            with act.If(n_over > 0):
                with act.Fori(0, NX) as x_block:
                    with act.If(x_block < n_over):
                        moe_round(x_block + NE)
                    act.nop()
            act.nop()
            end = n_over + NE
            ehi_chunk(end, 0)
            ehi_chunk(end, 1)
            ht_evac(end - 1)
            y_evac(end - 2, number(end, -1))
            for i in range(2, 4):
                ehi_chunk(end, i)
            y_evac(end - 1, number(end, 3))
            act.wait_ge(y_done, 4 * n_over + 4 * NE)
            act.wait_ge(xt_hi, 4 * n_over + 4 * (NE + 1))
            act.sem_inc(moe_end, 1)

            act.wait_ge(f_eps, 1)
            for j, t in enumerate(fin_order):
                _, nmean, sq, sd, rs, nm = [fin_small[0:fin_rows[t], k, t:t + 1] for k in range(6)]
                act.wait_ge(f_mean, j + 1)
                act.activation(fin_y[t][0], fin_h[t], ACT.Square, bias=nmean, accum_out=sq).then_inc(f_sq, 1)
                act.wait_ge(f_sq, j + 1)
                act.activation(sd, sq, ACT.Sqrt, bias=fin_eps[0:fin_rows[t], :], scale=1.0 / D).then_inc(f_std, 1)
                act.wait_ge(f_mv, 2 * j + 2)
                act.activation(fin_h[t], fin_h[t], ACT.Identity, bias=nm, scale=rs).then_inc(f_norm, 1)

        @block.vector
        def _(dve):
            def lo_of(dst, src, hi, done):
                dve.tensor_tensor(dst, src, hi, ALU.subtract).then_inc(done, 1)

            def piece_stats(t, n, width, done):
                dve.bn_stats(stats[:, t, n, :], rows[:, t, width * n:width * (n + 1)]).then_inc(done, 1)

            def ln_variance(i, t, pieces):
                dve.bn_aggr(mv[:, t, :], stats[:, t, 0:pieces, :].rearrange("p a b -> p (a b)")).then_inc(s_agg[i], 1)
                dve.wait_ge(s_agg[i], t + 1)
                dve.tensor_scalar(std[:, t:t + 1], mv[:, t, 1:2], EPS, None, ALU.add).then_inc(ln_var[i], 1)

            def ln_scale(i, t):
                dve.wait_ge(ln_std[i], t + 1)
                dve.reciprocal(rstd[:, t:t + 1], std[:, t:t + 1]).then_inc(ln_mv[i], 1)
                dve.wait_ge(ln_mv[i], 2 * t + 1)
                dve.scalar_tensor_tensor(out=nmr[:, t:t + 1], in0=mv[:, t, 0:1], scalar=-1.0, in1=rstd[:, t:t + 1],
                                         op0=ALU.mult, op1=ALU.mult).then_inc(ln_mv[i], 1)

            def mult_g(i, t):
                dve.wait_ge(ln_norm[i], t + 1)
                dve.tensor_tensor(rows[:, t, :], rows[:, t, :], gb[:, 0, :], ALU.mult).then_inc(ln_g[i], 1)

            def h0_evac(t):
                sl = own_columns(t)
                for q in range(4):
                    dve.wait_ge(tr_hi, 4 * t + q + 1)
                    lo_of(act_lo[:, 4 * q:4 * q + 4, sl], own_part(t, q), act_hi[:, 4 * q:4 * q + 4, sl], tr_lo)

            def lo(base, i, loops, per, width=MC):
                n = base + i
                dve.wait_ge(hi_done, n + 1 + per * loops)
                lo_of(wlo[:, n % RING, 0:width], raw[:, n % RAW, 0:width], whi[:, n % RING, 0:width], lo_done)

            for t in range(TILES):
                dve.wait_ge(s_row[t], 32 if t == 0 else 16)
                for n in range(4):
                    piece_stats(t, n, 512, s_ln0)
                dve.wait_ge(s_ln0, 4 * t + 4)
                ln_variance(0, t, 4)
                if t == 1:
                    dve.wait_ge(s_gb0[0], 16)
                if t:
                    mult_g(0, t - 1)
                ln_scale(0, t)
            h0_evac(0)
            h0_evac(1)
            mult_g(0, TILES - 1)
            lo(F0, 0, 0, FCH)
            h0_evac(2)
            lo(F0, 1, 0, FCH)
            h0_evac(3)
            h0_evac(4)

            def fourier_out(g):
                past(dve, fo_lo, 2 * g)
                for m in range(2):
                    dve.wait_ge(fo_sin, 2 * g + m + 1)
                    c, s = ps[:, 2 + 2 * m, :], sine[:, m, :]
                    k = HALF + 1
                    dve.tensor_tensor(stage[:, 1 + m, 0:k], c[:, 0:k], s[:, 0:k], ALU.add).then_inc(fo_sum, 1)
                    dve.tensor_tensor(stage[:, 1 + m, k:T], c[:, HALF - 1:0:-1], s[:, HALF - 1:0:-1],
                                      ALU.subtract).then_inc(fo_sum, 1)
                for m in range(2):
                    dve.wait_ge(fo_hi, 2 * g + m + 1)
                    hi_part, lo_part = [z[:, at(8 + 2 * g + m, 1), :].rearrange("p a n -> p (a n)") for z in (mix_hi, mix_lo)]
                    lo_of(lo_part, stage[:, 1 + m, 0:T], hi_part, fo_lo)

            def fourier_group(g):
                def u_evac(m):
                    dve.wait_ge(fu_hi, 2 * g + m + 1)
                    lo_of(chan_lo[:, m, :].rearrange("p (h n) -> p h n", h=2), ps[:, 2 * m:2 * m + 2, 0:HALF],
                          chan_hi[:, m, :].rearrange("p (h n) -> p h n", h=2), fu_lo)

                if not (isinstance(g, int) and g == 0):
                    lo(F0, 0, g, FCH)
                    fourier_out(g - 1)
                    lo(F0, 1, g, FCH)
                for i in range(2, 4):
                    lo(F0, i, g, FCH)
                u_evac(0)
                lo(F0, 4, g, FCH, 512)
                lo(F0, 5, g, FCH, 512)
                u_evac(1)
                lo(F0, 6, g, FCH, 2 * HC)
                for t in range(TILES):
                    dve.wait_ge(fv_hi, TILES * g + t + 1)
                    lo_of(freq_lo[:, t, :], ps[:, (4 + t) % 8, :], freq_hi[:, t, :], fv_lo)
                for i in range(7, FCH):
                    lo(F0, i, g, FCH, pos_width(i))

            fourier_group(0)
            fourier_group(1)
            with dve.Fori(2, NG) as g:
                fourier_group(g)

            def window_lo(n):
                dve.wait_ge(pd_hi, n + 1)
                lo_of(mix_lo[:, n, :], stage[:, 1 + (n // 2) % 2, 0:T], mix_hi[:, n, :], pd_lo)

            def pool_out(g):
                for m in range(2):
                    n = 2 * g + m
                    dve.wait_ge(pm_hi, n + 1)
                    dve.scalar_tensor_tensor(out=mix_lo[:, n, :].rearrange("p (h n) -> p h n", h=2),
                                             in0=ps[:, 4 + 2 * m:6 + 2 * m, 0:HALF], scalar=cols[:, 32 + n:33 + n],
                                             in1=mix_hi[:, n, :].rearrange("p (h n) -> p h n", h=2),
                                             op0=ALU.mult, op1=ALU.subtract).then_inc(pm_lo, 1)

            for g in range(NG):
                u, gc = u_chunk(g), g_chunk(g - 1)
                lo(u, 0, 0, 0)
                if g == 0:
                    fourier_out(NG - 1)
                if g >= 2:
                    pool_out(g - 2)
                lo(u, 1, 0, 0)
                lo(u, 2, 0, 0)
                if g >= 1:
                    window_lo(2 * g - 1)
                lo(u, 3, 0, 0)
                if g >= 1:
                    lo(gc, 0, 0, 0, GD)
                window_lo(2 * g)
                if g >= 1:
                    lo(gc, 1, 0, 0, GD)
            lo(GATE0, 0, 0, 0)
            pool_out(NG - 2)
            lo(GATE0, 1, 0, 0)
            lo(J0, 0, 0, 0, GD)
            window_lo(2 * NG - 1)
            lo(J0, 1, 0, 0, GD)

            def gate_half(a, dst, jj, b):
                dve.wait_ge(used, J0 + JCH * b + 5 + a + 2 * JCH * jj)
                dve.wait_ge(gate_done, 4 * jj + 2 * b + a + 1)
                dve.tensor_tensor(dst, halved(stage[:, a, 0:T]), ps[:, 4 + 2 * a:6 + 2 * a, 0:HALF],
                                  ALU.mult).then_inc(mul_done, 1)

            def halved(ap):
                return ap.rearrange("p (h n) -> p h n", h=2)

            def column(jj, b):
                return merged[:, at(2 * jj + b, 1), :].rearrange("p a (h n) -> p (a h) n", h=2)

            def finish_column(jj, b):
                gate_half(1, halved(stage[:, 2, 0:T]), jj, b)
                dve.wait_ge(mul_done, 4 * jj + 2 * b + 2)
                dve.tensor_tensor(column(jj, b), column(jj, b), halved(stage[:, 2, 0:T]), ALU.add).then_inc(merge_done, 1)

            def gate_columns(jj):
                for b in range(2):
                    if isinstance(jj, int) and b == 0:
                        lo(J0, 2, 0, 0)
                        pool_out(NG - 1)
                        rest = range(3, JCH)
                    else:
                        lo(J0 + JCH * b, 0, jj, 2 * JCH)
                        finish_column(jj if b else jj - 1, 1 - b)
                        rest = range(1, JCH)
                    for i in rest:
                        lo(J0 + JCH * b, i, jj, 2 * JCH)
                    past(dve, merge_done, 2 * jj + b)
                    gate_half(0, column(jj, b), jj, b)

            gate_columns(0)
            with dve.Fori(1, KC // 2) as jj:
                gate_columns(jj)

            def merged_lo(q):
                dve.wait_ge(mt_hi, q + 1)
                lo_of(act_lo[:, 2 * q:2 * q + 2, :], merged[:, 2 * q:2 * q + 2, :], act_hi[:, 2 * q:2 * q + 2, :], mt_lo)

            def out_rows(p):
                n, c = divmod(256 * p, 512)
                dve.wait_ge(out_tr, 2 * p + 2)
                dve.wait_ge(s_res[n % 2], 16 * TILES * (n // 2 + 1))
                for t in range(TILES):
                    dve.scalar_tensor_tensor(out=rows[:, t, 256 * p:256 * (p + 1)], in0=resid[:, n % 2, t, c:c + 256],
                                             scalar=ALPHA, in1=out_bank(t), op0=ALU.mult,
                                             op1=ALU.add).then_inc(acc_free, 1)
                    dve.wait_ge(acc_free, TILES * p + t + 1)
                    piece_stats(t, p, 256, bn_done)
                    if p == PAIRS - 1:
                        dve.wait_ge(bn_done, TILES * p + t + 1)
                        ln_variance(1, t, PAIRS)
                        if t >= 1:
                            ln_scale(1, t - 1)
                        if t == 2:
                            dve.wait_ge(s_gb1, 32)
                        if t >= 2:
                            mult_g(1, t - 2)
                            add_b(dve, 1, t - 2)

            merged_lo(0)
            merged_lo(1)
            lo(W0, 0, 0, 0)
            finish_column(KC // 2 - 1, 1)
            merged_lo(2)
            merged_lo(3)
            lo(W0, 1, 0, 0)
            for q in range(4, 8):
                merged_lo(q)
            for p in range(PAIRS):
                for i in range(2 if p == 0 else 0, WCH):
                    lo(W0 + WCH * p, i, 0, 0)
                if p:
                    out_rows(p - 1)
            out_rows(PAIRS - 1)
            ln_scale(1, TILES - 1)
            mult_g(1, 3)
            mult_g(1, 4)
            add_b(dve, 1, 4)

            dve.wait_ge(used, WEND)
            for t in range(TILES):
                dve.wait_ge(lg_ready, t + 1)
                dve.tensor_tensor(logit[:, t, :], ps[:, 3 + t % 4, 0:NG + NE], rbias[:, :], ALU.add).then_inc(lg_done, 1)
            dve.wait_ge(lg_done, TILES)
            rsteps = 0

            def r(ins):
                nonlocal rsteps
                rsteps += 1
                ins.then_inc(r_step, 1)
                dve.wait_ge(r_step, rsteps)

            def wide(ap, n):
                shape = list(ap.shape)
                return ap.unsqueeze(len(shape)).broadcast_to(shape + [n])

            def over_tiles(ap, n):
                return ap.unsqueeze(1).broadcast_to([ap.shape[0], n, ap.shape[1]])

            gl, el = logit[:, :, 0:NG], logit[:, :, NG:NG + NE]
            r(dve.memset(ones[:, :], 1.0))
            r(dve.tensor_reduce(gmax[:, :], gl, AX, ALU.max))
            dve.tensor_tensor(gdif[:, :, :], gl, wide(gmax[:, :], NG), ALU.subtract).then_inc(r_gexp, 1)
            r(dve.tensor_tensor(gone[:, :, :], gl, wide(gmax[:, :], NG), ALU.is_equal))
            r(dve.tensor_tensor(gone[:, :, :], gone[:, :, :], over_tiles(const("r4"), TILES), ALU.mult))
            r(dve.tensor_reduce(gpick[:, :], gone[:, :, :], AX, ALU.max))
            r(dve.tensor_tensor(gone[:, :, :], gone[:, :, :], wide(gpick[:, :], NG), ALU.is_equal))
            r(dve.tensor_scalar(gone[:, :, :], gone[:, :, :], -1.0, BIG, ALU.add, ALU.mult))
            r(dve.tensor_tensor(masked[:, :, :].rearrange("p t (g e) -> p t g e", e=EG),
                                el.rearrange("p t (g e) -> p t g e", e=EG), wide(gone[:, :, :], EG), ALU.add))
            for a in range(2):
                src = (masked, masked2)[a]
                r(dve.tensor_reduce(emax[:, a, :], src[:, :, :], AX, ALU.max))
                r(dve.tensor_tensor(etmp[:, :, :], src[:, :, :], wide(emax[:, a, :], NE), ALU.is_equal))
                r(dve.tensor_tensor(etmp[:, :, :], etmp[:, :, :], over_tiles(const("r32"), TILES), ALU.mult))
                r(dve.tensor_reduce(epick[:, a, :], etmp[:, :, :], AX, ALU.max))
                r(dve.tensor_tensor(one[:, a, :, :], etmp[:, :, :], wide(epick[:, a, :], NE), ALU.is_equal))
                if a == 0:
                    r(dve.scalar_tensor_tensor(out=masked2[:, :, :], in0=one[:, 0, :, :], scalar=-2 * BIG,
                                               in1=masked[:, :, :], op0=ALU.mult, op1=ALU.add))
            r(dve.tensor_tensor(one[:, :, :, :], one[:, :, :, :], wide(over_tiles(const("valid"), 2), NE), ALU.mult))
            dve.tensor_tensor(ediff[:, :], emax[:, 1, :], emax[:, 0, :], ALU.subtract).then_inc(r_eexp, 1)
            dve.tensor_tensor(anyone[:, :, :], one[:, 0, :, :], one[:, 1, :, :], ALU.add).then_inc(r_any, 1)
            dve.wait_ge(r_gexp, 2)
            r(dve.tensor_reduce(gsum[:, :], gexp[:, :, :], AX, ALU.add))
            dve.wait_ge(r_eexp, 2)
            r(dve.tensor_scalar(esum[:, :], eexp[:, :], 1.0, None, ALU.add))
            r(dve.tensor_tensor(gsum[:, :], gsum[:, :], esum[:, :], ALU.mult))
            r(dve.reciprocal(gprob[:, :], gsum[:, :]))
            r(dve.tensor_tensor(gate[:, 0, :], gprob[:, :], const("valid"), ALU.mult))
            r(dve.tensor_tensor(gate[:, 1, :], gate[:, 0, :], eexp[:, :], ALU.mult))
            dve.wait_ge(r_pos, 1)
            r(dve.tensor_copy(earlier[:, 1, :], ps[:, 6, 0:NE]))
            for t in range(1, TILES):
                r(dve.tensor_tensor(earlier[:, t + 1, :], earlier[:, t, :], ps[:, 6, NE * t:NE * (t + 1)], ALU.add))
            r(dve.tensor_copy(posn[:, 0, :], ps[:, 5, 0:NE]))
            r(dve.tensor_tensor(posn[:, 1:TILES, :], ps[:, 5, NE:TILES * NE].rearrange("p (t e) -> p t e", e=NE),
                                earlier[:, 1:TILES, :], ALU.add))
            count = earlier[:, TILES, :]
            r(dve.tensor_tensor(over[:, :, :], over_tiles(count, 8), wide(const("steps"), NE), ALU.is_gt))
            r(dve.tensor_reduce(nover[:, :], over[:, :, :].rearrange("p k e -> p e k"), AX, ALU.add))
            r(dve.tensor_tensor_scan(cum[:, :], ones[:, 0:NE], nover[:, :], 0.0, ALU.mult, ALU.add))
            r(dve.tensor_tensor(excl[:, :], cum[:, :], nover[:, :], ALU.subtract))

            def flat(b):
                return b[:, :, :].rearrange("p a t -> p (a t)")

            def pick(dst, values):
                v = values if len(values.shape) == 3 else over_tiles(values, TILES)
                v = v.unsqueeze(1).broadcast_to([P, 2, TILES, NE])
                r(dve.tensor_tensor(prod[:, :, :, :], one[:, :, :, :], v, ALU.mult))
                r(dve.tensor_reduce(dst[:, :, :], prod[:, :, :, :], AX, ALU.add))

            pick(apos, posn[:, :, :])
            r(dve.tensor_scalar(flat(aexp), flat(epick), -1.0, float(NE), ALU.mult, ALU.add))
            pick(aexc, excl[:, :])
            r(dve.tensor_tensor(step8[:, :, :], over_tiles(flat(apos), 8), wide(const("steps"), 2 * TILES), ALU.is_ge))
            r(dve.tensor_reduce(flat(turn), step8[:, :, :].rearrange("p k n -> p n k"), AX, ALU.add))
            r(dve.scalar_tensor_tensor(out=flat(aslot), in0=flat(turn), scalar=-float(CAP), in1=flat(apos),
                                       op0=ALU.mult, op1=ALU.add))
            r(dve.tensor_scalar(flat(turn1), flat(turn), 1.0, None, ALU.min))
            r(dve.scalar_tensor_tensor(out=flat(ablock), in0=flat(aexc), scalar=float(NE - 1), in1=flat(aexp),
                                       op0=ALU.add, op1=ALU.subtract))
            r(dve.tensor_tensor(flat(ablock), flat(ablock), flat(turn1), ALU.mult))
            r(dve.tensor_tensor(flat(ablock), flat(ablock), flat(aexp), ALU.add))
            r(dve.tensor_tensor(flat(ablock), flat(ablock), flat(turn), ALU.add))
            dve.wait_ge(s_h1, 16 * TILES)
            r(dve.tensor_tensor(slot1[:, :, :], over_tiles(const("slot"), 2 * TILES), wide(flat(aslot), CAP), ALU.is_equal))
            r(dve.tensor_tensor(block1[:, :, :], over_tiles(const("block"), 2 * TILES), wide(flat(ablock), NTAB), ALU.is_equal))
            r(dve.tensor_tensor(block2[:, :, 0, :], block1[:, :, :], wide(const("token"), NTAB), ALU.mult))
            dve.tensor_tensor(block2[:, :, 1, :], block1[:, :, :], wide(flat(gate), NTAB), ALU.mult).then_inc(r_hot, 1)
            r(dve.tensor_tensor(below[:, :, :], over_tiles(cum[:, :], NX), wide(const("x"), NE), ALU.is_le))
            r(dve.memset(steerf[:, 0:1], float(NE - 1)))
            r(dve.tensor_reduce(steerf[:, 1:NX + 1], below[:, :, :], AX, ALU.add))
            r(dve.tensor_scalar(steerf[:, 1:NX + 1], steerf[:, 1:NX + 1], float(NE - 1), None, ALU.min))
            r(dve.tensor_copy(steerf[:, NX + 1:NX + 2], cum[:, NE - 1:NE]))
            r(dve.tensor_copy(steer[:, :], steerf[0:1, :]))
            dve.wait_ge(r_table, 1)
            r(dve.tensor_copy(table[:, :, :], ps[0:CAP, 6, 0:2 * NTAB].rearrange("p (a n) -> p a n", a=2)))
            r(dve.tensor_scalar(none[:, :], table[:, 0, :], 0.0, float(EMPTY), ALU.is_equal, ALU.mult))
            r(dve.scalar_tensor_tensor(out=sidxf[:, :], in0=table[:, 0, :], scalar=-1.0, in1=none[:, :],
                                       op0=ALU.add, op1=ALU.add))
            r(dve.tensor_scalar(second[:, :], sidxf[:, :], float(T), -float(T), ALU.is_ge, ALU.mult))
            r(dve.tensor_tensor(gidxf[:, :], sidxf[:, :], second[:, :], ALU.add))
            dve.tensor_copy(gidx[:, :], gidxf[:, :]).then_inc(r_gidx, 1)
            r(dve.tensor_copy(sidx[:, :], sidxf[:, :]))
            r(dve.tensor_copy(gatew[:, :], table[:, 1, :]))
            dve.sem_inc(r_done, 1)
            dve.wait_ge(pad_cols, 5)
            dve.wait_ge(elo_done, ERING)

            def elo_chunk(b, i):
                slot, _ = place(b, i)
                dve.wait_ge(ehi_done, number(b, i) + 1)
                lo_of(elo[:, i % ERING, :], eraw[slot][:, :], ehi[:, i % ERING, :], elo_done)

            def xt_evac(b, q):
                dve.wait_ge(xt_hi, 4 * b + q + 1)
                lo_of(xT_lo[:, 4 * q:4 * q + 4, 0:CAP], used_cols(ps[:, 6 + q % 2, :]),
                      xT_hi[:, 4 * q:4 * q + 4, 0:CAP], xt_lo)

            def ht_evac(b):
                dve.wait_ge(ht_hi, b + 1)
                lo_of(hT_lo[:, :, 0:CAP], used_cols(ps[:, 1, :]), hT_hi[:, :, 0:CAP], ht_lo)

            def gate_weights(b):
                past(dve, y_done, 4 * b)
                dve.tensor_scalar(gcol[:, :], gatew[:, at(b, 1)], 1.0, None, ALU.mult).then_inc(gcol_done, 1)

            def moe_round(b):
                if not (isinstance(b, int) and b < 1):
                    for i in range(4):
                        elo_chunk(b, i)
                if not (isinstance(b, int) and b < 1):
                    ht_evac(b - 1)
                for i in range(4, 8):
                    elo_chunk(b, i)
                if not (isinstance(b, int) and b < 1):
                    for i in range(8, 12):
                        elo_chunk(b, i)
                dve.wait_ge(silu_done, b + 1)
                dve.wait_ge(eused, number(b, 7) + (1 + ERING))
                past(dve, ht_lo, b)
                dve.tensor_tensor(hrow[:, :], srow[:, :], ps[:, 1, :], ALU.mult).then_inc(h_done, 1)
                for q in range(4):
                    xt_evac(b + 1, q)
                if not (isinstance(b, int) and b < 1):
                    gate_weights(b - 1)

            for q in range(4):
                xt_evac(0, q)
            moe_round(0)
            moe_round(1)
            with dve.Fori(2, NE) as b:
                moe_round(b)
            n_over = dve.value_load(steer[0:1, NX + 1:NX + 2], min_val=0, max_val=NX)
            with dve.If(n_over > 0):
                with dve.Fori(0, NX) as x_block:
                    with dve.If(x_block < n_over):
                        moe_round(x_block + NE)
                    dve.nop()
            dve.nop()
            end = n_over + NE
            elo_chunk(end, 0)
            elo_chunk(end, 1)
            ht_evac(end - 1)
            for i in range(2, 4):
                elo_chunk(end, i)
            gate_weights(end - 1)
            dve.wait_ge(xt_lo, 4 * n_over + 4 * (NE + 1))
            dve.wait_ge(elo_done, number(end, 3) + 1)
            dve.sem_inc(moe_end, 1)

            def fin_mult_g(j):
                t = fin_order[j]
                dve.wait_ge(f_norm, j + 1)
                dve.tensor_tensor(fin_h[t], fin_h[t], fin_g[0:fin_rows[t], :], ALU.mult).then_inc(f_g, 1)

            dve.memset(fin_eps[:, :], EPS).then_inc(f_eps, 1)
            for j, t in enumerate(fin_order):
                total, nmean, _, sd, rs, nm = [fin_small[0:fin_rows[t], k, t:t + 1] for k in range(6)]
                dve.wait_ge(s_fh[t], 16)
                if j < 2:
                    dve.wait_ge(s_fy[t], 32)
                    dve.tensor_tensor(fin_y[t][1], fin_y[t][0], fin_y[t][1], ALU.add).then_inc(f_sum, 1)
                    dve.wait_ge(f_sum, 2 * j + 1)
                else:
                    dve.wait_ge(f_pair, j - 1)
                dve.scalar_tensor_tensor(out=fin_h[t], in0=fin_h[t], scalar=ALPHA, in1=fin_y[t][1],
                                         op0=ALU.mult, op1=ALU.add, accum_out=total).then_inc(f_sum, 1)
                dve.wait_ge(f_sum, 2 * j + 2 if j < 2 else j + 3)
                dve.tensor_scalar(nmean, total, -1.0 / D, None, ALU.mult).then_inc(f_mean, 1)
                if j == 1:
                    dve.wait_ge(s_gb2, 32)
                if j:
                    fin_mult_g(j - 1)
                if j in (2, 3):
                    fin_add_b(dve, j - 2)
                dve.wait_ge(f_std, j + 1)
                dve.reciprocal(rs, sd).then_inc(f_mv, 1)
                dve.wait_ge(f_mv, 2 * j + 1)
                dve.tensor_tensor(nm, nmean, rs, ALU.mult).then_inc(f_mv, 1)
            fin_mult_g(TILES - 1)
            fin_add_b(dve, TILES - 1, slice(0, D // 2))
            fin_add_b(dve, TILES - 1, slice(D // 2, D), 1)

        @block.tensor
        def _(pe):
            def product(outs, l_hi, l_lo, r_hi, r_lo, start, stop):
                last = None
                for k, (l, r) in enumerate(((l_hi, r_hi), (l_hi, r_lo), (l_lo, r_hi))):
                    for o, rr in zip(outs, r, strict=True):
                        last = pe.matmul(o, l, rr, start=start and k == 0, stop=stop and k == 2)
                return last

            def halves(buf, k):
                return [buf[:, k, 0:HALF], buf[:, k, HALF:T]]

            pe.wait_ge(s_small, 16 * 6)
            pe.transpose(ps[:, 7, 0:40], colsrc[:, :], ident[0:40, 0:40]).then_inc(cols_ready, 1)

            def h0_transposes(t):
                pe.wait_ge(ln_done[0][t], 1)
                if t == 1:
                    pe.wait_ge(cols_done, 1)
                for q in range(4):
                    if t >= 2:
                        pe.wait_ge(tr_lo, 4 * (t - 2 if t < 4 else 3) + q + 1)
                    for c in range(4):
                        k = 4 * q + c
                        last = pe.transpose(ps[:, q + TR_BANK[t], P * c:P * (c + 1)], rows[:, t, P * k:P * (k + 1)], ident)
                    last.then_inc(tr_ready, 1)

            for t in range(4):
                h0_transposes(t)

            def project(base, i0, loops, per, bank, fresh=False):
                for half in range(2):
                    n = base + i0 + half
                    pe.wait_ge(lo_done, n + 1 + per * loops)
                    for k in range(8):
                        if fresh and k % 2 == 0:
                            pe.wait_ge(mt_lo, 4 * half + k // 2 + 1)
                        last = product([ps[:, bank, 0:HALF], ps[:, bank + 1, 0:HALF]],
                                       whi[:, n % RING, P * k:P * (k + 1)], wlo[:, n % RING, P * k:P * (k + 1)],
                                       halves(act_hi, 8 * half + k), halves(act_lo, 8 * half + k),
                                       half == 0 and k == 0, half == 1 and k == 7)
                    last.then_inc(used, 1)
                return last

            def first_project():
                for h in range(2):
                    if h == 1:
                        h0_transposes(4)
                    pe.wait_ge(tr_lo, 12 if h == 0 else 4 * TILES)
                    for half in range(2):
                        n = F0 + half
                        pe.wait_ge(lo_done, n + 1)
                        for k in range(8):
                            last = product([ps[:, h, 0:HALF]],
                                           whi[:, n, P * k:P * (k + 1)], wlo[:, n, P * k:P * (k + 1)],
                                           [halves(act_hi, 8 * half + k)[h]], [halves(act_lo, 8 * half + k)[h]],
                                           half == 0 and k == 0, half == 1 and k == 7)
                        if h == 1:
                            last.then_inc(used, 1)

            def fourier_group(g):
                for m in range(2):
                    if isinstance(g, int) and m == 0:
                        first_project()
                        continue
                    if m == 0:
                        pe.wait_ge(fv_lo, TILES * g)
                    else:
                        past(pe, fo_sum, 4 * g)
                    project(F0, 2 * m, g, FCH, 2 * m)
                for m in range(2):
                    n = F0 + 4 + m
                    pe.wait_ge(lo_done, n + 1 + FCH * g)
                    pe.wait_ge(fu_lo, 2 * g + m + 1)
                    for t, s in enumerate(STARTS):
                        last = product([ps[:, (4 + t) % 8, :]], chan_hi[:, m, s:s + P], chan_lo[:, m, s:s + P],
                                       [whi[:, n % RING, 0:512]], [wlo[:, n % RING, 0:512]], m == 0, m == 1)
                        if m == 1 and t < TILES - 1:
                            last.then_inc(fv_ready, 1)
                    last.then_inc(used, 1)
                for i in range(6, FCH):
                    t, part = pos_part(i)
                    n = F0 + i
                    pe.wait_ge(fv_lo, TILES * g + max(t + 1, 2))
                    pe.wait_ge(lo_done, n + 1 + FCH * g)
                    for c in range(part.start, part.stop, HC):
                        cs, at_c = c // HC, c - part.start
                        for m in range(2):
                            f = GD * cs + P * m
                            last = product([ps[:, 2 + 2 * m + cs, 0:HC]], freq_hi[:, t, f:f + P], freq_lo[:, t, f:f + P],
                                           [whi[:, n % RING, at_c:at_c + HC]], [wlo[:, n % RING, at_c:at_c + HC]],
                                           t == 0, t == TILES - 1)
                            if i == FCH - 1 and m == 0:
                                last.then_inc(fo_ready, 1)
                    last.then_inc(used, 1)

            fourier_group(0)
            with pe.Fori(1, NG) as g:
                fourier_group(g)

            def pool_project(g):
                for m in range(2):
                    if isinstance(g, int) and g == 0:
                        if m == 1:
                            pe.wait_ge(fo_sum, 4 * NG)
                        project(P0, 2 * m, 0, 0, 2 * m)
                    else:
                        pe.wait_ge(pu_copied, 2 * g - 1 + m)
                        project(P0 - 2, 2 * m, g, PCH, 2 * m)

            def pool_map(g, base, loops):
                past(pe, pm_lo, 2 * g)
                for k in range(2):
                    n = base + k
                    pe.wait_ge(lo_done, n + 1 + PCH * loops)
                    pe.wait_ge(pd_lo, 2 * g + k + 1)
                    hi = [mix_hi[:, at(2 * g + k, 1), h * HALF:(h + 1) * HALF].rearrange("p a n -> p (a n)") for h in range(2)]
                    lo = [mix_lo[:, at(2 * g + k, 1), h * HALF:(h + 1) * HALF].rearrange("p a n -> p (a n)") for h in range(2)]
                    for m in range(2):
                        last = product([ps[:, 4 + 2 * m, 0:HALF], ps[:, 5 + 2 * m, 0:HALF]],
                                       whi[:, n % RING, P * m:P * (m + 1)], wlo[:, n % RING, P * m:P * (m + 1)],
                                       hi, lo, k == 0, k == 1)
                    last.then_inc(used, 1)

            pool_project(0)
            pool_project(1)
            pool_map(0, g_chunk(0), 0)
            with pe.Fori(2, NG) as g:
                pool_project(g)
                pool_map(g - 1, g_chunk(0) - PCH, g)

            def gate_column(j):
                for a in range(2):
                    past(pe, gate_done, 2 * j)
                    if isinstance(j, int) and a == 0:
                        project(GATE0, 0, 0, 0, 0)
                        pool_map(NG - 1, J0, 0)
                    else:
                        project(J0, 2 * a, j, JCH, 2 * a)
                for a in range(2):
                    n = J0 + 4 + a
                    pe.wait_ge(lo_done, n + 1 + JCH * j)
                    past(pe, mul_done, 2 * j)
                    if isinstance(j, int):
                        pe.wait_ge(pm_lo, 2 * NG)
                    for k in range(8):
                        last = product([ps[:, 4 + 2 * a, 0:HALF], ps[:, 5 + 2 * a, 0:HALF]],
                                       whi[:, n % RING, P * k:P * (k + 1)], wlo[:, n % RING, P * k:P * (k + 1)],
                                       halves(mix_hi, 8 * a + k), halves(mix_lo, 8 * a + k), k == 0, k == 7)
                    last.then_inc(used, 1)

            gate_column(0)
            with pe.Fori(1, KC) as j:
                gate_column(j)

            def out_block(j, p, c):
                if isinstance(j, int) and j < 2:
                    pe.wait_ge(gate_done, 2 * KC)
                else:
                    pe.wait_ge(out_copied, j - 1)
                project(W0, 2 * c, p, WCH, 2 * c, fresh=isinstance(j, int) and j == 0)

            def out_transposes(j, p, c):
                pe.wait_ge(out_copied, j + 1)
                if c == 0:
                    if isinstance(p, int) and p == 0:
                        pe.wait_ge(mul_done, 2 * KC)
                    else:
                        pe.wait_ge(acc_free, TILES * p)
                for t, s in enumerate(STARTS):
                    last = pe.transpose(out_bank(t)[:, P * c:P * (c + 1)], outT[:, c, s:s + P], ident)
                last.then_inc(out_tr, 1)

            out_block(0, 0, 0)
            out_block(1, 0, 1)
            out_transposes(0, 0, 0)
            with pe.Fori(1, PAIRS) as p:
                out_block(2 * p, p, 0)
                out_transposes(2 * p - 1, p - 1, 1)
                out_block(2 * p + 1, p, 1)
                out_transposes(2 * p, p, 0)
            out_transposes(KC - 1, PAIRS - 1, 1)

            def logits(t):
                pe.wait_ge(rt_done, 4 * t + 4)
                if t == 0:
                    pe.wait_ge(s_wr, 32)
                    pe.wait_ge(acc_free, TILES * PAIRS)
                if t == 4:
                    pe.wait_ge(lg_done, 1)
                for k in range(KC):
                    last = pe.matmul(ps[:, 3 + t % 4, 0:NG + NE], h1T[:, t % 2, k, :], wrout[:, k, :],
                                     start=k == 0, stop=k == KC - 1)
                last.then_inc(lg_ready, 1)

            for t in range(TILES):
                pe.wait_ge(ln_done[1][t], 1)
                for q in range(4):
                    if t:
                        pe.wait_ge(rt_done, 4 * (t - 1) + q + 1)
                    for c in range(4):
                        k = 4 * q + c
                        last = pe.transpose(ps[:, RT_BANK[q], P * c:P * (c + 1)], rows[:, t, P * k:P * (k + 1)], ident)
                    last.then_inc(rt_ready, 1)
                if t:
                    logits(t - 1)
            logits(TILES - 1)
            pe.wait_ge(lg_done, TILES)
            pe.sem_inc(eused, ERING)
            pe.wait_ge(r_any, 1)
            every = anyone[:, :, :].rearrange("p t e -> p (t e)")
            pe.matmul(ps[:, 5, 0:TILES * NE], const("ltri"), every, start=True, stop=True)
            pe.matmul(ps[:, 6, 0:TILES * NE], ones[:, :], every, start=True, stop=True).then_inc(r_pos, 1)
            pe.wait_ge(r_hot, 1)
            for n in range(2 * TILES):
                last = pe.matmul(ps[0:CAP, 6, 0:2 * NTAB], slot1[:, n, :],
                                 block2[:, n, :, :].rearrange("p a n -> p (a n)"), start=n == 0, stop=n == 2 * TILES - 1)
            last.then_inc(r_table, 1)

            def xt(b, q):
                if q == 0:
                    pe.wait_ge(gathered, 16 * b + 16)
                past(pe, xt_lo, 4 * b + q - 1 if q else 4 * b)
                pe.wait_ge(pad_cols, 1)
                for c in range(4):
                    k = 4 * q + c
                    last = pe.transpose(ps[:, 6 + q % 2, P * c:P * (c + 1)], xrow[:, P * k:P * (k + 1)], ident)
                last.then_inc(xt_ready, 1)

            def ht(b):
                pe.wait_ge(h_done, b + 1)
                pe.wait_ge(pad_cols, 5)
                for c in range(4):
                    last = pe.transpose(ps[:, 1, P * c:P * (c + 1)], hrow[:, P * c:P * (c + 1)], ident)
                last.then_inc(ht_ready, 1)

            def down_product(b, i, k):
                pe.wait_ge(elo_done, number(b, i) + 1)
                for n in range(4):
                    last = product([ps[:, 2 + n, :]], hT_hi[:, k, :], hT_lo[:, k, :],
                                   [ehi[:, i % ERING, 512 * n:512 * (n + 1)]],
                                   [elo[:, i % ERING, 512 * n:512 * (n + 1)]], k == 0, k == 3)
                    if k == 3 and n < 3:
                        last.then_inc(y_ready, 1)
                last.then_inc(eused, 1)

            def moe_round(b):
                follows = not (isinstance(b, int) and b < 1)
                for i in range(8):
                    if i < 4:
                        pe.wait_ge(xt_lo, 4 * b + i + 1)
                    if i == 0:
                        past(pe, silu_done, b)
                    if i == 2 and follows:
                        ht(b - 1)
                    if i == 4:
                        past(pe, ht_lo, b)
                    pe.wait_ge(elo_done, number(b, i) + 1)
                    for kk in range(4):
                        k = 4 * (i % 4) + kk
                        last = product([ps[:, i // 4, :]], xT_hi[:, k, :], xT_lo[:, k, :],
                                       [ehi[:, i % ERING, F * kk:F * (kk + 1)]],
                                       [elo[:, i % ERING, F * kk:F * (kk + 1)]], k == 0, k == KC - 1)
                    last.then_inc(eused, 1)
                xt(b + 1, 0)
                xt(b + 1, 1)
                if follows:
                    past(pe, y_done, 4 * (b - 1))
                    down_product(b, 8, 0)
                xt(b + 1, 2)
                xt(b + 1, 3)
                if follows:
                    for k in range(1, 4):
                        down_product(b, 8 + k, k)

            for q in range(4):
                xt(0, q)
            moe_round(0)
            moe_round(1)
            with pe.Fori(2, NE) as b:
                moe_round(b)
            n_over = pe.value_load(steer[0:1, NX + 1:NX + 2], min_val=0, max_val=NX)
            with pe.If(n_over > 0):
                with pe.Fori(0, NX) as x_block:
                    with pe.If(x_block < n_over):
                        moe_round(x_block + NE)
                    pe.nop()
            pe.nop()
            end = n_over + NE
            ht(end - 1)
            pe.wait_ge(ht_lo, end)
            pe.wait_ge(y_done, 4 * (end - 1))
            for k in range(4):
                down_product(end, k, k)
            pe.wait_ge(eused, number(end, 3) + (1 + ERING))
            pe.sem_inc(moe_end, 1)


_INS = ["x", "meta_tokens", "in_ln_g", "in_ln_b", "w_in", "b_gate", "w_pool_group", "pool_scale", "w_branch_pool",
        "w_branch_fourier", "w_out", "ln1_g", "ln1_b", "w_router_group", "b_router_group", "w_router_expert",
        "b_router_expert", "w_gate", "w_up", "w_down", "ln2_g", "ln2_b"]


def kernel(**inputs):
    import concourse.bacc as _bacc
    from concourse.bass_utils import run_bass_kernel_spmd as _run

    nc = _bacc.Bacc("TRN2", target_bir_lowering=False, num_devices=1)
    small, chan, pos, edge = shape_constants()
    arrays, args = {}, []

    def add(name, a):
        arrays[name] = a
        args.append(nc.dram_tensor(name, a.shape, mybir.dt.from_np(a.dtype), kind="ExternalInput").ap())

    for name in _INS:
        a = np.ascontiguousarray(inputs[name])
        if a.ndim == 1:
            a = a.reshape(1, -1)
        add(f"in_{name}", a)
    add("k_small", small)
    add("k_chan", chan)
    add("k_pos", pos)
    add("k_edge", edge.reshape(1, -1))
    args.append(nc.dram_tensor("out", (1, SEQ, D), F32, kind="ExternalOutput").ap())
    encoder_kernel(nc, *args)
    r = _run(nc, [arrays], core_ids=[0])
    return r.results[0]["out"]
```
